# Optimizing a Trainium2 kernel written in Bass

```python
import math
import jax, jax.numpy as jnp
from jax import lax
import numpy as np

D_MODEL = 1024
BATCH = 1
SEQ = 512
DEPTH = 1

HEAD_DIM = 64
Q_BLOCK = 128
NSA_HEADS = 8
NSA_KV = 2
NSA_BLOCK = 64
NSA_TOPN = 16
NSA_LOCAL = 2
NSA_WINDOW = 512
NSA_CMP_HIDDEN = 256
SWA_HEADS = 8
SWA_KV = 2
SWA_WINDOW = 128
DIFF_HEADS = 4
N_EXPERTS = 64
TOP_K = 8
N_GROUPS = 8
TOPK_GROUPS = 4
EXPERT_DIM = 256
SHARED_DIM = 256
ROUTED_SCALE = 2.5
MOE_BLOCK = 128
PLE_DIM = 256
ALPHA = (2 * DEPTH) ** 0.25
BETA = (8 * DEPTH) ** -0.25
LN_EPS = 1e-5
NEG = -1e30
FORCE = 1e4

IN_SIZES = (NSA_HEADS * HEAD_DIM,) + (NSA_KV * HEAD_DIM,) * 6 + (NSA_HEADS * 3,) + \
    (SWA_HEADS * HEAD_DIM, SWA_KV * HEAD_DIM, SWA_KV * HEAD_DIM) + \
    (DIFF_HEADS * 2 * HEAD_DIM,) * 3 + (3 * D_MODEL,)
IN_COLS = sum(IN_SIZES)

kernel_name = "hybrid_nsa_swa_diff_moe_deepnorm"

def alibi_slopes(n):
    return jnp.asarray(2.0 ** (-8.0 * np.arange(1, n + 1) / n), dtype=jnp.float32)

def layer_norm(x, g, b):
    xf = x.astype(jnp.float32)
    mu = xf.mean(-1, keepdims=True)
    var = jnp.square(xf - mu).mean(-1, keepdims=True)
    return ((xf - mu) * lax.rsqrt(var + LN_EPS) * g + b).astype(x.dtype)

def masked_softmax(s, mask):
    s = jnp.where(mask, s, NEG)
    mx = s.max(-1, keepdims=True)
    e = jnp.where(mask, jnp.exp(s - mx), 0.0)
    return e / jnp.maximum(e.sum(-1, keepdims=True), 1e-30)

def banded_gqa(q, k, v, window, slopes, sinks=None):
    B, S, H, dh = q.shape
    HKV = k.shape[2]
    G = H // HKV
    nq = S // Q_BLOCK
    nb = window // Q_BLOCK + 1
    span = nb * Q_BLOCK
    pad = ((0, 0), (window, 0), (0, 0), (0, 0))
    kp = jnp.pad(k, pad).reshape(B, nq + window // Q_BLOCK, Q_BLOCK, HKV, dh)
    vp = jnp.pad(v, pad).reshape(B, nq + window // Q_BLOCK, Q_BLOCK, HKV, dh)
    kband = jnp.concatenate([kp[:, j:j + nq] for j in range(nb)], axis=2)
    vband = jnp.concatenate([vp[:, j:j + nq] for j in range(nb)], axis=2)
    qb = q.reshape(B, nq, Q_BLOCK, HKV, G, dh)
    s = jnp.einsum('bnqkgd,bnckd->bnkgqc', qb, kband).astype(jnp.float32) * (dh ** -0.5)
    blk0 = jnp.arange(nq)[:, None] * Q_BLOCK
    t = blk0 + jnp.arange(Q_BLOCK)[None, :]
    spos = blk0 - window + jnp.arange(span)[None, :]
    dist = t[:, :, None] - spos[:, None, :]
    mask = (dist >= 0) & (dist < window) & (spos >= 0)[:, None, :]
    slopes_kg = slopes.reshape(HKV, G)
    s = s - slopes_kg[None, None, :, :, None, None] * dist.astype(jnp.float32)[None, :, None, None, :, :]
    s = jnp.where(mask[None, :, None, None, :, :], s, NEG)
    if sinks is None:
        p = jax.nn.softmax(s, axis=-1)
    else:
        sk = jnp.broadcast_to(sinks.astype(jnp.float32).reshape(HKV, G)[None, None, :, :, None, None], s.shape[:-1] + (1,))
        p = jax.nn.softmax(jnp.concatenate([s, sk], axis=-1), axis=-1)[..., :-1]
    o = jnp.einsum('bnkgqc,bnckd->bnqkgd', p.astype(v.dtype), vband)
    return o.reshape(B, S, H, dh)

def nsa_attention(q, k_cmp, v_cmp, k_slc, v_slc, k_win, v_win, gates, pe_k, w1_k, w2_k, pe_v, w1_v, w2_v, slopes):
    B, S, H, dh = q.shape
    HKV = k_cmp.shape[2]
    G = H // HKV
    NB = S // NSA_BLOCK
    n_sel = min(NSA_TOPN, NB)
    scale = dh ** -0.5
    slopes_kg = slopes.reshape(HKV, G)

    def compress(kv, pe, w1, w2):
        kb = kv.reshape(B, NB, NSA_BLOCK, HKV, dh) + pe[None, None, :, None, :]
        kb = kb.transpose(0, 1, 3, 2, 4).reshape(B, NB, HKV, NSA_BLOCK * dh)
        return jax.nn.gelu(kb @ w1) @ w2

    kc = compress(k_cmp, pe_k, w1_k, w2_k)
    vc = compress(v_cmp, pe_v, w1_v, w2_v)
    qg = q.reshape(B, S, HKV, G, dh)
    t = jnp.arange(S)

    cpos = jnp.arange(NB) * NSA_BLOCK + NSA_BLOCK - 1
    dist_c = t[:, None] - cpos[None, :]
    s_c = jnp.einsum('bskgd,bnkd->bskgn', qg, kc).astype(jnp.float32) * scale
    s_c = s_c - slopes_kg[None, None, :, :, None] * dist_c.astype(jnp.float32)[None, :, None, None, :]
    p_c = masked_softmax(s_c, (dist_c >= 0)[None, :, None, None, :])
    o_c = jnp.einsum('bskgn,bnkd->bskgd', p_c.astype(vc.dtype), vc)

    imp = p_c.sum(axis=3)
    blk = jnp.arange(NB)
    rel = (t // NSA_BLOCK)[:, None] - blk[None, :]
    forced = (blk[None, :] == 0) | ((rel >= 0) & (rel < NSA_LOCAL))
    imp = jnp.where(forced[None, :, None, :], FORCE, jnp.where((rel >= 0)[None, :, None, :], imp, -1.0))
    top_val, top_idx = lax.top_k(imp, n_sel)
    sel_ok = top_val >= 0

    ksb = k_slc.reshape(B, NB, NSA_BLOCK, HKV, dh).transpose(0, 3, 1, 2, 4)
    vsb = v_slc.reshape(B, NB, NSA_BLOCK, HKV, dh).transpose(0, 3, 1, 2, 4)
    nq = S // Q_BLOCK
    bi = jnp.arange(B)[:, None, None, None]
    ki = jnp.arange(HKV)[None, None, :, None]

    def to_chunks(a):
        return a.reshape((B, nq, Q_BLOCK) + a.shape[2:]).swapaxes(0, 1)

    def sel_chunk(args):
        qi, idx, ok, n = args
        kg = ksb[bi, ki, idx]
        vg = vsb[bi, ki, idx]
        tq = n * Q_BLOCK + jnp.arange(Q_BLOCK)
        kpos = idx[..., None] * NSA_BLOCK + jnp.arange(NSA_BLOCK)
        dist = tq[None, :, None, None, None] - kpos
        m = ok[..., None] & (dist >= 0)
        L = n_sel * NSA_BLOCK
        kg = kg.reshape(B, Q_BLOCK, HKV, L, dh)
        vg = vg.reshape(B, Q_BLOCK, HKV, L, dh)
        dist = dist.reshape(B, Q_BLOCK, HKV, L).astype(jnp.float32)
        m = m.reshape(B, Q_BLOCK, HKV, L)
        s = jnp.einsum('bqkgd,bqkld->bqkgl', qi, kg).astype(jnp.float32) * scale
        s = s - slopes_kg[None, None, :, :, None] * dist[:, :, :, None, :]
        p = masked_softmax(s, m[:, :, :, None, :])
        return jnp.einsum('bqkgl,bqkld->bqkgd', p.astype(vg.dtype), vg)

    o_s = lax.map(sel_chunk, (to_chunks(qg), to_chunks(top_idx), to_chunks(sel_ok), jnp.arange(nq)))
    o_s = o_s.swapaxes(0, 1).reshape(B, S, H, dh)

    o_w = banded_gqa(q, k_win, v_win, NSA_WINDOW, slopes)

    g = jax.nn.sigmoid(gates)
    o = g[..., 0:1] * o_c.reshape(B, S, H, dh) + g[..., 1:2] * o_s + g[..., 2:3] * o_w
    return o.reshape(B, S, H * dh)

def diff_attention(q, k, v, lam, lambda_init, slopes, norm_g):
    B, S, HC, _, dh = q.shape
    nq = S // Q_BLOCK
    scale = dh ** -0.5
    spos = jnp.arange(S)
    qc = q.reshape(B, nq, Q_BLOCK, HC, 2, dh).swapaxes(0, 1)

    def chunk(args):
        qi, n = args
        tq = n * Q_BLOCK + jnp.arange(Q_BLOCK)
        dist = tq[:, None] - spos[None, :]
        s = jnp.einsum('bqhrd,bkhrd->bhrqk', qi, k).astype(jnp.float32) * scale
        s = s - slopes[None, :, None, None, None] * dist.astype(jnp.float32)[None, None, None, :, :]
        s = jnp.where((dist >= 0)[None, None, None, :, :], s, NEG)
        a = jax.nn.softmax(s, axis=-1)
        w = a[:, :, 0] - lam * a[:, :, 1]
        return jnp.einsum('bhqk,bkhe->bqhe', w.astype(v.dtype), v)

    o = lax.map(chunk, (qc, jnp.arange(nq))).swapaxes(0, 1).reshape(B, S, HC, 2 * dh)
    of = o.astype(jnp.float32)
    of = of * lax.rsqrt(jnp.mean(of * of, axis=-1, keepdims=True) + LN_EPS) * norm_g
    of = of * (1.0 - lambda_init)
    return of.astype(v.dtype).reshape(B, S, HC * 2 * dh)

def moe(x, router_w, router_bias, w_gate, w_up, w_down, sh_gate, sh_up, sh_down):
    B, S, D = x.shape
    T = B * S
    xt = x.reshape(T, D)
    scores = jax.nn.sigmoid((xt @ router_w).astype(jnp.float32))
    biased = scores + router_bias.astype(jnp.float32)
    grp = biased.reshape(T, N_GROUPS, N_EXPERTS // N_GROUPS)
    grp_score = lax.top_k(grp, 2)[0].sum(-1)
    _, grp_idx = lax.top_k(grp_score, TOPK_GROUPS)
    grp_mask = jax.nn.one_hot(grp_idx, N_GROUPS).sum(-2) > 0
    exp_mask = jnp.repeat(grp_mask, N_EXPERTS // N_GROUPS, axis=-1)
    _, eidx = lax.top_k(jnp.where(exp_mask, biased, NEG), TOP_K)
    w = jnp.take_along_axis(scores, eidx, axis=-1)
    w = w / w.sum(-1, keepdims=True) * ROUTED_SCALE

    A = T * TOP_K
    flat_e = eidx.reshape(A)
    flat_tok = jnp.arange(A) // TOP_K
    flat_w = w.reshape(A)
    order = jnp.argsort(flat_e)
    e_sorted = flat_e[order]
    counts = jnp.bincount(flat_e, length=N_EXPERTS)
    padded = (counts + MOE_BLOCK - 1) // MOE_BLOCK * MOE_BLOCK
    pad_end = jnp.cumsum(padded)
    pad_start = pad_end - padded
    start = jnp.cumsum(counts) - counts
    dest = pad_start[e_sorted] + jnp.arange(A) - start[e_sorted]
    P = A + N_EXPERTS * MOE_BLOCK
    NBP = P // MOE_BLOCK
    buf_tok = jnp.full((P,), T, dtype=jnp.int32).at[dest].set(flat_tok[order].astype(jnp.int32))
    buf_w = jnp.zeros((P,), jnp.float32).at[dest].set(flat_w[order])
    blk_exp = jnp.minimum(jnp.searchsorted(pad_end, jnp.arange(NBP) * MOE_BLOCK, side='right'), N_EXPERTS - 1)
    x_pad = jnp.concatenate([xt, jnp.zeros((1, D), xt.dtype)], axis=0)

    def expert_block(args):
        tok, wb, e = args
        xb = x_pad[tok]
        h = jax.nn.silu(xb @ w_gate[e]) * (xb @ w_up[e])
        return (h @ w_down[e]) * wb[:, None].astype(xb.dtype)

    yb = lax.map(expert_block, (buf_tok.reshape(NBP, MOE_BLOCK), buf_w.reshape(NBP, MOE_BLOCK), blk_exp))
    y = jnp.zeros((T + 1, D), x.dtype).at[buf_tok].add(yb.reshape(P, D))[:T]
    shared = (jax.nn.silu(xt @ sh_gate) * (xt @ sh_up)) @ sh_down
    return (y + shared).reshape(B, S, D)

def setup_inputs(seed: int = 0) -> dict:
    key = jax.random.key(seed)
    ks = iter(jax.random.split(key, 40))
    L, D = DEPTH, D_MODEL

    def nrm(shape, scale):
        return jax.random.normal(next(ks), shape, jnp.float32) * scale

    return {
        "x": nrm((BATCH, SEQ, D), 1.0),
        "p": nrm((DEPTH, BATCH, SEQ, PLE_DIM), 1.0),
        "w_in": nrm((L, D, IN_COLS), D ** -0.5),
        "nsa_pe_k": nrm((L, NSA_BLOCK, HEAD_DIM), 0.02),
        "nsa_w1_k": nrm((L, NSA_BLOCK * HEAD_DIM, NSA_CMP_HIDDEN), (NSA_BLOCK * HEAD_DIM) ** -0.5),
        "nsa_w2_k": nrm((L, NSA_CMP_HIDDEN, HEAD_DIM), NSA_CMP_HIDDEN ** -0.5),
        "nsa_pe_v": nrm((L, NSA_BLOCK, HEAD_DIM), 0.02),
        "nsa_w1_v": nrm((L, NSA_BLOCK * HEAD_DIM, NSA_CMP_HIDDEN), (NSA_BLOCK * HEAD_DIM) ** -0.5),
        "nsa_w2_v": nrm((L, NSA_CMP_HIDDEN, HEAD_DIM), NSA_CMP_HIDDEN ** -0.5),
        "swa_sinks": nrm((L, SWA_HEADS), 1.0),
        "diff_lq1": nrm((L, HEAD_DIM), 0.1),
        "diff_lk1": nrm((L, HEAD_DIM), 0.1),
        "diff_lq2": nrm((L, HEAD_DIM), 0.1),
        "diff_lk2": nrm((L, HEAD_DIM), 0.1),
        "diff_norm_g": 1.0 + nrm((L, 2 * HEAD_DIM), 0.02),
        "w_branch_a": nrm((L, NSA_HEADS * HEAD_DIM, D), (NSA_HEADS * HEAD_DIM) ** -0.5),
        "w_branch_b": nrm((L, SWA_HEADS * HEAD_DIM, D), (SWA_HEADS * HEAD_DIM) ** -0.5),
        "w_branch_c": nrm((L, DIFF_HEADS * 2 * HEAD_DIM, D), (DIFF_HEADS * 2 * HEAD_DIM) ** -0.5),
        "w_out": nrm((L, D, D), D ** -0.5 * BETA),
        "ln1_g": 1.0 + nrm((L, D), 0.02),
        "ln1_b": nrm((L, D), 0.02),
        "router_w": nrm((L, D, N_EXPERTS), D ** -0.5),
        "router_bias": nrm((L, N_EXPERTS), 0.01),
        "exp_w_gate": nrm((L, N_EXPERTS, D, EXPERT_DIM), D ** -0.5),
        "exp_w_up": nrm((L, N_EXPERTS, D, EXPERT_DIM), D ** -0.5),
        "exp_w_down": nrm((L, N_EXPERTS, EXPERT_DIM, D), EXPERT_DIM ** -0.5 * BETA),
        "sh_w_gate": nrm((L, D, SHARED_DIM), D ** -0.5),
        "sh_w_up": nrm((L, D, SHARED_DIM), D ** -0.5),
        "sh_w_down": nrm((L, SHARED_DIM, D), SHARED_DIM ** -0.5 * BETA),
        "ple_w_proj": nrm((L, PLE_DIM, D), PLE_DIM ** -0.5 * BETA),
        "ple_w_gate": nrm((L, D, D), D ** -0.5),
        "ln2_g": 1.0 + nrm((L, D), 0.02),
        "ln2_b": nrm((L, D), 0.02),
    }

def reference(x, p, w_in, nsa_pe_k, nsa_w1_k, nsa_w2_k, nsa_pe_v, nsa_w1_v, nsa_w2_v, swa_sinks,
              diff_lq1, diff_lk1, diff_lq2, diff_lk2, diff_norm_g, w_branch_a, w_branch_b, w_branch_c,
              w_out, ln1_g, ln1_b, router_w, router_bias, exp_w_gate, exp_w_up, exp_w_down,
              sh_w_gate, sh_w_up, sh_w_down, ple_w_proj, ple_w_gate, ln2_g, ln2_b):
    B, S, D = x.shape
    split_points = np.cumsum(IN_SIZES)[:-1].tolist()
    slopes_a = alibi_slopes(NSA_HEADS)
    slopes_b = alibi_slopes(SWA_HEADS)
    slopes_c = alibi_slopes(DIFF_HEADS)
    for i in range(DEPTH):
        proj = x @ w_in[i]
        (q_a, kc_a, vc_a, ks_a, vs_a, kw_a, vw_a, g_a,
         q_b, k_b, v_b, q_c, k_c, v_c, g_m) = jnp.split(proj, split_points, axis=-1)

        o_a = nsa_attention(
            q_a.reshape(B, S, NSA_HEADS, HEAD_DIM),
            kc_a.reshape(B, S, NSA_KV, HEAD_DIM), vc_a.reshape(B, S, NSA_KV, HEAD_DIM),
            ks_a.reshape(B, S, NSA_KV, HEAD_DIM), vs_a.reshape(B, S, NSA_KV, HEAD_DIM),
            kw_a.reshape(B, S, NSA_KV, HEAD_DIM), vw_a.reshape(B, S, NSA_KV, HEAD_DIM),
            g_a.reshape(B, S, NSA_HEADS, 3),
            nsa_pe_k[i], nsa_w1_k[i], nsa_w2_k[i], nsa_pe_v[i], nsa_w1_v[i], nsa_w2_v[i], slopes_a)

        o_b = banded_gqa(q_b.reshape(B, S, SWA_HEADS, HEAD_DIM), k_b.reshape(B, S, SWA_KV, HEAD_DIM),
                         v_b.reshape(B, S, SWA_KV, HEAD_DIM), SWA_WINDOW, slopes_b,
                         sinks=swa_sinks[i]).reshape(B, S, SWA_HEADS * HEAD_DIM)

        lambda_init = 0.8 - 0.6 * math.exp(-0.3 * i)
        lam = (jnp.exp(jnp.sum(diff_lq1[i].astype(jnp.float32) * diff_lk1[i].astype(jnp.float32)))
               - jnp.exp(jnp.sum(diff_lq2[i].astype(jnp.float32) * diff_lk2[i].astype(jnp.float32)))
               + lambda_init)
        o_c = diff_attention(q_c.reshape(B, S, DIFF_HEADS, 2, HEAD_DIM), k_c.reshape(B, S, DIFF_HEADS, 2, HEAD_DIM),
                             v_c.reshape(B, S, DIFF_HEADS, 2 * HEAD_DIM), lam, lambda_init, slopes_c, diff_norm_g[i])

        g = jax.nn.sigmoid(g_m).reshape(B, S, 3, D)
        merged = (g[:, :, 0] * (o_a @ w_branch_a[i]) + g[:, :, 1] * (o_b @ w_branch_b[i])
                  + g[:, :, 2] * (o_c @ w_branch_c[i]))
        x = layer_norm(ALPHA * x + merged @ w_out[i], ln1_g[i], ln1_b[i])

        ffn = moe(x, router_w[i], router_bias[i], exp_w_gate[i], exp_w_up[i], exp_w_down[i],
                  sh_w_gate[i], sh_w_up[i], sh_w_down[i])
        ple = jax.nn.sigmoid(x @ ple_w_gate[i]) * (p[i] @ ple_w_proj[i])
        x = layer_norm(ALPHA * x + ffn + ple, ln2_g[i], ln2_b[i])
    return x


_drawn_inputs = setup_inputs


def setup_inputs(seed=0):
    import zlib

    import numpy as np

    out = dict(_drawn_inputs(seed))
    spreads = {}
    factors = {'nsa_pe_k': 130.506,
     'nsa_pe_v': 4.447,
     'diff_lq1': 7.15,
     'diff_norm_g': 3.188,
     'ln2_g': 24.346,
     'ln2_b': 23.045}
    for name, (base, spread) in spreads.items():
        noise = np.random.default_rng([zlib.crc32(name.encode()), seed]).standard_normal(out[name].shape)
        drawn = base * np.exp(spread * noise) if base else spread * noise
        out[name] = __import__('jax').numpy.asarray(drawn.astype(out[name].dtype))
    for name, factor in factors.items():
        out[name] = (out[name] * factor).astype(out[name].dtype)
    return out
```

```python
import math

import numpy as np

import concourse.bass as bass
from concourse import mybir
from contextlib import ExitStack

F32 = mybir.dt.float32
BF16 = mybir.dt.bfloat16
I32 = mybir.dt.int32
U32 = mybir.dt.uint32
ALU = mybir.AluOpType
ACT = mybir.ActivationFunctionType
AXX = mybir.AxisListType.X

P = 128
T, D = 512, 1024
NT, ND = T // P, D // P
DH = 64
SCALE = DH ** -0.5
NEXP, TOPK, NGRP, TOPG = 64, 8, 8, 4
GSZ = NEXP // NGRP
F = 256
NF = F // P
ROUTED_SCALE = 2.5
ALPHA = 2 ** 0.25
EPS = 1e-5
LAMBDA_INIT = 0.8 - 0.6 * math.exp(0.0)
NBLK = T // 64
HUGE = 3e32
CAP = 128
NPASS = T // CAP
YROWS = TOPK * T

C_QA, C_KC, C_VC, C_KS, C_VS, C_KW, C_VW, C_GA = 0, 512, 640, 768, 896, 1024, 1152, 1280
C_QB, C_KB, C_VB, C_QC, C_KD, C_VD, C_GM = 1304, 1816, 1944, 2072, 2584, 3096, 3608
IN_CHUNKS_FIRST = [(0, 256), (256, 512), (512, 768), (768, 1024), (1024, 1304)]
IN_CHUNKS_REST = [(c, c + 256) for c in range(C_QB, 6680, 256)]
NW1 = 4
N_FIRST = len(IN_CHUNKS_FIRST)
REST0 = N_FIRST + 2 * NW1
NSLOT, SLOT = 4, 2240
BIG = 2 * SLOT

JOBS = [(kind, g, i) for i in range(NT) for g in range(2) for kind in ("slc", "win", "cmp")]
JOBS += [("swa", g, i) for i in range(NT) for g in range(2)]
JOBS += [("dif", g, i) for i in range(NT) for g in range(2)]
NJ = len(JOBS)


def keys_of(kind, i):
    if kind == "cmp":
        return 0, NBLK
    lo = max(0, i - 1) if kind == "swa" else 0
    return lo, (i + 1 - lo) * P


def blocks_of(kind, i):
    return 1 if kind == "cmp" else keys_of(kind, i)[1] // P


def turns_of(kind, i):
    return 2 if kind == "dif" else blocks_of(kind, i)


TURN0 = np.cumsum([0] + [turns_of(k, i) for k, g, i in JOBS]).tolist()
CLOSES = [k != "slc" and k != "win" for k, g, i in JOBS]
OUT0 = np.cumsum([0] + [int(c) for c in CLOSES]).tolist()


def build(nc, A, out):
    ctx = ExitStack()
    with ctx:
        def sem(name):
            return ctx.enter_context(nc.semaphore(name))

        ARENA = 52000
        arena = ctx.enter_context(nc.sbuf_tensor("arena", [P, ARENA], F32))
        small = ctx.enter_context(nc.sbuf_tensor("small", [P, 1024], F32))

        def at(off, n):
            return arena[:, off:off + n]

        W = at(0, NSLOT * SLOT)
        qa = at(8960, 2048).rearrange("p (j t) -> p j t", t=T)
        qb = at(11008, 2048).rearrange("p (j t) -> p j t", t=T)
        qc = at(13056, 2048).rearrange("p (j t) -> p j t", t=T)
        kd = at(15104, 2048).rearrange("p (j t) -> p j t", t=T)
        vd = at(17152, 2048).rearrange("p (i c) -> p i c", i=NT)
        ks, kw = at(19200, 512), at(19712, 512)
        vs = at(20224, 512).rearrange("p (i c) -> p i c", i=NT)
        vw = at(20736, 512).rearrange("p (i c) -> p i c", i=NT)
        kb = at(21248, 512)
        vb = at(21760, 512).rearrange("p (i c) -> p i c", i=NT)
        KV = at(22272, 1024).rearrange("p (w l c) -> p w l c", w=2, c=16)
        hcx, hcu, hct = at(23296, 512), at(23808, 512), at(24320, 256)
        xT = at(24576, 4096).rearrange("p (k t) -> p k t", t=T)
        gm = at(28672, 12288).rearrange("p (m t) -> p m t", t=T)
        S = at(40960, 4096).rearrange("p (u n) -> p u n", n=T)
        PT = at(45056, 2048).rearrange("p (u n) -> p u n", n=T)
        oa = at(47104, 2048).rearrange("p (j t) -> p j t", t=T)
        ob = at(49152, 2048).rearrange("p (j t) -> p j t", t=T)
        dist = at(51200, T)
        distw = at(51712, 2 * P)
        distc = at(51968, NT * NBLK).rearrange("p (i n) -> p i n", i=NT)
        x0 = at(28672, 4096).rearrange("p (i d) -> p i d", i=NT)
        odn = at(19200, 2048).rearrange("p (i c) -> p i c", i=NT)
        oc = at(8960, 2048).rearrange("p (j t) -> p j t", t=T)
        merged = at(11008, 4096).rearrange("p (m t) -> p m t", t=T)
        xr = at(15104, 4096).rearrange("p (i d) -> p i d", i=NT)
        x1 = at(28672, 4096).rearrange("p (i d) -> p i d", i=NT)
        acc = at(32768, 4096).rearrange("p (i d) -> p i d", i=NT)
        lnp = at(36864, 4096).rearrange("p (w d) -> p w d", w=4)
        x1T = xT
        z = at(40960, 2048).rearrange("p (r d) -> p r d", r=2)
        mtmp = at(43008, 1024).rearrange("p (r t) -> p r t", r=2)
        ppw = at(45056, 2048).rearrange("p (k d) -> p k d", k=2)
        pn = at(47104, 1024).rearrange("p (i c) -> p i c", i=NT)
        pT = at(49152, 1024).rearrange("p (k t) -> p k t", k=2)
        rw = at(22272, 512).rearrange("p (k e) -> p k e", k=ND)
        NR, ESLOT = 4, 3 * ND * F

        def eslot(n):
            o = ((n + 2) % NR) * ESLOT
            return (at(o, 2 * ND * F).rearrange("p (w k f) -> p w k f", w=2, k=ND),
                    at(o + 2 * ND * F, NF * D).rearrange("p (k d) -> p k d", k=NF))

        xg = at(40960, 4096).rearrange("p (r d) -> p r d", r=NR)
        xgT = at(49152, 2048).rearrange("p (r k s) -> p r k s", r=2, k=ND)
        y = at(24576, 4096).rearrange("p (r d) -> p r d", r=NR)
        sg = at(48128, 512).rearrange("p (r f) -> p r f", r=2)
        h = at(48640, 512).rearrange("p (r f) -> p r f", r=2)
        NHOT = 16
        HOT0 = [0, 10, 20, 30, 40, 46, 52, 58, NEXP]
        onehot = at(28672, 4096).bitcast(BF16).rearrange("p (r i s) -> p r i s", r=NHOT, i=NT)
        ple_sg = at(43008, 1024).rearrange("p (r t) -> p r t", r=2)
        RW5 = at(47104, 640).bitcast(BF16).rearrange("p (e i c) -> p e i c", e=NEXP, c=5)
        posE = at(47744, 256).rearrange("p (e i) -> p e i", i=NT)
        hT = at(51200, 512).rearrange("p (r k s) -> p r k s", r=2, k=NF)
        dest = at(51712, 32).bitcast(U32).rearrange("p (i k) -> p i k", i=NT)
        def last_rows(n):
            return at(n * D, D) if n < NT * TOPK - 4 else at(40960 + (n - NT * TOPK + 4) * D, D)


        def rt(n, w=256):
            return at(8960 + 256 * n, w)

        sc, bi, m1, rep, sel, ws = [rt(n).rearrange("p (i e) -> p i e", i=NT) for n in range(6)]
        g8 = rt(6).rearrange("p (i g c) -> p i g c", i=NT, g=NGRP)
        selb = at(8960 + 1792, 128).bitcast(BF16).rearrange("p (i e) -> p i e", i=NT)
        gs = at(10880, 48).rearrange("p (i g) -> p i g", i=NT)
        gr = at(10928, 48).rearrange("p (i g) -> p i g", i=NT)
        gt8 = at(10976, 32).rearrange("p (i g) -> p i g", i=NT)
        gmask = at(11008, 32).rearrange("p (i g) -> p i g", i=NT)
        gneg = at(11040, 32).rearrange("p (i g) -> p i g", i=NT)
        v8 = at(11072, 32).rearrange("p (i g) -> p i g", i=NT)
        dd = at(11136, 256).rearrange("p (i e) -> p i e", i=NT)
        d8 = at(11392, 32).rearrange("p (i g) -> p i g", i=NT)
        wr1 = at(11424, 256).rearrange("p (i e) -> p i e", i=NT)
        wsum = at(11680, 4)
        wrec = at(11684, 4)
        cmax = at(11688, 1)
        before = [at(11968, 64), at(12032, 64)]
        minus_p = at(12096, 1)
        pos1 = at(11712, 256).rearrange("p (i e) -> p i e", i=NT)

        def sm(o, n):
            return small[:, o:o + n]

        ident = sm(0, 128)
        iota_s = sm(128, 64).bitcast(BF16)
        tri = sm(192, 64).bitcast(BF16)
        ones = sm(256, 64).bitcast(BF16)
        slot_row = sm(320, 64)
        negm = sm(384, 8).rearrange("p (r j) -> p r j", r=2)
        esum = sm(392, 8).rearrange("p (r j) -> p r j", r=2)
        fac = sm(400, 8).rearrange("p (r j) -> p r j", r=2)
        sinks = sm(408, 8)
        lamv = sm(416, 4)
        ga = sm(420, 96).rearrange("p (i c) -> p i c", i=NT)
        kcmp = sm(516, 8)
        pe2 = sm(524, 64).rearrange("p (w l) -> p w l", w=2)
        gcol = sm(588, 1)
        ssq, rms = sm(592, 16), sm(608, 16)
        stats = sm(624, 12).rearrange("p (c s) -> p c s", c=2)
        mv, var_e, rstd = sm(636, 2), sm(638, 1), sm(639, 1)
        vcmp = sm(640, 128)
        hcT = sm(768, 64).rearrange("p (f c) -> p f c", f=4)
        IDX = sm(832, 64)
        WG = sm(896, 64)
        cnt = sm(960, 1).bitcast(I32)
        lamt = sm(961, 4)
        idxr = sm(965, 4).bitcast(U32)
        idyr = sm(969, 4).bitcast(U32)
        wgr = sm(973, 4)
        small2 = ctx.enter_context(nc.sbuf_tensor("small2", [P, 128], F32))
        rbias = small2[:, 64:128]
        IDY = small2[:, 0:64]
        w2 = hct
        pe_raw = at(45056, 256).rearrange("p (w l) -> p w l", w=2)
        lq = at(45312, 256).rearrange("p (w d) -> p w d", w=4)

        bank = [ctx.enter_context(nc.psum_tensor(f"bank{n}", [P, 512], F32)) for n in range(8)]
        x1_dram = nc.dram_tensor("x1_rows", (T, D), F32, kind="Internal").ap()
        y_dram = nc.dram_tensor("y_rows", (YROWS, D), F32, kind="Internal").ap()

        x_in = [sem(f"x_in{i}") for i in range(NT)]
        const_in = sem("const_in")
        w_in = [sem(f"w_in{s}") for s in range(NSLOT)]
        w_used = sem("w_used")
        pool_const = sem("pool_const")
        group_done = sem("group_done")
        group_out = sem("group_out")
        pe_added = sem("pe_added")
        chain = sem("vector_chain")
        hc_done, hc_copied, hc_cubic, hc_tanh, hc_ready = (sem(n) for n in (
            "hc_done", "hc_copied", "hc_cubic", "hc_tanh", "hc_ready"))
        hct_done, hct_out, cmp_done, cmp_out = (sem(n) for n in (
            "hct_done", "hct_out", "cmp_done", "cmp_out"))
        ga_ready, lam_dot, lam_exp, lam_ready = (sem(n) for n in (
            "ga_ready", "lam_dot", "lam_exp", "lam_ready"))
        scored, biased, max_ready, exped, probs = (sem(n) for n in (
            "scored", "biased", "max_ready", "exped", "probs"))
        turned, turned_out, pv_done, o_done, o_out = (sem(n) for n in (
            "turned", "turned_out", "pv_done", "o_done", "o_out"))
        sq_done, rms_in, rms_root, od_ready, oct_done, oct_out = (sem(n) for n in (
            "sq_done", "rms_in", "rms_root", "od_ready", "oct_done", "oct_out"))
        big_in = [sem(f"big_in{s}") for s in range(2)]
        big_used = sem("big_used")
        sig_done, branch_done, branch_used, merged_ready = (sem(n) for n in (
            "sig_done", "branch_done", "branch_used", "merged_ready"))
        xr_in, late_in, ppw_in = sem("xr_in"), sem("late_in"), sem("ppw_in")
        att_done, att_used, var_ready, root_ready, x1_ready = (sem(n) for n in (
            "att_done", "att_used", "var_ready", "root_ready", "x1_ready"))
        residual_in = sem("residual_in")
        x1t_done, x1t_out, x1_stored = sem("x1t_done"), sem("x1t_out"), sem("x1_stored")
        pt_done, pt_out = sem("pt_done"), sem("pt_out")
        route_done, route_sig, sel_ready, pos_done, pos_used = (sem(n) for n in (
            "route_done", "route_sig", "sel_ready", "pos_done", "pos_used"))
        ple_done, ple_sig, ple_used = sem("ple_done"), sem("ple_sig"), sem("ple_used")
        sh_gu, sh_sig, sh_h, sh_ht, sh_hto, sh_y, sh_used = (sem(n) for n in (
            "sh_gu", "sh_sig", "sh_h", "sh_ht", "sh_hto", "sh_y", "sh_used"))
        index_chain = sem("index_chain")
        cnt_ready, hot_ready, hot_used, idx_done, idx_used = (sem(n) for n in (
            "cnt_ready", "hot_ready", "hot_used", "idx_done", "idx_used"))
        xg_zero = sem("xg_zero")
        pool_turn = sem("pool_turn")
        wgu_in = [sem(f"wgu_in{s}") for s in range(NR)]
        wd_in = [sem(f"wd_in{s}") for s in range(NR)]
        col_ready = sem("col_ready")
        ycol_ready = sem("ycol_ready")
        gathered = [sem(f"gathered{s}") for s in range(NR)]
        scattered = [sem(f"scattered{s}") for s in range(NR)]
        xgt_done, xgt_out, gu_done, e_sig, h_ready, ht_done, ht_out, y_done, y_out = (
            sem(n) for n in ("xgt_done", "xgt_out", "gu_done", "e_sig", "h_ready", "ht_done",
                             "ht_out", "y_done", "y_out"))
        row_in = [sem(f"row_in{s}") for s in range(NT * TOPK)]
        row_added, out_ready, stored = sem("row_added"), sem("out_ready"), sem("stored")
        experts_done = sem("experts_done")

        w_rows = A["w_in"][0].rearrange("(k p) c -> p k c", p=P)
        w1k = A["nsa_w1_k"][0].rearrange("(a p) f -> p a f", p=P)
        w1v = A["nsa_w1_v"][0].rearrange("(a p) f -> p a f", p=P)

        def slot_of(n):
            return n % NSLOT

        def chunk(n, width=256):
            o = slot_of(n) * SLOT
            return W[:, o:o + ND * width].rearrange("p (k c) -> p k c", k=ND)

        def paired(col, c, n):
            for two in range(2):
                for j in range(2):
                    a = col + DH * (2 * c + j + 4 * two)
                    yield w_rows[:, :, a:a + DH], chunk(n)[:, :, P * j + DH * two:P * j + DH * two + DH]

        def chunk_loads():
            for n, (a, b) in enumerate(IN_CHUNKS_FIRST):
                yield list(paired(C_QA, n, n)) if n < 2 else [(w_rows[:, :, a:b], chunk(n, b - a))]
            for w, src in enumerate((w1k, w1v)):
                for c in range(NW1):
                    yield [(src[:, ND * c:ND * c + ND, :], chunk(N_FIRST + NW1 * w + c))]
            for n, (a, b) in enumerate(IN_CHUNKS_REST):
                yield (list(paired(C_QB, n, REST0 + n)) if n < 2 else
                       [(w_rows[:, :, a:b], chunk(REST0 + n))])

        def w_count(n):
            return 16 * sum(4 if m in (0, 1, REST0, REST0 + 1) else 1
                            for m in range(n % NSLOT, n + 1, NSLOT))

        def pair_groups(n, dst):
            return [("T", n + j // 2, (j % 2) * P, dst[:, j, :], SCALE, j % 2) for j in range(4)]

        FIRST = pair_groups(0, qa)
        FIRST += [("T", 2, 0, "kc", 1.0, 0), ("T", 2, P, "vc", 1.0, 1),
                  ("T", 3, 0, ks, 1.0, 0), ("N", 3, P, vs, 1.0, 1),
                  ("T", 4, 0, kw, 1.0, 0), ("N", 4, P, vw, 1.0, 0), ("G", 4, 2 * P, ga, 1.0, 1)]
        REST = pair_groups(REST0, qb)
        REST += [("T", REST0 + 2, 0, kb, 1.0, 0), ("N", REST0 + 2, P, vb, 1.0, 1)]
        for base, dst, scale in ((3, qc, SCALE), (5, kd, 1.0)):
            REST += [("T", REST0 + base + j // 2, (j % 2) * P, dst[:, j, :], scale, j % 2)
                     for j in range(4)]
        for c in range(2):
            REST += [("N2", REST0 + 7 + c, 2 * i, vd[:, 2 * i:2 * i + 2, 256 * c:256 * c + 256], 1.0, i)
                     for i in range(2)]
        REST += [("T", REST0 + 9 + m // 2, (m % 2) * P, gm[:, m, :], 1.0, m % 2) for m in range(24)]
        NXG = 2 * NT + 1
        G0, G1 = NXG, NXG + len(FIRST)
        N_STEPS = NJ
        PER_STEP = [2 if s in (4, 12) else 1 for s in range(N_STEPS)]
        assert sum(PER_STEP) == len(REST)
        REST_AT = np.cumsum([0] + PER_STEP).tolist()

        def group_bank(n):
            return bank[6 + n % 2] if n < G1 else bank[7]

        def need_group(kind):
            return {"slc": G1, "win": G1, "cmp": G1, "swa": G1 + 6, "dif": G1 + 18}[kind]

        def width_of(n):
            return 280 if n == 4 else 256

        def unit_operands(kind, g, i, j):
            lo, n = keys_of(kind, i)
            tq = slice(i * P, (i + 1) * P)
            if kind == "dif":
                r, hd = j % 2, 2 * g + j // 2
                rows = slice(DH * r, DH * r + DH)
                return qc[rows, hd, tq], kd[rows, hd, 0:n]
            rows = slice(DH * g, DH * g + DH)
            q = (qb if kind == "swa" else qa)[rows, j, tq]
            k = {"slc": ks, "win": kw, "swa": kb, "cmp": kcmp}[kind]
            return q, k[rows, lo * P:lo * P + n]

        def slope_of(kind, g, j):
            return 2.0 ** (-2.0 * (2 * g + j // 2 + 1)) if kind == "dif" else 2.0 ** -(4 * g + j + 1)

        def distances(kind, i, n):
            if kind == "cmp":
                return distc[:, i, :]
            if kind == "swa":
                return distw[:, 2 * P - n:2 * P]
            return dist[:, T - n:T]

        gu_w, down_w = {}, {}
        big0 = W[:, 0:4096]
        big1 = W[:, BIG:BIG + 4096]
        bigs = [big0, big1]
        wb = [bigs[b % 2].rearrange("p (j d) -> p j d", j=4) for b in range(3)]
        wo_h = [bigs[1].rearrange("p (k d) -> p k d", k=ND), bigs[0].rearrange("p (k d) -> p k d", k=ND)]
        pg_h = [bigs[1].rearrange("p (k d) -> p k d", k=ND), bigs[0].rearrange("p (k d) -> p k d", k=ND)]
        sgu = bigs[1].rearrange("p (w k f) -> p w k f", w=2, k=ND)
        sdn = bigs[0][:, 0:2048].rearrange("p (k d) -> p k d", k=NF)
        B_BR, B_WO, B_PG, B_SG, B_SD = 0, 3, 5, 7, 8
        BIG_DMAS = [2, 2, 1, 1, 1, 1, 1, 2, 1]

        def big_count(n):
            return 16 * sum(BIG_DMAS[m] for m in range(n % 2, n + 1, 2))

        def turn(b, it, r):
            return NEXP * b + NR * it + r

        block = ctx.enter_context(nc.Block())

        @block.sync
        def _(sp):
            for i in range(NT):
                sp.dma_start(x0[:, i, :], A["x"][0, i * P:(i + 1) * P, :]).then_inc(x_in[i], 16)
            n_small = 0
            for n, parts in enumerate(chunk_loads()):
                if n >= NSLOT:
                    sp.wait_ge(w_used, n - NSLOT + 1)
                for src, dst in parts:
                    sp.dma_start(dst, src).then_inc(w_in[slot_of(n)], 16)
                n_small = n + 1

            def big_load(n, parts):
                if n < 2:
                    sp.wait_ge(w_used, n_small)
                else:
                    sp.wait_ge(big_used, n - 1)
                for dst, src in parts:
                    sp.dma_start(dst, src).then_inc(big_in[n % 2], 16)

            for b, name in enumerate(("w_branch_a", "w_branch_b", "w_branch_c")):
                src = A[name][0]
                if b < 2:
                    src = src.rearrange("(two j d) n -> two d j n", two=2, j=4)
                    parts = [(wb[b][DH * s:DH * s + DH], src[s]) for s in range(2)]
                else:
                    parts = [(wb[b], src.rearrange("(j p) n -> p j n", p=P))]
                big_load(B_BR + b, parts)
                if b == 1:
                    sp.wait_ge(o_out, OUT0[NJ])
                    sp.dma_start(xr, A["x"][0].rearrange("(i p) d -> p i d", p=P)).then_inc(xr_in, 16)
                    sp.dma_start(ppw, A["ple_w_proj"][0].rearrange("(k p) d -> p k d", p=P)).then_inc(ppw_in, 16)
            wo = A["w_out"][0].rearrange("(k p) d -> p k d", p=P)
            big_load(B_WO, [(wo_h[0], wo[:, :, 0:512])])
            big_load(B_WO + 1, [(wo_h[1], wo[:, :, 512:1024])])
            sp.wait_ge(merged_ready, 1)
            for n, name in enumerate(("ln1_g", "ln1_b", "ln2_g", "ln2_b")):
                sp.dma_start(lnp[:, n, :], A[name][0:1, :].to_broadcast([P, D])).then_inc(late_in, 16)
            sp.wait_ge(branch_done, 24)
            sp.dma_start(pn, A["p"][0, 0].rearrange("(i p) c -> p i c", p=P)).then_inc(late_in, 16)
            sp.dma_start(rw, A["router_w"][0].rearrange("(k p) e -> p k e", p=P)).then_inc(late_in, 16)
            sp.dma_start(rbias, A["router_bias"][0:1, :].to_broadcast([P, NEXP])).then_inc(late_in, 16)
            pg = A["ple_w_gate"][0].rearrange("(k p) d -> p k d", p=P)
            big_load(B_PG, [(pg_h[0], pg[:, :, 0:512])])
            big_load(B_PG + 1, [(pg_h[1], pg[:, :, 512:1024])])
            big_load(B_SG, [(sgu[:, w], A[name][0].rearrange("(k p) f -> p k f", p=P))
                            for w, name in enumerate(("sh_w_gate", "sh_w_up"))])
            big_load(B_SD, [(sdn, A["sh_w_down"][0].rearrange("(k p) d -> p k d", p=P))])

            def load_expert(b, it, r):
                n = turn(b, it, r)
                e = NR * it + r
                gu, dn = eslot(r)
                first = b == 0 and isinstance(it, int) and it == 0
                if not first:
                    sp.wait_ge(gu_done, n - NR + 1)
                for w, name in enumerate(("exp_w_gate", "exp_w_up")):
                    sp.dma_start(gu[:, w], A[name][0, bass.ds(e, 1)].rearrange(
                        "e (p k) f -> p (e k) f", p=P)).then_inc(wgu_in[r], 16)
                if not first:
                    sp.wait_ge(y_done, n - NR + 1)
                sp.dma_start(dn, A["exp_w_down"][0, bass.ds(e, 1)].rearrange(
                    "e (p k) d -> p (e k) d", p=P)).then_inc(wd_in[r], 16)

            sp.wait_ge(route_done, 1)
            load_expert(0, 0, 0)
            load_expert(0, 0, 1)
            sp.wait_ge(sh_y, NT)
            sp.wait_ge(pos_used, 1)
            load_expert(0, 0, 2)
            load_expert(0, 0, 3)

            def expert_loads(b, it0):
                with sp.Fori(it0, NEXP // NR) as it:
                    for r in range(NR):
                        load_expert(b, it, r)

            expert_loads(0, 1)
            sp.wait_ge(cnt_ready, 1)
            most = sp.value_load(cnt[0:1, 0:1], min_val=0, max_val=T)
            with sp.If(most > CAP):
                expert_loads(1, 0)
                with sp.If(most > 2 * CAP):
                    expert_loads(2, 0)
                    with sp.If(most > 3 * CAP):
                        expert_loads(3, 0)
                        sp.nop()
                    sp.nop()
                sp.nop()
            for i in range(NT):
                sp.wait_ge(out_ready, i + 1)
                sp.dma_start(out[0, i * P:(i + 1) * P, :], acc[:, i, :]).then_inc(stored, 16)
            sp.wait_ge(stored, 16 * NT)

        @block.gpsimd
        def _(pool):
            n_const = [0]

            def made(ins):
                n_const[0] += 1
                ins.then_inc(pool_const, 1)
                pool.wait_ge(pool_const, n_const[0])

            made(pool.memset(ident, 0.0))
            made(pool.affine_select(out=ident, in_=ident, compare_op=ALU.not_equal, fill=1.0, base=0,
                                    pattern=[[-1, P]], channel_multiplier=1))
            made(pool.memset(ones, 1.0))
            made(pool.affine_select(out=tri, in_=ones, compare_op=ALU.is_gt, fill=0.0, base=0,
                                    pattern=[[1, P]], channel_multiplier=-1))
            made(pool.iota(iota_s, pattern=[[1, P]], base=0, channel_multiplier=0,
                           allow_small_or_imprecise_dtypes=True))
            made(pool.iota(slot_row, pattern=[[0, NEXP]], base=0, channel_multiplier=1,
                           allow_small_or_imprecise_dtypes=True))
            made(pool.iota(dist, pattern=[[-1, T]], base=T - P, channel_multiplier=1,
                           allow_small_or_imprecise_dtypes=True))
            made(pool.affine_select(out=dist, in_=dist, compare_op=ALU.is_ge, fill=HUGE, base=T - P,
                                    pattern=[[-1, T]], channel_multiplier=1))
            made(pool.iota(distw, pattern=[[-1, 2 * P]], base=P, channel_multiplier=1,
                           allow_small_or_imprecise_dtypes=True))
            made(pool.affine_select(out=distw, in_=distw, compare_op=ALU.is_ge, fill=HUGE, base=P,
                                    pattern=[[-1, 2 * P]], channel_multiplier=1))
            made(pool.affine_select(out=distw, in_=distw, compare_op=ALU.is_gt, fill=HUGE, base=0,
                                    pattern=[[1, 2 * P]], channel_multiplier=-1))
            made(pool.iota(distc, pattern=[[P, NT], [-64, NBLK]], base=-63, channel_multiplier=1,
                           allow_small_or_imprecise_dtypes=True))
            made(pool.affine_select(out=distc, in_=distc, compare_op=ALU.is_ge, fill=HUGE, base=-63,
                                    pattern=[[P, NT], [-64, NBLK]], channel_multiplier=1))
            assert n_const[0] == 13
            for i in range(NT):
                pool.wait_ge(x1_ready, i + 1)
                pool.dma_start(x1_dram[i * P:(i + 1) * P, :], x1[:, i, :]).then_inc(x1_stored, 16)
            pool.wait_ge(pt_done, 2)
            pool.iota(RW5[:, :, :, 0], pattern=[[0, NEXP], [0, NT]], base=0, channel_multiplier=1,
                      allow_small_or_imprecise_dtypes=True)
            pool.iota(RW5[:, :, :, 1], pattern=[[0, NEXP], [P, NT]], base=-1024, channel_multiplier=0,
                      allow_small_or_imprecise_dtypes=True).then_inc(xg_zero, 1)
            pool.wait_ge(ple_used, 2 * NT)
            pool.memset(xg, 0.0).then_inc(xg_zero, 1)
            pool.wait_ge(xg_zero, 2)
            pool.wait_ge(x1_stored, 16 * NT)

            last_token = pool.to_reg(T - 1)
            last_row = pool.to_reg(YROWS - 1)

            def gather(b, it, r):
                n = turn(b, it, r)
                pool.wait_ge(col_ready, n + 1)
                if not (isinstance(n, int) and n < NR):
                    pool.wait_ge(xgt_done, 2 * (n - NR) + 2)
                pool.sem_inc(pool_turn, 1)
                pool.indirect_dma_start(
                    xg[:, r, :], None, x1_dram,
                    bass.IndirectOffsetOnAxis(ap=idxr[:, r:r + 1], axis=0),
                    bounds_check=last_token, oob_is_err=False).then_inc(gathered[r], 16)

            def scatter(b, it, r):
                n = turn(b, it, r)
                pool.wait_ge(y_out, 2 * n + 2)
                pool.sem_inc(pool_turn, 1)
                pool.indirect_dma_start(
                    y_dram, bass.IndirectOffsetOnAxis(ap=idyr[:, r:r + 1], axis=0),
                    y[:, r, :], None,
                    bounds_check=last_row, oob_is_err=False).then_inc(scattered[r], 16)

            def expert_rows(b):
                for r in range(NR):
                    gather(b, 0, r)
                last = NEXP // NR - 1
                with pool.Fori(0, last) as it:
                    for r in range(NR):
                        gather(b, it + 1, r)
                        scatter(b, it, r)
                for r in range(NR):
                    scatter(b, last, r)
                for s in range(NR):
                    pool.wait_ge(scattered[s], 16 * (NEXP // NR) * (b + 1))

            expert_rows(0)
            pool.wait_ge(cnt_ready, 1)
            most = pool.value_load(cnt[0:1, 0:1], min_val=0, max_val=T)
            with pool.If(most > CAP):
                expert_rows(1)
                with pool.If(most > 2 * CAP):
                    expert_rows(2)
                    with pool.If(most > 3 * CAP):
                        expert_rows(3)
                        pool.nop()
                    pool.nop()
                pool.nop()
            for i in range(NT):
                for k in range(TOPK):
                    n = i * TOPK + k
                    pool.indirect_dma_start(
                        last_rows(n), None, y_dram,
                        bass.IndirectOffsetOnAxis(ap=dest[:, i, k:k + 1], axis=0),
                        bounds_check=last_row, oob_is_err=False).then_inc(row_in[n], 16)

        @block.scalar
        def _(act):
            act.dma_start(pe_raw[0:32, 0, :], A["nsa_pe_k"][0].rearrange("(l two) d -> l (two d)", two=2)).then_inc(const_in, 16)
            act.dma_start(pe_raw[0:32, 1, :], A["nsa_pe_v"][0].rearrange("(l two) d -> l (two d)", two=2)).then_inc(const_in, 16)
            act.dma_start(w2[:, 0:128].rearrange("p (f d) -> p f d", f=2),
                          A["nsa_w2_k"][0].rearrange("(f p) d -> p f d", p=P)).then_inc(const_in, 16)
            act.dma_start(w2[:, 128:256].rearrange("p (f d) -> p f d", f=2),
                          A["nsa_w2_v"][0].rearrange("(f p) d -> p f d", p=P)).then_inc(const_in, 16)
            act.dma_start(sinks, A["swa_sinks"][0:1, :].to_broadcast([P, 8])).then_inc(const_in, 16)
            for n, name in enumerate(("diff_lq1", "diff_lk1", "diff_lq2", "diff_lk2")):
                act.dma_start(lq[:, n, :], A[name][0:1, :].to_broadcast([P, DH])).then_inc(const_in, 16)
            with nc.allow_non_contiguous_dma(reason="a column of 128 gains"):
                act.dma_start(gcol, A["diff_norm_g"][0].rearrange("(p o) -> p o", o=1)).then_inc(const_in, 16)
            act.wait_ge(lam_dot, 1)
            act.activation(lamt[:, 2:4], lamt[:, 0:2], ACT.Exp).then_inc(lam_exp, 1)
            for n in range(2 * NT):
                act.wait_ge(group_done, n + 1)
                i, half = n // 2, n % 2
                act.activation(xT[:, 4 * half:4 * half + 4, i * P:(i + 1) * P],
                               group_bank(n)[:, :].rearrange("p (k t) -> p k t", k=4), ACT.Copy).then_inc(group_out, 1)
            act.wait_ge(group_done, NXG)
            act.activation(pe2, group_bank(NXG - 1)[:, 0:64].rearrange("p (w l) -> p w l", w=2),
                           ACT.Copy).then_inc(group_out, 1)

            def group_evac(n, group):
                form, _, _, dst, scale, _ = group
                src = group_bank(n)
                act.wait_ge(group_done, n + 1)
                if isinstance(dst, str):
                    w = 0 if dst == "kc" else 1
                    for kv in range(2):
                        for par in range(2):
                            last = act.activation(
                                KV[DH * par:DH * par + DH, w, :, 8 * kv:8 * kv + 8],
                                src[DH * kv:DH * kv + DH, :].rearrange(
                                    "p (n l two) -> p two l n", n=NBLK, two=2)[:, par], ACT.Copy)
                    last.then_inc(group_out, 1)
                elif form == "G":
                    act.activation(dst, src[:, 0:96].rearrange("p (i c) -> p i c", i=NT),
                                   ACT.Sigmoid).then_inc(group_out, 1)
                elif form == "N":
                    act.activation(dst, src[:, :].rearrange("p (i c) -> p i c", i=NT), ACT.Copy).then_inc(group_out, 1)
                elif form == "N2":
                    act.activation(dst, src[:, :].rearrange("p (i c) -> p i c", i=2), ACT.Copy).then_inc(group_out, 1)
                else:
                    act.activation(dst, src[:, :], ACT.Copy, scale=scale).then_inc(group_out, 1)

            for n, group in enumerate(FIRST):
                group_evac(G0 + n, group)
            act.wait_ge(hc_done, 1)
            act.activation(hcx[0:16, :], bank[4][0:16, :], ACT.Copy).then_inc(hc_copied, 1)
            act.wait_ge(hc_cubic, 1)
            act.activation(hcu[0:16, :], hcu[0:16, :], ACT.Tanh, scale=math.sqrt(2 / math.pi)).then_inc(hc_tanh, 1)
            act.wait_ge(hct_done, 1)
            act.activation(hcT, bank[5][:, 0:64].rearrange("p (f c) -> p f c", f=4), ACT.Copy,
                           scale=0.5).then_inc(hct_out, 1)
            act.wait_ge(cmp_done, 1)
            act.activation(kcmp, bank[4][:, 0:8], ACT.Copy)
            act.activation(vcmp[0:8, :], bank[4][0:8, 128:256], ACT.Copy).then_inc(cmp_out, 1)

            def exps(s):
                kind, g, i = JOBS[s]
                n = keys_of(kind, i)[1] + (kind == "swa")
                act.wait_ge(max_ready, s + 1)
                for j in range(4):
                    row = S[:, 4 * (s % 2) + j, 0:n]
                    last = act.activation(row, row, ACT.Exp, bias=negm[:, s % 2, j:j + 1],
                                          accum_out=esum[:, s % 2, j:j + 1])
                last.then_inc(exped, 1)

            def turned_evacs(s, part):
                first, last = TURN0[s], TURN0[s + 1]
                for n in range(first, last)[:2] if part == 0 else range(first, last)[2:]:
                    act.wait_ge(turned, n + 1)
                    if n >= 4:
                        act.wait_ge(pv_done, n - 3)
                    act.activation(PT[:, n % 4, :], bank[4 + n % 2][:, :], ACT.Copy).then_inc(turned_out, 1)
                if CLOSES[s] and part:
                    kind, g, i = JOBS[s]
                    act.wait_ge(o_done, OUT0[s + 1])
                    rows = slice(DH * g, DH * g + DH)
                    if kind == "dif":
                        act.activation(odn[:, i, 256 * g:256 * g + 256], bank[6][:, 0:256], ACT.Copy).then_inc(o_out, 1)
                    else:
                        dst = ob if kind == "swa" else oa
                        act.activation(dst[rows, :, i * P:(i + 1) * P],
                                       bank[6][rows, :].rearrange("p (j t) -> p j t", j=4),
                                       ACT.Copy).then_inc(o_out, 1)

            for s in range(NJ + 1):
                if s < NJ:
                    exps(s)
                if s >= 1:
                    turned_evacs(s - 1, 0)
                if s < NJ:
                    for n in range(REST_AT[s], REST_AT[s + 1]):
                        group_evac(G1 + n, REST[n])
                if s >= 1:
                    turned_evacs(s - 1, 1)
            act.wait_ge(o_out, OUT0[NJ])
            for n in range(16):
                row = odn[:, n // 4, P * (n % 4):P * (n % 4) + P]
                last = act.activation(S[:, n // 4, P * (n % 4):P * (n % 4) + P], row, ACT.Square, accum_out=ssq[:, n:n + 1])
            last.then_inc(sq_done, 1)
            act.wait_ge(rms_in, 1)
            act.activation(rms, ssq, ACT.Sqrt).then_inc(rms_root, 1)
            act.wait_ge(group_out, G1 + len(REST))
            for n in range(24):
                if n == 16:
                    for hd in range(4):
                        act.wait_ge(oct_done, hd + 1)
                        act.activation(oc[:, hd, :], bank[4 + hd % 2][:, :], ACT.Copy,
                                       scale=gcol).then_inc(oct_out, 1)
                act.activation(gm[:, n, :], gm[:, n, :], ACT.Sigmoid).then_inc(sig_done, 1)
            def x1t_evac(i):
                for half in range(2):
                    n = 2 * i + half
                    act.wait_ge(x1t_done, n + 1)
                    act.activation(x1T[:, 4 * half:4 * half + 4, i * P:(i + 1) * P],
                                   bank[4 + half][:, :].rearrange("p (k t) -> p k t", k=4), ACT.Copy).then_inc(x1t_out, 1)

            def residual(i):
                act.wait_ge(x1_ready, i + 1)
                act.activation(acc[:, i, :], x1[:, i, :], ACT.Copy, scale=ALPHA).then_inc(residual_in, 1)

            for i in range(NT):
                act.wait_ge(var_ready, i + 1)
                act.activation(rstd, var_e, ACT.Sqrt).then_inc(root_ready, 1)
                if i >= 1:
                    x1t_evac(i - 1)
                    residual(i - 1)
            x1t_evac(NT - 1)
            residual(NT - 1)
            for k in range(2):
                act.wait_ge(pt_done, k + 1)
                act.activation(pT[:, k, :], bank[4 + k][:, :], ACT.Copy).then_inc(pt_out, 1)
            act.wait_ge(route_done, 1)
            act.activation(sc, bank[6][:, 0:256].rearrange("p (i e) -> p i e", i=NT), ACT.Sigmoid).then_inc(route_sig, 1)
            for n in range(2 * NT):
                act.wait_ge(ple_done, n + 1)
                if n >= 2:
                    act.wait_ge(ple_used, n - 1)
                act.activation(ple_sg[:, n % 2, :], bank[n % 2][:, :], ACT.Sigmoid).then_inc(ple_sig, 1)
            for i in range(NT):
                act.wait_ge(sh_gu, i + 1)
                act.activation(sg[:, i % 2, :], bank[i % 2][:, 0:F], ACT.Sigmoid).then_inc(sh_sig, 1)

            def xgt_evac(b, it, r):
                n = turn(b, it, r)
                for half in range(2):
                    act.wait_ge(xgt_done, 2 * n + half + 1)
                    if half == 0 and not (isinstance(n, int) and n < 2):
                        act.wait_ge(gu_done, n - 1)
                    act.activation(xgT[:, r % 2, 4 * half:4 * half + 4, :],
                                   bank[half][:, :].rearrange("p (k s) -> p k s", k=4), ACT.Copy).then_inc(xgt_out, 1)

            def gate_sig(b, it, r):
                n = turn(b, it, r)
                act.wait_ge(gu_done, n + 1)
                if not (isinstance(n, int) and n < 2):
                    act.wait_ge(h_ready, n - 1)
                act.activation(sg[:, r % 2, :], bank[2 + r % 2][:, 0:F], ACT.Sigmoid).then_inc(e_sig, 1)

            def y_evac(b, it, r):
                n = turn(b, it, r)
                act.wait_ge(y_done, n + 1)
                act.wait_ge(ycol_ready, n + 1)
                for half in range(2):
                    act.activation(y[:, r, 512 * half:512 * half + 512], bank[5 + half][:, :],
                                   ACT.Copy, scale=wgr[:, r:r + 1]).then_inc(y_out, 1)

            def expert_acts(b):
                xgt_evac(b, 0, 0)

                def step(it, r, before):
                    gate_sig(b, it, r)
                    xgt_evac(b, it + (r + 1) // NR, (r + 1) % NR)
                    if before is not None:
                        y_evac(b, *before)

                for r in range(NR):
                    step(0, r, (0, r - 1) if r else None)
                last = NEXP // NR - 1
                with act.Fori(1, last) as it:
                    for r in range(NR):
                        step(it, r, (it, r - 1) if r else (it - 1, NR - 1))
                for r in range(NR - 1):
                    step(last, r, (last, r - 1) if r else (last - 1, NR - 1))
                gate_sig(b, last, NR - 1)
                y_evac(b, last, NR - 2)
                y_evac(b, last, NR - 1)

            expert_acts(0)
            act.wait_ge(cnt_ready, 1)
            most = act.value_load(cnt[0:1, 0:1], min_val=0, max_val=T)
            with act.If(most > CAP):
                expert_acts(1)
                with act.If(most > 2 * CAP):
                    expert_acts(2)
                    with act.If(most > 3 * CAP):
                        expert_acts(3)
                        act.nop()
                    act.nop()
                act.nop()
            for i in range(NT):
                act.wait_ge(var_ready, NT + i + 1)
                act.activation(rstd, var_e, ACT.Sqrt).then_inc(root_ready, 1)

        @block.vector
        def _(dve):
            links = [0]
            in_loop = [False]

            def link(ins):
                links[0] += 1
                ins.then_inc(chain, 1)
                dve.wait_ge(chain, links[0])

            dve.memset(vcmp, 0.0)
            dve.memset(esum[:, :, :].rearrange("p r j -> p (r j)"), 0.0)
            dve.wait_ge(const_in, 16 * 10)
            link(dve.tensor_tensor(lq[:, 0:3:2, :], lq[:, 0:3:2, :], lq[:, 1:4:2, :], ALU.mult))
            dve.tensor_reduce(lamt[:, 0:2], lq[:, 0:3:2, :], axis=AXX, op=ALU.add).then_inc(lam_dot, 1)
            dve.wait_ge(lam_exp, 1)
            link(dve.tensor_tensor(lamt[:, 0:1], lamt[:, 3:4], lamt[:, 2:3], ALU.subtract))
            dve.memset(lamv, 1.0)
            link(dve.tensor_scalar(gcol, gcol, 1.0 - LAMBDA_INIT, None, ALU.mult))
            for j in (1, 3):
                last = dve.tensor_scalar(lamv[:, j:j + 1], lamt[:, 0:1], -LAMBDA_INIT, None, ALU.add)
            link(last)
            for w in range(2):
                dve.wait_ge(group_out, G0 + 4 + w + 1)
                dve.tensor_tensor(KV[:, w], KV[:, w], pe2[:, w, :].unsqueeze(2).to_broadcast([P, 32, 16]),
                                  ALU.add).then_inc(pe_added, 1)
            dve.wait_ge(hc_copied, 1)
            link(dve.tensor_tensor(hcu[0:16, :], hcx[0:16, :], hcx[0:16, :], ALU.mult))
            link(dve.tensor_scalar(hcu[0:16, :], hcu[0:16, :], 0.044715, 1.0, ALU.mult, ALU.add))
            dve.tensor_tensor(hcu[0:16, :], hcu[0:16, :], hcx[0:16, :], ALU.mult).then_inc(hc_cubic, 1)
            dve.wait_ge(hc_tanh, 1)
            dve.scalar_tensor_tensor(hcu[0:16, :], hcu[0:16, :], 1.0, hcx[0:16, :], ALU.add,
                                     ALU.mult).then_inc(hc_ready, 1)
            dve.wait_ge(pool_const, 13)

            def bias_and_max(s):
                kind, g, i = JOBS[s]
                n = keys_of(kind, i)[1]
                rows = S[:, 4 * (s % 2):4 * (s % 2) + 4, :]
                if s >= 2:
                    dve.wait_ge(turned, TURN0[s - 1])
                if kind == "cmp":
                    dve.memset(rows[:, :, NBLK:P], 0.0)
                if kind == "swa":
                    dve.tensor_copy(rows[:, :, n:n + 1], sinks[:, 4 * g:4 * g + 4].unsqueeze(2))
                for j in range(4):
                    dve.wait_ge(scored, 4 * s + j + 1)
                    last = dve.scalar_tensor_tensor(rows[:, j, 0:n], distances(kind, i, n),
                                                    -slope_of(kind, g, j), bank[j][:, 0:n],
                                                    ALU.mult, ALU.add)
                    last.then_inc(biased, 1)
                dve.wait_ge(biased, 4 * s + 4)
                if s >= 2:
                    dve.wait_ge(exped, s - 1)
                m = dve.tensor_reduce(negm[:, s % 2, :], rows[:, :, 0:n + (kind == "swa")], axis=AXX,
                                      op=ALU.max, negate=True)
                if kind == "cmp":
                    link(m)
                    m = dve.tensor_scalar(negm[:, s % 2, :], negm[:, s % 2, :], 1e29, None, ALU.min)
                m.then_inc(max_ready, 1)

            def weigh(s):
                kind, g, i = JOBS[s]
                n = keys_of(kind, i)[1]
                f = fac[:, s % 2, :]
                dve.wait_ge(exped, s + 1)
                e = esum[:, s % 2, :]
                if kind == "cmp":
                    link(dve.tensor_scalar(e, e, 1e-30, None, ALU.max))
                link(dve.reciprocal(f, e))
                if kind in ("slc", "win", "cmp"):
                    br = ("cmp", "slc", "win").index(kind)
                    gates = ga[:, i, 12 * g + br:12 * g + br + 10:3]
                    link(dve.tensor_tensor(f, f, gates, ALU.mult))
                if kind == "dif":
                    link(dve.tensor_tensor(f, f, lamv, ALU.mult))
                    for hh in range(2):
                        a, b = (S[:, 4 * (s % 2) + 2 * hh + r, 0:n] for r in range(2))
                        link(dve.tensor_scalar(b, b, f[:, 2 * hh + 1:2 * hh + 2], None, ALU.mult))
                        last = dve.scalar_tensor_tensor(a, a, f[:, 2 * hh:2 * hh + 1], b, ALU.mult, ALU.add)
                else:
                    for j in range(4):
                        row = S[:, 4 * (s % 2) + j, 0:n]
                        last = dve.tensor_scalar(row, row, f[:, j:j + 1], None, ALU.mult)
                last.then_inc(probs, 1)

            for s in range(NJ):
                bias_and_max(s)
                weigh(s)
            dve.wait_ge(sq_done, 1)
            dve.tensor_scalar(ssq, ssq, 1.0 / (2 * DH), EPS, ALU.mult, ALU.add).then_inc(rms_in, 1)
            dve.wait_ge(rms_root, 1)
            link(dve.reciprocal(rms, rms))
            for n in range(16):
                row = odn[:, n // 4, P * (n % 4):P * (n % 4) + P]
                last = dve.tensor_scalar(row, row, rms[:, n:n + 1], None, ALU.mult)
            last.then_inc(od_ready, 1)
            for n in range(24):
                m = n % 8
                dve.wait_ge(sig_done, n + 1)
                dve.wait_ge(branch_done, n + 1)
                dst = merged[:, m, :] if n < 8 else mtmp[:, n % 2, :]
                ins = dve.tensor_tensor(dst, bank[n % 4][:, :], gm[:, n, :], ALU.mult)
                ins.then_inc(branch_used, 1)
                if n >= 8:
                    dve.wait_ge(branch_used, n + 1)
                    last = dve.tensor_tensor(merged[:, m, :], merged[:, m, :], mtmp[:, n % 2, :], ALU.add)
                    if n == 23:
                        last.then_inc(merged_ready, 1)

            def layer_norm(src, dst, w, root):
                for c in range(2):
                    last = dve.bn_stats(stats[:, c, :], src[:, 512 * c:512 * c + 512])
                link(last)
                link(dve.bn_aggr(mv, stats))
                if root > 1:
                    dve.wait_ge(root_ready, root - 1)
                dve.tensor_scalar(var_e, mv[:, 1:2], EPS, None, ALU.add).then_inc(var_ready, 1)
                dve.wait_ge(root_ready, root)
                link(dve.reciprocal(rstd, rstd))
                link(dve.tensor_scalar(dst, src, mv[:, 0:1], rstd, ALU.subtract, ALU.mult))
                link(dve.tensor_tensor(dst, dst, lnp[:, w, :], ALU.mult))
                return dve.tensor_tensor(dst, dst, lnp[:, w + 1, :], ALU.add)

            dve.wait_ge(xr_in, 16)
            for i in range(NT):
                for half in range(2):
                    cols = slice(512 * half, 512 * half + 512)
                    dve.wait_ge(att_done, 2 * i + half + 1)
                    last = dve.scalar_tensor_tensor(z[:, i % 2, cols], xr[:, i, cols], ALPHA,
                                                    bank[2 * (i % 2) + half][:, :], ALU.mult, ALU.add)
                    last.then_inc(att_used, 1)
                dve.wait_ge(att_used, 2 * i + 2)
                if i == 0:
                    dve.wait_ge(late_in, 16 * 7)
                layer_norm(z[:, i % 2, :], x1[:, i, :], 0, i + 1).then_inc(x1_ready, 1)

            dve.wait_ge(route_sig, 1)
            dve.memset(gs[:, :, NGRP:NGRP + 4], -1e30)
            link(dve.tensor_tensor(bi, sc, rbias.unsqueeze(1).to_broadcast([P, NT, NEXP]), ALU.add))
            for i in range(NT):
                for g in range(NGRP):
                    last = dve.max(g8[:, i, g, :], bi[:, i, GSZ * g:GSZ * g + GSZ])
            link(last)
            link(dve.tensor_tensor(gs[:, :, 0:NGRP], g8[:, :, :, 0], g8[:, :, :, 1], ALU.add))
            for i in range(NT):
                last = dve.max(gt8[:, i, :], gs[:, i, 0:NGRP])
            link(last)
            link(dve.memset(gt8[:, :, TOPG:8], -1e30))
            for i in range(NT):
                last = dve.match_replace(gr[:, i, :], gt8[:, i, :], gs[:, i, :], -2e30)
            link(last)
            link(dve.tensor_scalar(gmask, gr[:, :, 0:NGRP], -1.5e30, None, ALU.is_lt))
            link(dve.tensor_scalar(gneg, gmask, -1.0, 1e30, ALU.add, ALU.mult))

            def by_expert(t):
                return t.rearrange("p i (g c) -> p i g c", g=NGRP)

            for i in range(NT):
                gb = gmask[:, i, :].unsqueeze(2).to_broadcast([P, NGRP, GSZ])
                last = dve.tensor_tensor(by_expert(m1)[:, i], by_expert(bi)[:, i], gb, ALU.mult)
            link(last)
            for i in range(NT):
                gb = gneg[:, i, :].unsqueeze(2).to_broadcast([P, NGRP, GSZ])
                last = dve.tensor_tensor(by_expert(m1)[:, i], by_expert(m1)[:, i], gb, ALU.add)
            link(last)
            for i in range(NT):
                last = dve.max(v8[:, i, :], m1[:, i, :])
            link(last)
            for i in range(NT):
                last = dve.match_replace(rep[:, i, :], v8[:, i, :], m1[:, i, :], -3e30)
            link(last)
            link(dve.tensor_scalar(sel, rep, -2e30, None, ALU.is_lt))
            dve.tensor_copy(selb, sel).then_inc(sel_ready, 1)
            link(dve.tensor_tensor(ws, sc, sel, ALU.mult))
            link(dve.tensor_reduce(wsum, ws, axis=AXX, op=ALU.add))
            link(dve.reciprocal(wrec, wsum))
            for i in range(NT):
                last = dve.tensor_scalar(ws[:, i, :], ws[:, i, :], wrec[:, i:i + 1], ROUTED_SCALE,
                                         ALU.mult, ALU.mult)
            link(last)
            dve.wait_ge(xg_zero, 1)

            def part(c):
                return RW5[:, :, :, c].rearrange("p e i -> p i e")

            link(dve.tensor_copy(part(2), ws))
            link(dve.tensor_tensor(wr1, ws, part(2), ALU.subtract))
            link(dve.tensor_copy(part(3), wr1))
            link(dve.tensor_tensor(part(4), wr1, part(3), ALU.subtract))

            def ple(n):
                half, i = n // NT, n % NT
                cols = slice(512 * half, 512 * half + 512)
                dve.wait_ge(ple_sig, n + 1)
                ins = dve.tensor_tensor(ple_sg[:, n % 2, :], ple_sg[:, n % 2, :], bank[2 + n % 2][:, :], ALU.mult)
                link(ins)
                dve.tensor_tensor(acc[:, i, cols], acc[:, i, cols], ple_sg[:, n % 2, :],
                                  ALU.add).then_inc(ple_used, 1)

            dve.wait_ge(residual_in, NT)
            for n in range(NT):
                ple(n)
            dve.wait_ge(pos_done, 1)
            posp = bank[7][:, 0:256].rearrange("p (i e) -> p i e", i=NT)
            link(dve.scalar_tensor_tensor(pos1, posp, 1.0, sel, ALU.add, ALU.mult))
            count = bank[7][:, 256:320]
            link(dve.tensor_copy(before[0], count))
            link(dve.tensor_scalar(minus_p, slot_row[:, 0:1], -1.0, None, ALU.mult))
            for step in range(6):
                a, b, w = before[step % 2], before[(step + 1) % 2], 1 << step
                dve.tensor_copy(b[:, 0:w], a[:, 0:w])
                link(dve.tensor_tensor(b[:, w:], a[:, w:], a[:, 0:NEXP - w], ALU.add))
            link(dve.tensor_tensor(slot_row, slot_row, before[0], ALU.add))
            link(dve.tensor_tensor(slot_row, slot_row, count, ALU.subtract))
            dve.tensor_scalar(posE.rearrange("p e i -> p i e"), pos1, -1.0, None, ALU.add)
            for i in range(NT):
                last = dve.tensor_tensor(dd[:, i, :], sel[:, i, :], slot_row, ALU.mult)
            link(last)
            link(dve.tensor_tensor(dd, dd, pos1, ALU.add))
            for i in range(NT):
                last = dve.max(d8[:, i, :], dd[:, i, :])
            link(last)
            link(dve.tensor_scalar(d8, d8, minus_p, -1.0, ALU.add, ALU.add))
            link(dve.tensor_copy(dest, d8))
            link(dve.tensor_reduce(cmax, bank[7][:, 256:320], axis=AXX, op=ALU.max))
            dve.tensor_copy(cnt, cmax).then_inc(cnt_ready, 1)
            dve.nop().then_inc(pos_used, 1)

            def hot(r, e, n):
                if not (isinstance(n, int) and n < NHOT):
                    dve.wait_ge(hot_used, n - NHOT + 1)
                for i in range(NT):
                    last = dve.tensor_scalar(onehot[:, r, i, :], iota_s, posE[:, bass.ds(e, 1), i], None,
                                             ALU.is_equal)
                last.then_inc(hot_ready, 1)

            def index_tables(b):
                dve.wait_ge(idx_done, b + 1)
                t5 = bank[7][:, 0:320].rearrange("p (e c) -> p e c", c=5)
                dve.tensor_copy(IDX, t5[:, :, 0]).then_inc(index_chain, 1)
                dve.wait_ge(index_chain, 7 * b + 1)
                dve.tensor_tensor(IDX, IDX, t5[:, :, 1], ALU.add).then_inc(index_chain, 1)
                dve.tensor_reduce(WG, t5[:, :, 2:5], axis=AXX, op=ALU.add)
                dve.wait_ge(index_chain, 7 * b + 2)
                dve.tensor_scalar(IDX, IDX, 1024.0, None, ALU.add).then_inc(index_chain, 1)
                dve.wait_ge(index_chain, 7 * b + 3)
                dve.tensor_scalar(IDY, IDX, float(T), 65536.0, ALU.is_ge, ALU.mult).then_inc(index_chain, 1)
                dve.wait_ge(index_chain, 7 * b + 4)
                dve.tensor_tensor(IDY, IDY, slot_row, ALU.add).then_inc(index_chain, 1)
                dve.wait_ge(index_chain, 7 * b + 5)
                dve.tensor_scalar(IDY, IDY, float(CAP * b), None, ALU.add).then_inc(index_chain, 1)
                dve.wait_ge(index_chain, 7 * b + 6)
                dve.tensor_scalar(posE, posE, -float(CAP), None, ALU.add).then_inc(index_chain, 1)
                dve.wait_ge(index_chain, 7 * b + 7)
                dve.nop().then_inc(idx_used, 1)

            def index_pass(b):
                with dve.Fori(0, NEXP // 4) as it:
                    for r in range(4):
                        n = turn(b, it, r)
                        hot_loop(r, 4 * it + r, n)
                index_tables(b)

            def hot_loop(r, e, n):
                dve.wait_ge(hot_used, n - 3)
                for i in range(NT):
                    last = dve.tensor_scalar(onehot[:, r, i, :], iota_s, posE[:, bass.ds(e, 1), i], None,
                                             ALU.is_equal)
                last.then_inc(hot_ready, 1)

            def hots(batch):
                for n in range(HOT0[batch], HOT0[batch + 1]):
                    hot(n % NHOT, n, n)

            def tokens_of(it, r):
                e = NR * it + r
                dve.tensor_copy(idxr[:, r:r + 1], IDX[:, bass.ds(e, 1)]).then_inc(col_ready, 1)

            dve.wait_ge(x1_stored, 16 * NT)
            for n in range(NT, 2 * NT):
                ple(n)
                hots(n - NT)
            for i in range(NT):
                dve.wait_ge(sh_sig, i + 1)
                if i >= 2:
                    dve.wait_ge(sh_ht, i - 1)
                link(dve.tensor_tensor(sg[:, i % 2, :], sg[:, i % 2, :], bank[i % 2][:, 0:F], ALU.mult))
                dve.tensor_tensor(h[:, i % 2, :], sg[:, i % 2, :], bank[i % 2][:, F:2 * F], ALU.mult).then_inc(sh_h, 1)
                if i < 2:
                    hots(NT + 2 * i)
                dve.wait_ge(sh_ht, i + 1)
                dve.tensor_copy(hT[:, i % 2], bank[4][:, 0:256].rearrange("p (k s) -> p k s", k=NF)).then_inc(sh_hto, 1)
                if i < 2:
                    hots(NT + 2 * i + 1)
                for half in range(2):
                    cols = slice(512 * half, 512 * half + 512)
                    dve.wait_ge(sh_y, i + 1)
                    last = dve.tensor_tensor(acc[:, i, cols], acc[:, i, cols], bank[2 + half][:, :], ALU.add)
                last.then_inc(sh_used, 1)
                if i == 1:
                    index_tables(0)
                    for r in range(NR):
                        tokens_of(0, r)

            def rows_of(b, it, r):
                n = turn(b, it, r)
                e = NR * it + r
                if not (isinstance(n, int) and n < NR):
                    dve.wait_ge(scattered[r], 16 * (NEXP // NR * b + it))
                dve.tensor_copy(idyr[:, r:r + 1], IDY[:, bass.ds(e, 1)])
                dve.tensor_copy(wgr[:, r:r + 1], WG[:, bass.ds(e, 1)]).then_inc(ycol_ready, 1)

            silu = sem("silu")

            def hidden_all(b, it, r):
                n = turn(b, it, r)
                dve.wait_ge(e_sig, n + 1)
                if not (isinstance(n, int) and n < 2):
                    dve.wait_ge(ht_done, n - 1)
                dve.tensor_tensor(sg[:, r % 2, :], sg[:, r % 2, :], bank[2 + r % 2][:, 0:F],
                                  ALU.mult).then_inc(silu, 1)
                dve.wait_ge(silu, n + 1)
                dve.tensor_tensor(h[:, r % 2, :], sg[:, r % 2, :], bank[2 + r % 2][:, F:2 * F],
                                  ALU.mult).then_inc(h_ready, 1)

            def hidden_evac(b, it, r):
                n = turn(b, it, r)
                dve.wait_ge(ht_done, n + 1)
                if not (isinstance(n, int) and n < 2):
                    dve.wait_ge(y_done, n - 1)
                dve.tensor_copy(hT[:, r % 2], bank[4][:, 0:256].rearrange("p (k s) -> p k s", k=NF)).then_inc(ht_out, 1)

            def expert_vectors(b):
                if b:
                    index_pass(b)
                    for r in range(NR):
                        tokens_of(0, r)

                def step(it, r, before, after=True):
                    if before is not None:
                        hidden_evac(b, *before)
                    hidden_all(b, it, r)
                    if after:
                        tokens_of(it + 1, r)
                    rows_of(b, it, r)

                for r in range(NR):
                    step(0, r, (0, r - 1) if r else None)
                last = NEXP // NR - 1
                with dve.Fori(1, last) as it:
                    for r in range(NR):
                        step(it, r, (it, r - 1) if r else (it - 1, NR - 1))
                for r in range(NR):
                    step(last, r, (last, r - 1) if r else (last - 1, NR - 1), after=False)
                hidden_evac(b, last, NR - 1)

            expert_vectors(0)
            after_first = links[0]
            dve.wait_ge(cnt_ready, 1)
            most = dve.value_load(cnt[0:1, 0:1], min_val=0, max_val=T)
            with dve.If(most > CAP):
                expert_vectors(1)
                with dve.If(most > 2 * CAP):
                    expert_vectors(2)
                    with dve.If(most > 3 * CAP):
                        expert_vectors(3)
                        dve.nop()
                    dve.nop()
                dve.nop()
            final = sem("final_chain")
            links_f = [0]

            def flink(ins):
                links_f[0] += 1
                ins.then_inc(final, 1)
                dve.wait_ge(final, links_f[0])

            for i in range(NT):
                for k in range(TOPK):
                    n = i * TOPK + k
                    dve.wait_ge(row_in[n], 16)
                    dve.tensor_tensor(acc[:, i, :], acc[:, i, :], last_rows(n), ALU.add).then_inc(row_added, 1)
                    dve.wait_ge(row_added, n + 1)
                for c in range(2):
                    last = dve.bn_stats(stats[:, c, :], acc[:, i, 512 * c:512 * c + 512])
                flink(last)
                flink(dve.bn_aggr(mv, stats))
                dve.tensor_scalar(var_e, mv[:, 1:2], EPS, None, ALU.add).then_inc(var_ready, 1)
                dve.wait_ge(root_ready, NT + i + 1)
                flink(dve.reciprocal(rstd, rstd))
                flink(dve.tensor_scalar(acc[:, i, :], acc[:, i, :], mv[:, 0:1], rstd, ALU.subtract, ALU.mult))
                flink(dve.tensor_tensor(acc[:, i, :], acc[:, i, :], lnp[:, 2, :], ALU.mult))
                dve.tensor_tensor(acc[:, i, :], acc[:, i, :], lnp[:, 3, :], ALU.add).then_inc(out_ready, 1)

        @block.tensor
        def _(pe):
            mm = pe.matmul
            pe.wait_ge(pool_const, 13)
            for n in range(2 * NT):
                i, half = n // 2, n % 2
                if half == 0:
                    pe.wait_ge(x_in[i], 16)
                if n >= 2:
                    pe.wait_ge(group_out, n - 1)
                for k in range(4):
                    last = pe.transpose(group_bank(n)[:, k * P:(k + 1) * P],
                                        x0[:, i, (4 * half + k) * P:(4 * half + k + 1) * P], ident)
                last.then_inc(group_done, 1)
            pe.wait_ge(const_in, 16 * 10)
            pe.wait_ge(group_out, NXG - 2)
            for w in range(2):
                last = pe.transpose(group_bank(NXG - 1)[:, 32 * w:32 * w + 32], pe_raw[0:32, w, :], ident[0:32, 0:32])
            last.then_inc(group_done, 1)

            def wait_chunk(n):
                pe.wait_ge(w_in[slot_of(n)], w_count(n))

            def group(n, desc):
                form, c, col, dst, _, frees = desc
                dstb = group_bank(n)
                wait_chunk(c)
                pe.wait_ge(group_out, n - 1 if n < G1 else n)
                wv = chunk(c, width_of(c))
                if form == "T":
                    for k in range(ND):
                        last = mm(dstb[:, :], wv[:, k, col:col + P], xT[:, k, :], start=(k == 0), stop=(k == ND - 1))
                else:
                    tiles, width = {"N": (range(NT), P), "G": (range(NT), 24),
                                    "N2": (range(col, col + 2) if form == "N2" else (), 256)}[form]
                    c0 = 0 if form == "N2" else col
                    for a, i in enumerate(tiles):
                        for k in range(ND):
                            last = mm(dstb[:, a * width:(a + 1) * width], xT[:, k, i * P:(i + 1) * P],
                                      wv[:, k, c0:c0 + width], start=(k == 0), stop=(k == ND - 1))
                last.then_inc(group_done, 1)
                if frees:
                    pe.wait_ge(group_done, n + 1)
                    pe.sem_inc(w_used, frees)

            pe.wait_ge(group_out, 2 * NT)
            for n, desc in enumerate(FIRST):
                group(G0 + n, desc)
            for w in range(2):
                pe.wait_ge(pe_added, w + 1)
                for c in range(NW1):
                    n = N_FIRST + NW1 * w + c
                    wait_chunk(n)
                    for a in range(ND):
                        la = c * ND + a
                        last = mm(bank[4][0:16, 256 * w:256 * w + 256], KV[:, w, la, :], chunk(n)[:, a, :],
                                  start=(la == 0), stop=(la == NW1 * ND - 1))
                    last.then_inc(w_used, 1)
            pe.wait_ge(w_used, REST0)
            pe.sem_inc(hc_done, 1)
            pe.wait_ge(hc_ready, 1)
            for f in range(4):
                last = pe.transpose(bank[5][:, 16 * f:16 * f + 16], hcu[0:16, P * f:P * f + P], ident[0:16, 0:16])
            last.then_inc(hct_done, 1)
            pe.wait_ge(hct_out, 1)
            w2k = w2[:, 0:128].rearrange("p (f d) -> p f d", f=2)
            w2v = w2[:, 128:256].rearrange("p (f d) -> p f d", f=2)
            for g in range(2):
                for f in range(2):
                    mm(bank[4][DH * g:DH * g + DH, 0:8], w2k[:, f, :], hcT[:, f, 8 * g:8 * g + 8],
                       start=(f == 0), stop=(f == 1))
            for g in range(2):
                for f in range(2):
                    last = mm(bank[4][0:8, 128 + DH * g:128 + DH * g + DH], hcT[:, 2 + f, 8 * g:8 * g + 8],
                              w2v[:, f, :], start=(f == 0), stop=(f == 1))
            last.then_inc(cmp_done, 1)
            pe.wait_ge(cmp_out, 1)

            def scores(s):
                kind, g, i = JOBS[s]
                n = keys_of(kind, i)[1]
                pe.wait_ge(group_out, need_group(kind))
                for j in range(4):
                    if s >= 1:
                        pe.wait_ge(biased, 4 * (s - 1) + j + 1)
                    q, k = unit_operands(kind, g, i, j)
                    mm(bank[j][:, 0:n], q, k, start=True, stop=True).then_inc(scored, 1)

            opened = {}

            def turn_and_value(s, between):
                kind, g, i = JOBS[s]
                lo = keys_of(kind, i)[0]
                nb = blocks_of(kind, i)
                pe.wait_ge(probs, s + 1)
                first_of_out = s == 0 or CLOSES[s - 1]

                def transposes(n, a):
                    if n >= 2:
                        pe.wait_ge(turned_out, n - 1)
                    for q in range(nb if kind == "dif" else 4):
                        if kind == "dif":
                            src = S[:, 4 * (s % 2) + 2 * a, q * P:(q + 1) * P]
                        else:
                            src = S[:, 4 * (s % 2) + q, a * P:(a + 1) * P]
                        last = pe.transpose(bank[4 + n % 2][:, q * P:(q + 1) * P], src, ident)
                    last.then_inc(turned, 1)

                def values(n, a):
                    pe.wait_ge(turned_out, n + 1)
                    if first_of_out and a == 0 and OUT0[s] >= 1:
                        pe.wait_ge(o_out, OUT0[s])
                    rows = slice(DH * g, DH * g + DH)
                    if kind == "dif":
                        hd = 2 * g + a
                        for q in range(nb):
                            last = mm(bank[6][:, P * a:P * a + P], PT[:, n % 4, q * P:(q + 1) * P],
                                      vd[:, q, P * hd:P * hd + P], start=(q == 0), stop=(q == nb - 1))
                    else:
                        v = {"slc": lambda: vs[:, a, rows], "win": lambda: vw[:, a, rows],
                             "swa": lambda: vb[:, lo + a, rows], "cmp": lambda: vcmp[:, rows]}[kind]()
                        last = mm(bank[6][rows, :], v, PT[:, n % 4, :], start=first_of_out and a == 0,
                                  stop=CLOSES[s] and a == turns - 1)
                    last.then_inc(pv_done, 1)

                turns = turns_of(kind, i)
                t0 = TURN0[s]
                ahead = min(2, turns)
                for a in range(ahead):
                    transposes(t0 + a, a)
                between()
                for a in range(turns):
                    values(t0 + a, a)
                    if a + ahead < turns:
                        transposes(t0 + a + ahead, a + ahead)
                if CLOSES[s]:
                    pe.wait_ge(pv_done, TURN0[s + 1])
                    pe.sem_inc(o_done, 1)

            for s in range(NJ + 1):
                def project():
                    if s < NJ:
                        for n in range(REST_AT[s], REST_AT[s + 1]):
                            group(G1 + n, REST[n])

                if s < NJ:
                    scores(s)
                if s >= 1:
                    turn_and_value(s - 1, project)
                else:
                    project()

            pe.wait_ge(o_out, OUT0[NJ])
            for n in range(24):
                b, m = n // 8, n % 8
                if m == 0:
                    pe.wait_ge(big_in[b % 2], big_count(B_BR + b))
                if n == 16:
                    pe.wait_ge(od_ready, 1)
                    for hd in range(4):
                        if hd >= 2:
                            pe.wait_ge(oct_out, hd - 1)
                        for i in range(NT):
                            last = pe.transpose(bank[4 + hd % 2][:, i * P:(i + 1) * P],
                                                odn[:, i, P * hd:P * hd + P], ident)
                        last.then_inc(oct_done, 1)
                    pe.wait_ge(oct_out, 4)
                if n >= 4:
                    pe.wait_ge(branch_used, n - 3)
                src = (oa, ob, oc)[b]
                for j in range(4):
                    last = mm(bank[n % 4][:, :], wb[b][:, j, m * P:(m + 1) * P], src[:, j, :],
                              start=(j == 0), stop=(j == 3))
                last.then_inc(branch_done, 1)
                if m == 7:
                    pe.wait_ge(branch_done, n + 1)
                    pe.sem_inc(big_used, 1)

            pe.wait_ge(merged_ready, 1)

            def att_out(i):
                for half in range(2):
                    if i == 0:
                        pe.wait_ge(big_in[(B_WO + half) % 2], big_count(B_WO + half))
                    if i >= 2:
                        pe.wait_ge(att_used, 2 * (i - 2) + half + 1)
                    for m in range(ND):
                        last = mm(bank[2 * (i % 2) + half][:, :], merged[:, m, i * P:(i + 1) * P],
                                  wo_h[half][:, m, :], start=(m == 0), stop=(m == ND - 1))
                    last.then_inc(att_done, 1)

            def x1_turn(i):
                pe.wait_ge(x1_ready, i + 1)
                for half in range(2):
                    if i >= 1:
                        pe.wait_ge(x1t_out, 2 * (i - 1) + half + 1)
                    for k in range(4):
                        last = pe.transpose(bank[4 + half][:, k * P:(k + 1) * P],
                                            x1[:, i, (4 * half + k) * P:(4 * half + k + 1) * P], ident)
                    last.then_inc(x1t_done, 1)

            for i in range(NT):
                att_out(i)
                if i >= 1:
                    x1_turn(i - 1)
            pe.wait_ge(att_done, 2 * NT)
            pe.sem_inc(big_used, 2)
            x1_turn(NT - 1)
            pe.wait_ge(late_in, 16 * 7)
            for k in range(2):
                pe.wait_ge(x1t_out, 2 * (NT - 1) + k + 1)
                for i in range(NT):
                    last = pe.transpose(bank[4 + k][:, i * P:(i + 1) * P], pn[:, i, k * P:(k + 1) * P], ident)
                last.then_inc(pt_done, 1)
            for i in range(NT):
                for k in range(ND):
                    last = mm(bank[6][:, NEXP * i:NEXP * i + NEXP], x1T[:, k, i * P:(i + 1) * P], rw[:, k, :],
                              start=(k == 0), stop=(k == ND - 1))
            last.then_inc(route_done, 1)
            def places():
                pe.wait_ge(sel_ready, 1)
                for i in range(NT):
                    for a in range(i):
                        mm(bank[7][:, NEXP * i:NEXP * i + NEXP], ones, selb[:, a, :], start=(a == 0), stop=False)
                    mm(bank[7][:, NEXP * i:NEXP * i + NEXP], tri, selb[:, i, :], start=(i == 0), stop=True)
                for i in range(NT):
                    last = mm(bank[7][:, 256:320], ones, selb[:, i, :], start=(i == 0), stop=(i == NT - 1))
                last.then_inc(pos_done, 1)

            def index_of(r, e, n):
                pe.wait_ge(hot_ready, n + 1)
                for i in range(NT):
                    last = mm(bank[7][:, bass.ds(5 * e, 5)], onehot[:, r, i, :],
                              RW5[:, bass.ds(e, 1), i, :].rearrange("p e c -> p (e c)"),
                              start=(i == 0), stop=(i == NT - 1))
                last.then_inc(hot_used, 1)

            def indices(batch):
                if batch == 0:
                    pe.wait_ge(pos_used, 1)
                for n in range(HOT0[batch], HOT0[batch + 1]):
                    index_of(n % NHOT, n, n)

            pe.wait_ge(pt_out, 2)
            pe.wait_ge(ppw_in, 16)
            for n in range(2 * NT):
                half, i = n // NT, n % NT
                if n == NT:
                    places()
                if i == 0:
                    pe.wait_ge(big_in[(B_PG + half) % 2], big_count(B_PG + half))
                if n >= 2:
                    pe.wait_ge(ple_used, n - 1)
                else:
                    pe.wait_ge(att_used, 2 * NT)
                for k in range(ND):
                    mm(bank[n % 2][:, :], x1T[:, k, i * P:(i + 1) * P], pg_h[half][:, k, :],
                       start=(k == 0), stop=(k == ND - 1))
                for k in range(2):
                    last = mm(bank[2 + n % 2][:, :], pT[:, k, i * P:(i + 1) * P],
                              ppw[:, k, 512 * half:512 * half + 512], start=(k == 0), stop=(k == 1))
                last.then_inc(ple_done, 1)
                if n > NT:
                    indices(n - NT - 1)
                if i == NT - 1:
                    pe.wait_ge(ple_done, n + 1)
                    pe.sem_inc(big_used, 1)
            pe.wait_ge(ple_used, 2 * NT)

            def shared_up(i):
                if i == 0:
                    pe.wait_ge(big_in[B_SG % 2], big_count(B_SG))
                if i >= 2:
                    pe.wait_ge(sh_h, i - 1)
                for k in range(ND):
                    last = mm(bank[i % 2][:, :].rearrange("p (w f) -> p w f", w=2), x1T[:, k, i * P:(i + 1) * P],
                              sgu[:, :, k, :], start=(k == 0), stop=(k == ND - 1))
                last.then_inc(sh_gu, 1)

            shared_up(0)
            indices(NT - 1)
            for i in range(NT):
                if i + 1 < NT:
                    shared_up(i + 1)
                pe.wait_ge(sh_h, i + 1)
                if i >= 1:
                    pe.wait_ge(sh_hto, i)
                for k in range(NF):
                    last = pe.transpose(bank[4][:, k * P:(k + 1) * P], h[:, i % 2, k * P:(k + 1) * P], ident)
                last.then_inc(sh_ht, 1)
                pe.wait_ge(sh_hto, i + 1)
                if i == 0:
                    pe.wait_ge(big_in[B_SD % 2], big_count(B_SD))
                else:
                    pe.wait_ge(sh_used, i)
                for half in range(2):
                    for k in range(NF):
                        last = mm(bank[2 + half][:, :], hT[:, i % 2, k, :], sdn[:, k, 512 * half:512 * half + 512],
                                  start=(k == 0), stop=(k == NF - 1))
                last.then_inc(sh_y, 1)
                if i < 2:
                    indices(NT + 2 * i)
                    indices(NT + 2 * i + 1)
                if i == 1:
                    pe.wait_ge(hot_used, NEXP)
                    pe.sem_inc(idx_done, 1)
            pe.wait_ge(sh_used, NT)

            def index_pass(b):
                pe.wait_ge(idx_used, b)
                with pe.Fori(0, NEXP // 4) as it:
                    for r in range(4):
                        index_of(r, 4 * it + r, turn(b, it, r))
                pe.wait_ge(hot_used, NEXP * (b + 1))
                pe.sem_inc(idx_done, 1)

            def rows_turn(b, it, r):
                n = turn(b, it, r)
                pe.wait_ge(gathered[r], 16 * (NEXP // NR * b + it + 1))
                for half in range(2):
                    if not (isinstance(n, int) and n < 1):
                        pe.wait_ge(xgt_out, 2 * n - 1 + half)
                    for k in range(4):
                        kk = 4 * half + k
                        last = pe.transpose(bank[half][:, k * P:(k + 1) * P], xg[:, r, kk:D:ND], ident)
                    last.then_inc(xgt_done, 1)

            def up(b, it, r, ks_):
                n = turn(b, it, r)
                gu, _ = eslot(r)
                if ks_[0] == 0:
                    pe.wait_ge(xgt_out, 2 * n + 2)
                    pe.wait_ge(wgu_in[r], 32 * (NEXP // NR * b + it + 1))
                    if not (isinstance(n, int) and n < 2):
                        pe.wait_ge(h_ready, n - 1)
                for k in ks_:
                    last = mm(bank[2 + r % 2][:, :].rearrange("p (w f) -> p w f", w=2), xgT[:, r % 2, k, :],
                              gu[:, :, k, :], start=(k == 0), stop=(k == ND - 1))
                if ks_[-1] == ND - 1:
                    last.then_inc(gu_done, 1)

            def hidden_turn(b, it, r):
                n = turn(b, it, r)
                pe.wait_ge(h_ready, n + 1)
                if not (isinstance(n, int) and n < 1):
                    pe.wait_ge(ht_out, n)
                for k in range(NF):
                    last = pe.transpose(bank[4][:, k * P:(k + 1) * P], h[:, r % 2, k:F:NF], ident)
                last.then_inc(ht_done, 1)

            def down(b, it, r):
                n = turn(b, it, r)
                _, dn = eslot(r)
                pe.wait_ge(ht_out, n + 1)
                pe.wait_ge(wd_in[r], 16 * (NEXP // NR * b + it + 1))
                if not (isinstance(n, int) and n < 1):
                    pe.wait_ge(y_out, 2 * n)
                for half in range(2):
                    for k in range(NF):
                        last = mm(bank[5 + half][:, :], hT[:, r % 2, k, :], dn[:, k, 512 * half:512 * half + 512],
                                  start=(k == 0), stop=(k == NF - 1))
                last.then_inc(y_done, 1)

            def expert_products(b):
                if b:
                    index_pass(b)
                rows_turn(b, 0, 0)

                def step(it, r, before, after=True):
                    up(b, it, r, range(0, 4))
                    if before is not None:
                        hidden_turn(b, *before)
                    up(b, it, r, range(4, ND))
                    if after:
                        rows_turn(b, it + (r + 1) // NR, (r + 1) % NR)
                    if before is not None:
                        down(b, *before)

                for r in range(NR):
                    step(0, r, (0, r - 1) if r else None)
                last = NEXP // NR - 1
                with pe.Fori(1, last) as it:
                    for r in range(NR):
                        step(it, r, (it, r - 1) if r else (it - 1, NR - 1))
                for r in range(NR):
                    step(last, r, (last, r - 1) if r else (last - 1, NR - 1), after=r < NR - 1)
                hidden_turn(b, last, NR - 1)
                down(b, last, NR - 1)

            expert_products(0)
            pe.wait_ge(cnt_ready, 1)
            most = pe.value_load(cnt[0:1, 0:1], min_val=0, max_val=T)
            with pe.If(most > CAP):
                expert_products(1)
                with pe.If(most > 2 * CAP):
                    expert_products(2)
                    with pe.If(most > 3 * CAP):
                        expert_products(3)
                        pe.nop()
                    pe.nop()
                pe.nop()


_INS = ["x", "p", "w_in", "nsa_pe_k", "nsa_w1_k", "nsa_w2_k", "nsa_pe_v", "nsa_w1_v", "nsa_w2_v", "swa_sinks",
        "diff_lq1", "diff_lk1", "diff_lq2", "diff_lk2", "diff_norm_g", "w_branch_a", "w_branch_b", "w_branch_c",
        "w_out", "ln1_g", "ln1_b", "router_w", "router_bias", "exp_w_gate", "exp_w_up", "exp_w_down",
        "sh_w_gate", "sh_w_up", "sh_w_down", "ple_w_proj", "ple_w_gate", "ln2_g", "ln2_b"]


def kernel(**inputs):
    import numpy as _np
    import concourse.bacc as _bacc
    from concourse import mybir as _mybir
    from concourse.bass_utils import run_bass_kernel_spmd as _run

    nc = _bacc.Bacc("TRN2", target_bir_lowering=False, num_devices=1)
    arrays, aps = {}, {}
    for name in _INS:
        a = _np.ascontiguousarray(inputs[name])
        arrays[f"in_{name}_dram"] = a
        aps[name] = nc.dram_tensor(f"in_{name}_dram", a.shape, _mybir.dt.from_np(a.dtype), kind="ExternalInput").ap()
    out = nc.dram_tensor("out_0_dram", (1, T, D), F32, kind="ExternalOutput").ap()
    build(nc, aps, out)
    r = _run(nc, [arrays], core_ids=[0])
    return r.results[0]["out_0_dram"]
```

```python
import math

import numpy as np

import concourse.bass as bass
from concourse import mybir
from contextlib import ExitStack

F32 = mybir.dt.float32
F32R = mybir.dt.float32r
BF16 = mybir.dt.bfloat16
I32 = mybir.dt.int32
U32 = mybir.dt.uint32
ALU = mybir.AluOpType
ACT = mybir.ActivationFunctionType
AXX = mybir.AxisListType.X

P = 128
T, D = 512, 1024
NT, ND = T // P, D // P
DH = 64
SCALE = DH ** -0.5
NEXP, TOPK, NGRP, TOPG = 64, 8, 8, 4
GSZ = NEXP // NGRP
F = 256
NF = F // P
ROUTED_SCALE = 2.5
ALPHA = 2 ** 0.25
EPS = 1e-5
LAMBDA_INIT = 0.8 - 0.6 * math.exp(0.0)
NBLK = T // 64
HUGE = 3e32
CAP = 128
NPASS = T // CAP
YROWS = TOPK * T

C_QA, C_KC, C_VC, C_KS, C_VS, C_KW, C_VW, C_GA = 0, 512, 640, 768, 896, 1024, 1152, 1280
C_QB, C_KB, C_VB, C_QC, C_KD, C_VD, C_GM = 1304, 1816, 1944, 2072, 2584, 3096, 3608
IN_CHUNKS_FIRST = [[(C_QA, C_QA + 256)], [(C_QA + 256, C_KC)], [(C_KC, C_KS)],
                   [(C_KS, C_VS), (C_KW, C_VW)], [(C_VS, C_KW), (C_VW, C_QB)]]
IN_CHUNKS_REST = [[(c, c + 256)] for c in range(C_QB, 6680, 256)]
NGATE0 = 9
IN_CHUNKS_REST = IN_CHUNKS_REST[:NGATE0] + IN_CHUNKS_REST[NGATE0 + 4:] + IN_CHUNKS_REST[NGATE0:NGATE0 + 4]
NW1 = 4
IN_CHUNKS = IN_CHUNKS_FIRST + IN_CHUNKS_REST
REST0 = len(IN_CHUNKS_FIRST)
NSLOT, SLOT = 3, 2240
BIG = 2 * SLOT

JOBS = [(kind, g, i) for i in range(NT) for g in range(2) for kind in ("slc", "win", "cmp")]
JOBS += [("swa", g, i) for i in range(NT) for g in range(2)]
JOBS += [("dif", g, i) for i in range(NT) for g in range(2)]
NJ = len(JOBS)


def keys_of(kind, i):
    if kind == "cmp":
        return 0, NBLK
    lo = max(0, i - 1) if kind == "swa" else 0
    return lo, (i + 1 - lo) * P


def blocks_of(kind, i):
    return 1 if kind == "cmp" else keys_of(kind, i)[1] // P


def turns_of(kind, i):
    return 2 if kind == "dif" else blocks_of(kind, i)


TURN0 = np.cumsum([0] + [turns_of(k, i) for k, g, i in JOBS]).tolist()
CLOSES = [k != "slc" and k != "win" for k, g, i in JOBS]
OUT0 = np.cumsum([0] + [int(c) for c in CLOSES]).tolist()


def build(nc, A, out):
    ctx = ExitStack()
    with ctx:
        def sem(name):
            return ctx.enter_context(nc.semaphore(name))

        ARENA = 52000
        small = ctx.enter_context(nc.sbuf_tensor("small", [P, 1024], F32))
        small2 = ctx.enter_context(nc.sbuf_tensor("small2", [P, 128], F32))
        places = {}

        def place(off, n, dtype):
            assert off + n <= ARENA
            key = (off, n, dtype == F32R)
            if key not in places:
                name = f"{'halves' if dtype == F32R else 'floats'}_{off}_{n}"
                if off == 0:
                    with nc.sbuf_tensor(name, [P, n], dtype) as places[key]:
                        pass
                else:
                    with nc.sbuf_tensor(f"before_{name}", [P, off], F32):
                        with nc.sbuf_tensor(name, [P, n], dtype) as places[key]:
                            pass
            return places[key][:, :]

        def at(off, n):
            return place(off, n, F32)

        def half_at(off, n):
            return place(off, n, F32R)

        W = at(0, 4 * SLOT)
        upper_at = [NSLOT * SLOT, 37888]
        qa = at(8960, 2048).rearrange("p (j t) -> p j t", t=T)
        qb = at(11008, 2048).rearrange("p (j t) -> p j t", t=T)
        qc = at(13056, 2048).rearrange("p (j t) -> p j t", t=T)
        kd = at(15104, 2048).rearrange("p (j t) -> p j t", t=T)
        vd = at(17152, 2048).rearrange("p (i c) -> p i c", i=NT)
        ks, kw = at(19200, 512), at(19712, 512)
        vs = at(20224, 512).rearrange("p (i c) -> p i c", i=NT)
        vw = at(20736, 512).rearrange("p (i c) -> p i c", i=NT)
        kb = at(21248, 512)
        vb = at(21760, 512).rearrange("p (i c) -> p i c", i=NT)
        KV = at(22272, 1024).rearrange("p (w l c) -> p w l c", w=2, c=16)
        hcx, hcu, hct = at(23296, 512), at(23808, 512), at(24320, 256)
        xh = half_at(24576, 4096).rearrange("p (k t) -> p k t", t=T)
        xl = half_at(28672, 4096).rearrange("p (k t) -> p k t", t=T)
        gates_kept = at(32768, 4096).rearrange("p (m t) -> p m t", t=T)
        gates_ring = at(36864, 1024).rearrange("p (r t) -> p r t", t=T)
        gates_back = at(24576, 8192).rearrange("p (m t) -> p m t", t=T)
        S = at(40960, 4096).rearrange("p (u n) -> p u n", n=T)
        PT = at(45056, 2048).rearrange("p (u n) -> p u n", n=T)
        oa = at(47104, 2048).rearrange("p (j t) -> p j t", t=T)
        ob = at(49152, 2048).rearrange("p (j t) -> p j t", t=T)
        dist = at(51200, T)
        distw = at(51712, 2 * P)
        distc = at(51968, NT * NBLK).rearrange("p (i n) -> p i n", i=NT)
        x0 = at(32768, 4096).rearrange("p (i d) -> p i d", i=NT)
        odn = at(19200, 2048).rearrange("p (i c) -> p i c", i=NT)
        oc = at(8960, 2048).rearrange("p (j t) -> p j t", t=T)
        merged = at(11008, 4096).rearrange("p (m t) -> p m t", t=T)
        xr = at(15104, 4096).rearrange("p (i d) -> p i d", i=NT)
        x1 = at(28672, 4096).rearrange("p (i d) -> p i d", i=NT)
        acc = at(32768, 4096).rearrange("p (i d) -> p i d", i=NT)
        lnp = at(36864, 4096).rearrange("p (w d) -> p w d", w=4)
        x1T = at(24576, 4096).rearrange("p (k t) -> p k t", t=T)
        z = at(40960, 2048).rearrange("p (r d) -> p r d", r=2)
        mtmp = at(43008, 1024).rearrange("p (r t) -> p r t", r=2)
        ppw = at(45056, 2048).rearrange("p (k d) -> p k d", k=2)
        pn = at(47104, 1024).rearrange("p (i c) -> p i c", i=NT)
        pT = at(49152, 1024).rearrange("p (k t) -> p k t", k=2)
        rw = at(22272, 512).rearrange("p (k e) -> p k e", k=ND)
        NR, ESLOT = 4, 3 * ND * F

        def eslot(n):
            o = ((n + 2) % NR) * ESLOT
            return (at(o, 2 * ND * F).rearrange("p (w k f) -> p w k f", w=2, k=ND),
                    at(o + 2 * ND * F, NF * D).rearrange("p (k d) -> p k d", k=NF))

        xg = at(40960, 4096).rearrange("p (r d) -> p r d", r=NR)
        xgT = at(49152, 2048).rearrange("p (r k s) -> p r k s", r=2, k=ND)
        y = at(24576, 4096).rearrange("p (r d) -> p r d", r=NR)
        sg = at(48128, 512).rearrange("p (r f) -> p r f", r=2)
        h = at(48640, 512).rearrange("p (r f) -> p r f", r=2)
        NHOT = 16
        HOT0 = [0, 10, 20, 30, 40, 46, 52, 58, NEXP]
        onehot = at(28672, 4096).bitcast(BF16).rearrange("p (r i s) -> p r i s", r=NHOT, i=NT)
        ple_sg = at(43008, 1024).rearrange("p (r t) -> p r t", r=2)
        RW5 = at(47104, 640).bitcast(BF16).rearrange("p (e i c) -> p e i c", e=NEXP, c=5)
        posE = at(47744, 256).rearrange("p (e i) -> p e i", i=NT)
        hT = at(51200, 512).rearrange("p (r k s) -> p r k s", r=2, k=NF)
        dest = at(51712, 32).bitcast(U32).rearrange("p (i k) -> p i k", i=NT)
        def last_rows(n):
            return at(n * D, D) if n < NT * TOPK - 4 else at(40960 + (n - NT * TOPK + 4) * D, D)


        def rt(n, w=256):
            return at(8960 + 256 * n, w)

        sc, bi, m1, rep, sel, ws = [rt(n).rearrange("p (i e) -> p i e", i=NT) for n in range(6)]
        g8 = rt(6).rearrange("p (i g c) -> p i g c", i=NT, g=NGRP)
        selb = at(8960 + 1792, 128).bitcast(BF16).rearrange("p (i e) -> p i e", i=NT)
        gs = at(10880, 48).rearrange("p (i g) -> p i g", i=NT)
        gr = at(10928, 48).rearrange("p (i g) -> p i g", i=NT)
        gt8 = at(10976, 32).rearrange("p (i g) -> p i g", i=NT)
        gmask = at(11008, 32).rearrange("p (i g) -> p i g", i=NT)
        gneg = at(11040, 32).rearrange("p (i g) -> p i g", i=NT)
        v8 = at(11072, 32).rearrange("p (i g) -> p i g", i=NT)
        dd = at(11136, 256).rearrange("p (i e) -> p i e", i=NT)
        d8 = at(11392, 32).rearrange("p (i g) -> p i g", i=NT)
        wr1 = at(11424, 256).rearrange("p (i e) -> p i e", i=NT)
        wsum = at(11680, 4)
        wrec = at(11684, 4)
        cmax = at(11688, 1)
        before = [at(11968, 64), at(12032, 64)]
        minus_p = at(12096, 1)
        pos1 = at(11712, 256).rearrange("p (i e) -> p i e", i=NT)

        def sm(o, n):
            return small[:, o:o + n]

        ident = sm(0, 128)
        iota_s = sm(128, 64).bitcast(BF16)
        tri = sm(192, 64).bitcast(BF16)
        ones = sm(256, 64).bitcast(BF16)
        slot_row = sm(320, 64)
        negm = sm(384, 8).rearrange("p (r j) -> p r j", r=2)
        esum = sm(392, 8).rearrange("p (r j) -> p r j", r=2)
        fac = sm(400, 8).rearrange("p (r j) -> p r j", r=2)
        sinks = sm(408, 8)
        lamv = sm(416, 4)
        ga = sm(420, 96).rearrange("p (i c) -> p i c", i=NT)
        kcmp = sm(516, 8)
        pe2 = sm(524, 64).rearrange("p (w l) -> p w l", w=2)
        gcol = sm(588, 1)
        ssq, rms = sm(592, 16), sm(608, 16)
        stats = sm(624, 12).rearrange("p (c s) -> p c s", c=2)
        mv, var_e, rstd = sm(636, 2), sm(638, 1), sm(639, 1)
        vcmp = sm(640, 128)
        hcT = sm(768, 64).rearrange("p (f c) -> p f c", f=4)
        IDX = sm(832, 64)
        WG = sm(896, 64)
        cnt = sm(960, 1).bitcast(I32)
        lamt = sm(961, 4)
        idxr = sm(965, 4).bitcast(U32)
        idyr = sm(969, 4).bitcast(U32)
        wgr = sm(973, 4)
        rbias = small2[:, 64:128]
        IDY = small2[:, 0:64]
        w2 = hct
        pe_raw = at(45056, 256).rearrange("p (w l) -> p w l", w=2)
        lq = at(45312, 256).rearrange("p (w d) -> p w d", w=4)

        bank = [ctx.enter_context(nc.psum_tensor(f"bank{n}", [P, 512], F32)) for n in range(8)]
        x1_dram = nc.dram_tensor("x1_rows", (T, D), F32, kind="Internal").ap()
        gates_dram = nc.dram_tensor("gate_rows", (2 * D, T), F32, kind="Internal").ap()
        y_dram = nc.dram_tensor("y_rows", (YROWS, D), F32, kind="Internal").ap()

        x_in = [sem(f"x_in{i}") for i in range(NT)]
        const_in = sem("const_in")
        w_in = [sem(f"w_in{s}") for s in range(NSLOT)]
        w1_in = [sem(f"w1_in{w}") for w in range(2)]
        x_low, upper_ready, lower_ready = sem("x_low"), sem("upper_ready"), sem("lower_ready")
        spilled = [sem(f"spilled{s}") for s in range(2)]
        gates_in = [sem(f"gates_in{s}") for s in range(4)]
        pool_const = sem("pool_const")
        group_done = sem("group_done")
        group_out = sem("group_out")
        embed_done, embed_out, pe_added = sem("embed_done"), sem("embed_out"), sem("pe_added")
        chain = sem("vector_chain")
        hc_done, hc_copied, hc_cubic, hc_tanh, hc_ready = (sem(n) for n in (
            "hc_done", "hc_copied", "hc_cubic", "hc_tanh", "hc_ready"))
        hct_done, hct_out, cmp_done, cmp_out = (sem(n) for n in (
            "hct_done", "hct_out", "cmp_done", "cmp_out"))
        ga_ready, lam_dot, lam_exp, lam_ready = (sem(n) for n in (
            "ga_ready", "lam_dot", "lam_exp", "lam_ready"))
        scored, biased, max_ready, exped, probs = (sem(n) for n in (
            "scored", "biased", "max_ready", "exped", "probs"))
        turned, turned_out, pv_done, o_out = (sem(n) for n in (
            "turned", "turned_out", "pv_done", "o_out"))
        sq_done, rms_in, rms_root, od_ready, oct_done, oct_out = (sem(n) for n in (
            "sq_done", "rms_in", "rms_root", "od_ready", "oct_done", "oct_out"))
        big_in = [sem(f"big_in{s}") for s in range(2)]
        sig_done, branch_done, branch_used, merged_ready = (sem(n) for n in (
            "sig_done", "branch_done", "branch_used", "merged_ready"))
        xr_in, late_in, ppw_in = sem("xr_in"), sem("late_in"), sem("ppw_in")
        att_done, att_used, var_ready, root_ready, x1_ready = (sem(n) for n in (
            "att_done", "att_used", "var_ready", "root_ready", "x1_ready"))
        residual_in = sem("residual_in")
        x1t_done, x1t_out, x1_stored = sem("x1t_done"), sem("x1t_out"), sem("x1_stored")
        pt_done, pt_out = sem("pt_done"), sem("pt_out")
        route_done, route_sig, sel_ready, pos_done, pos_used = (sem(n) for n in (
            "route_done", "route_sig", "sel_ready", "pos_done", "pos_used"))
        ple_done, ple_sig, ple_used = sem("ple_done"), sem("ple_sig"), sem("ple_used")
        sh_gu, sh_sig, sh_h, sh_ht, sh_hto, sh_y, sh_used = (sem(n) for n in (
            "sh_gu", "sh_sig", "sh_h", "sh_ht", "sh_hto", "sh_y", "sh_used"))
        index_chain = sem("index_chain")
        cnt_ready, hot_ready, hot_used, idx_done, idx_used = (sem(n) for n in (
            "cnt_ready", "hot_ready", "hot_used", "idx_done", "idx_used"))
        xg_zero = sem("xg_zero")
        pool_turn = sem("pool_turn")
        wgu_in = [sem(f"wgu_in{s}") for s in range(NR)]
        wd_in = [sem(f"wd_in{s}") for s in range(NR)]
        col_ready = sem("col_ready")
        ycol_ready = sem("ycol_ready")
        gathered = [sem(f"gathered{s}") for s in range(NR)]
        scattered = [sem(f"scattered{s}") for s in range(NR)]
        xgt_done, xgt_out, gu_done, e_sig, h_ready, ht_done, ht_out, y_done, y_out = (
            sem(n) for n in ("xgt_done", "xgt_out", "gu_done", "e_sig", "h_ready", "ht_done",
                             "ht_out", "y_done", "y_out"))
        NROW = 12
        row_in = [sem(f"row_in{s}") for s in range(NROW)]
        row_added, out_ready, stored = sem("row_added"), sem("out_ready"), sem("stored")
        experts_done = sem("experts_done")

        w_rows = A["w_in"][0].rearrange("(k p) c -> p k c", p=P)
        w1k = A["nsa_w1_k"][0].rearrange("(a p) f -> p a f", p=P)
        w1v = A["nsa_w1_v"][0].rearrange("(a p) f -> p a f", p=P)

        def slot_of(n):
            return n % NSLOT

        def chunk(n, width=256):
            o = slot_of(n) * SLOT
            return W[:, o:o + ND * width].rearrange("p (k c) -> p k c", k=ND)

        def upper(n, width=256):
            o = upper_at[n % 2]
            return half_at(o, ND * width).rearrange("p (k c) -> p k c", k=ND)

        def lower(n, width=256):
            return half_at(slot_of(n) * SLOT, ND * width).rearrange("p (k c) -> p k c", k=ND)

        def w_count(n):
            return 16 * sum(len(IN_CHUNKS[m]) for m in range(n % NSLOT, n + 1, NSLOT))

        w1_at = [11008, 13056, 15104, 17152, 40960, 43008, 47104, 49152]

        def w1_chunk(w, c):
            return at(w1_at[NW1 * w + c], 2048).rearrange("p (a f) -> p a f", a=ND)

        def query_groups(n, dst):
            return [("Q", n + j // 2, (j % 2) * P, (dst, j), SCALE, j % 2) for j in range(4)]

        FIRST = query_groups(0, qa)
        FIRST += [("T", 2, 0, "kc", 1.0, 0), ("T", 2, P, "vc", 1.0, 1)]
        COMPRESS = len(FIRST)
        FIRST += [("T", 3, 0, ks, 1.0, 0), ("T", 3, P, kw, 1.0, 1)]
        FIRST += [("V", 4, i, None, 1.0, i == NT - 1) for i in range(NT)]
        REST = query_groups(REST0, qb)
        REST += [("T", REST0 + 2, 0, kb, 1.0, 0), ("N", REST0 + 2, P, vb, 1.0, 1)]
        for base, dst, scale in ((3, qc, SCALE), (5, kd, 1.0)):
            REST += [("T", REST0 + base + j // 2, (j % 2) * P, dst[:, j, :], scale, j % 2)
                     for j in range(4)]
        for c in range(2):
            REST += [("N2", REST0 + 7 + c, 2 * i, vd[:, 2 * i:2 * i + 2, 256 * c:256 * c + 256], 1.0, i)
                     for i in range(2)]
        GATES = len(REST)
        SPILL = 2 * ND
        REST += [("T", REST0 + NGATE0 + q // 2, (q % 2) * P,
                  gates_ring[:, q % 2, :] if q < SPILL else gates_kept[:, q - SPILL, :], 1.0, q % 2)
                 for q in range(3 * ND)]
        NCHUNK = len(IN_CHUNKS)

        def gates(n):
            return gates_kept[:, n, :] if n < ND else gates_back[:, n - ND, :]

        NXG = 2 * NT
        G0, G1 = NXG, NXG + len(FIRST)
        FREED = {desc[1]: G0 + n + 1 for n, desc in enumerate(FIRST + REST)}
        N_STEPS = NJ
        PER_STEP = [2 if s in (4, 12) else 1 for s in range(N_STEPS)]
        assert sum(PER_STEP) == len(REST)
        REST_AT = np.cumsum([0] + PER_STEP).tolist()

        def group_bank(n):
            return bank[n % 4] if n < G0 else bank[6 + n % 2] if n < G1 else bank[7]

        def need_group(kind):
            return {"slc": G1, "win": G1, "cmp": G1, "swa": G1 + 6, "dif": G1 + 18}[kind]

        def width_of(n):
            return sum(b - a for a, b in IN_CHUNKS[n])

        def unit_operands(kind, g, i, j):
            lo, n = keys_of(kind, i)
            tq = slice(i * P, (i + 1) * P)
            if kind == "dif":
                r, hd = j % 2, 2 * g + j // 2
                rows = slice(DH * r, DH * r + DH)
                return qc[rows, hd, tq], kd[rows, hd, 0:n]
            rows = slice(DH * g, DH * g + DH)
            q = (qb if kind == "swa" else qa)[rows, j, tq]
            k = {"slc": ks, "win": kw, "swa": kb, "cmp": kcmp}[kind]
            return q, k[rows, lo * P:lo * P + n]

        def slope_of(kind, g, j):
            return 2.0 ** (-2.0 * (2 * g + j // 2 + 1)) if kind == "dif" else 2.0 ** -(4 * g + j + 1)

        def distances(kind, i, n):
            if kind == "cmp":
                return distc[:, i, :]
            if kind == "swa":
                return distw[:, 2 * P - n:2 * P]
            return dist[:, T - n:T]

        gu_w, down_w = {}, {}
        big0 = W[:, 0:4096]
        big1 = W[:, BIG:BIG + 4096]
        bigs = [big0, big1]
        wb = [bigs[b % 2].rearrange("p (j d) -> p j d", j=4) for b in range(3)]
        wo_h = [bigs[1].rearrange("p (k d) -> p k d", k=ND), bigs[0].rearrange("p (k d) -> p k d", k=ND)]
        pg_h = [bigs[1].rearrange("p (k d) -> p k d", k=ND), bigs[0].rearrange("p (k d) -> p k d", k=ND)]
        sgu = bigs[1].rearrange("p (w k f) -> p w k f", w=2, k=ND)
        sdn = bigs[0][:, 0:2048].rearrange("p (k d) -> p k d", k=NF)
        B_BR, B_WO, B_PG, B_SG, B_SD = 0, 3, 5, 7, 8
        BIG_DMAS = [2, 2, 1, 1, 1, 1, 1, 2, 1]

        def big_count(n):
            return 16 * sum(BIG_DMAS[m] for m in range(n % 2, n + 1, 2))

        def turn(b, it, r):
            return NEXP * b + NR * it + r

        block = ctx.enter_context(nc.Block())

        @block.sync
        def _(sp):
            def load_chunk(n):
                if n >= NSLOT:
                    sp.wait_ge(group_done, FREED[n - NSLOT])
                c0 = 0
                for a, b in IN_CHUNKS[n]:
                    sp.dma_start(chunk(n, width_of(n))[:, :, c0:c0 + b - a],
                                 w_rows[:, :, a:b]).then_inc(w_in[slot_of(n)], 16)
                    c0 += b - a

            load_chunk(0)
            for i in range(NT):
                sp.dma_start(x0[:, i, :], A["x"][0, i * P:(i + 1) * P, :]).then_inc(x_in[i], 16)
            for n in range(1, NSLOT):
                load_chunk(n)
            for w, src in enumerate((w1k, w1v)):
                for c in range(NW1):
                    sp.dma_start(w1_chunk(w, c), src[:, ND * c:ND * c + ND, :]).then_inc(w1_in[w], 16)
                load_chunk(NSLOT + w)
            for n in range(NSLOT + 2, NCHUNK):
                load_chunk(n)

            BIG_FREED = [(branch_done, 8), (branch_done, 16), (branch_done, 24), (att_done, 2 * NT - 1),
                         (att_done, 2 * NT), (ple_done, NT), (ple_done, 2 * NT)]

            def big_load(n, parts):
                if n < 2:
                    sp.wait_ge(group_done, G1 + len(REST))
                else:
                    sp.wait_ge(*BIG_FREED[n - 2])
                for dst, src in parts:
                    sp.dma_start(dst, src).then_inc(big_in[n % 2], 16)

            for b, name in enumerate(("w_branch_a", "w_branch_b", "w_branch_c")):
                src = A[name][0]
                if b < 2:
                    src = src.rearrange("(two j d) n -> two d j n", two=2, j=4)
                    parts = [(wb[b][DH * s:DH * s + DH], src[s]) for s in range(2)]
                else:
                    parts = [(wb[b], src.rearrange("(j p) n -> p j n", p=P))]
                big_load(B_BR + b, parts)
                if b == 1:
                    for r in range(2):
                        sp.wait_ge(spilled[r], 16 * (SPILL // 2))
                    for q in range(4):
                        sp.dma_start(gates_back[:, 4 * q:4 * q + 4, :], gates_dram[
                            4 * q * P:4 * (q + 1) * P, :].rearrange("(m p) t -> p m t", p=P)).then_inc(gates_in[q], 16)
                    sp.wait_ge(o_out, OUT0[NJ])
                    sp.dma_start(xr, A["x"][0].rearrange("(i p) d -> p i d", p=P)).then_inc(xr_in, 16)
                    sp.dma_start(ppw, A["ple_w_proj"][0].rearrange("(k p) d -> p k d", p=P)).then_inc(ppw_in, 16)
            wo = A["w_out"][0].rearrange("(k p) d -> p k d", p=P)
            big_load(B_WO, [(wo_h[0], wo[:, :, 0:512])])
            big_load(B_WO + 1, [(wo_h[1], wo[:, :, 512:1024])])
            sp.wait_ge(merged_ready, 1)
            for n, name in enumerate(("ln1_g", "ln1_b", "ln2_g", "ln2_b")):
                sp.dma_start(lnp[:, n, :], A[name][0:1, :].to_broadcast([P, D])).then_inc(late_in, 16)
            sp.wait_ge(branch_done, 24)
            sp.dma_start(pn, A["p"][0, 0].rearrange("(i p) c -> p i c", p=P)).then_inc(late_in, 16)
            sp.dma_start(rw, A["router_w"][0].rearrange("(k p) e -> p k e", p=P)).then_inc(late_in, 16)
            sp.dma_start(rbias, A["router_bias"][0:1, :].to_broadcast([P, NEXP])).then_inc(late_in, 16)
            pg = A["ple_w_gate"][0].rearrange("(k p) d -> p k d", p=P)
            big_load(B_PG, [(pg_h[0], pg[:, :, 0:512])])
            big_load(B_PG + 1, [(pg_h[1], pg[:, :, 512:1024])])
            big_load(B_SG, [(sgu[:, w], A[name][0].rearrange("(k p) f -> p k f", p=P))
                            for w, name in enumerate(("sh_w_gate", "sh_w_up"))])
            big_load(B_SD, [(sdn, A["sh_w_down"][0].rearrange("(k p) d -> p k d", p=P))])

            def load_expert(b, it, r):
                n = turn(b, it, r)
                e = NR * it + r
                gu, dn = eslot(r)
                first = b == 0 and isinstance(it, int) and it == 0
                if not first:
                    sp.wait_ge(gu_done, n - NR + 1)
                for w, name in enumerate(("exp_w_gate", "exp_w_up")):
                    sp.dma_start(gu[:, w], A[name][0, bass.ds(e, 1)].rearrange(
                        "e (p k) f -> p (e k) f", p=P)).then_inc(wgu_in[r], 16)
                if not first:
                    sp.wait_ge(y_done, n - NR + 1)
                sp.dma_start(dn, A["exp_w_down"][0, bass.ds(e, 1)].rearrange(
                    "e (p k) d -> p (e k) d", p=P)).then_inc(wd_in[r], 16)

            sp.wait_ge(route_done, 1)
            load_expert(0, 0, 0)
            load_expert(0, 0, 1)
            sp.wait_ge(sh_y, NT)
            sp.wait_ge(pos_used, 1)
            load_expert(0, 0, 2)
            load_expert(0, 0, 3)

            def expert_loads(b, it0):
                with sp.Fori(it0, NEXP // NR) as it:
                    for r in range(NR):
                        load_expert(b, it, r)

            expert_loads(0, 1)
            sp.wait_ge(cnt_ready, 1)
            most = sp.value_load(cnt[0:1, 0:1], min_val=0, max_val=T)
            with sp.If(most > CAP):
                expert_loads(1, 0)
                with sp.If(most > 2 * CAP):
                    expert_loads(2, 0)
                    with sp.If(most > 3 * CAP):
                        expert_loads(3, 0)
                        sp.nop()
                    sp.nop()
                sp.nop()
            for i in range(NT):
                sp.wait_ge(out_ready, i + 1)
                sp.dma_start(out[0, i * P:(i + 1) * P, :], acc[:, i, :]).then_inc(stored, 16)
            sp.wait_ge(stored, 16 * NT)

        @block.gpsimd
        def _(pool):
            n_const = [0]

            def made(ins):
                n_const[0] += 1
                ins.then_inc(pool_const, 1)
                pool.wait_ge(pool_const, n_const[0])

            made(pool.memset(ident, 0.0))
            made(pool.affine_select(out=ident, in_=ident, compare_op=ALU.not_equal, fill=1.0, base=0,
                                    pattern=[[-1, P]], channel_multiplier=1))
            made(pool.memset(ones, 1.0))
            made(pool.affine_select(out=tri, in_=ones, compare_op=ALU.is_gt, fill=0.0, base=0,
                                    pattern=[[1, P]], channel_multiplier=-1))
            made(pool.iota(iota_s, pattern=[[1, P]], base=0, channel_multiplier=0,
                           allow_small_or_imprecise_dtypes=True))
            made(pool.iota(slot_row, pattern=[[0, NEXP]], base=0, channel_multiplier=1,
                           allow_small_or_imprecise_dtypes=True))
            made(pool.iota(dist, pattern=[[-1, T]], base=T - P, channel_multiplier=1,
                           allow_small_or_imprecise_dtypes=True))
            made(pool.affine_select(out=dist, in_=dist, compare_op=ALU.is_ge, fill=HUGE, base=T - P,
                                    pattern=[[-1, T]], channel_multiplier=1))
            made(pool.iota(distw, pattern=[[-1, 2 * P]], base=P, channel_multiplier=1,
                           allow_small_or_imprecise_dtypes=True))
            made(pool.affine_select(out=distw, in_=distw, compare_op=ALU.is_ge, fill=HUGE, base=P,
                                    pattern=[[-1, 2 * P]], channel_multiplier=1))
            made(pool.affine_select(out=distw, in_=distw, compare_op=ALU.is_gt, fill=HUGE, base=0,
                                    pattern=[[1, 2 * P]], channel_multiplier=-1))
            made(pool.iota(distc, pattern=[[P, NT], [-64, NBLK]], base=-63, channel_multiplier=1,
                           allow_small_or_imprecise_dtypes=True))
            made(pool.affine_select(out=distc, in_=distc, compare_op=ALU.is_ge, fill=HUGE, base=-63,
                                    pattern=[[P, NT], [-64, NBLK]], channel_multiplier=1))
            assert n_const[0] == 13
            for q in range(SPILL):
                pool.wait_ge(group_out, G1 + GATES + q + 1)
                pool.dma_start(gates_dram[q * P:(q + 1) * P, :], gates_ring[:, q % 2, :]).then_inc(spilled[q % 2], 16)
            for i in range(NT):
                pool.wait_ge(x1_ready, i + 1)
                pool.dma_start(x1_dram[i * P:(i + 1) * P, :], x1[:, i, :]).then_inc(x1_stored, 16)
            pool.wait_ge(pt_done, 2)
            pool.iota(RW5[:, :, :, 0], pattern=[[0, NEXP], [0, NT]], base=0, channel_multiplier=1,
                      allow_small_or_imprecise_dtypes=True)
            pool.iota(RW5[:, :, :, 1], pattern=[[0, NEXP], [P, NT]], base=-1024, channel_multiplier=0,
                      allow_small_or_imprecise_dtypes=True).then_inc(xg_zero, 1)
            pool.wait_ge(ple_used, 2 * NT)
            pool.memset(xg, 0.0).then_inc(xg_zero, 1)
            pool.wait_ge(xg_zero, 2)
            pool.wait_ge(x1_stored, 16 * NT)

            last_token = pool.to_reg(T - 1)
            last_row = pool.to_reg(YROWS - 1)

            def gather(b, it, r):
                n = turn(b, it, r)
                pool.wait_ge(col_ready, n + 1)
                if not (isinstance(n, int) and n < NR):
                    pool.wait_ge(xgt_done, 2 * (n - NR) + 2)
                pool.sem_inc(pool_turn, 1)
                pool.indirect_dma_start(
                    xg[:, r, :], None, x1_dram,
                    bass.IndirectOffsetOnAxis(ap=idxr[:, r:r + 1], axis=0),
                    bounds_check=last_token, oob_is_err=False).then_inc(gathered[r], 16)

            def scatter(b, it, r):
                n = turn(b, it, r)
                pool.wait_ge(y_out, 2 * n + 2)
                pool.sem_inc(pool_turn, 1)
                pool.indirect_dma_start(
                    y_dram, bass.IndirectOffsetOnAxis(ap=idyr[:, r:r + 1], axis=0),
                    y[:, r, :], None,
                    bounds_check=last_row, oob_is_err=False).then_inc(scattered[r], 16)

            def expert_rows(b):
                for r in range(NR):
                    gather(b, 0, r)
                last = NEXP // NR - 1
                with pool.Fori(0, last) as it:
                    for r in range(NR):
                        gather(b, it + 1, r)
                        scatter(b, it, r)
                for r in range(NR):
                    scatter(b, last, r)
                for s in range(NR):
                    pool.wait_ge(scattered[s], 16 * (NEXP // NR) * (b + 1))

            expert_rows(0)
            pool.wait_ge(cnt_ready, 1)
            most = pool.value_load(cnt[0:1, 0:1], min_val=0, max_val=T)
            with pool.If(most > CAP):
                expert_rows(1)
                with pool.If(most > 2 * CAP):
                    expert_rows(2)
                    with pool.If(most > 3 * CAP):
                        expert_rows(3)
                        pool.nop()
                    pool.nop()
                pool.nop()
            for i in range(NT):
                for k in range(TOPK):
                    n = i * TOPK + k
                    if n >= NROW:
                        pool.wait_ge(row_in[n % NROW], 16 * (n // NROW))
                    pool.indirect_dma_start(
                        last_rows(n), None, y_dram,
                        bass.IndirectOffsetOnAxis(ap=dest[:, i, k:k + 1], axis=0),
                        bounds_check=last_row, oob_is_err=False).then_inc(row_in[n % NROW], 16)

        @block.scalar
        def _(act):
            act.dma_start(pe_raw[0:32, 0, :], A["nsa_pe_k"][0].rearrange("(l two) d -> l (two d)", two=2)).then_inc(const_in, 16)
            act.dma_start(pe_raw[0:32, 1, :], A["nsa_pe_v"][0].rearrange("(l two) d -> l (two d)", two=2)).then_inc(const_in, 16)
            act.dma_start(w2[:, 0:128].rearrange("p (f d) -> p f d", f=2),
                          A["nsa_w2_k"][0].rearrange("(f p) d -> p f d", p=P)).then_inc(const_in, 16)
            act.dma_start(w2[:, 128:256].rearrange("p (f d) -> p f d", f=2),
                          A["nsa_w2_v"][0].rearrange("(f p) d -> p f d", p=P)).then_inc(const_in, 16)
            act.dma_start(sinks, A["swa_sinks"][0:1, :].to_broadcast([P, 8])).then_inc(const_in, 16)
            for n, name in enumerate(("diff_lq1", "diff_lk1", "diff_lq2", "diff_lk2")):
                act.dma_start(lq[:, n, :], A[name][0:1, :].to_broadcast([P, DH])).then_inc(const_in, 16)
            with nc.allow_non_contiguous_dma(reason="a column of 128 gains"):
                act.dma_start(gcol, A["diff_norm_g"][0].rearrange("(p o) -> p o", o=1)).then_inc(const_in, 16)
            def split_upper(n):
                act.wait_ge(w_in[slot_of(n)], w_count(n))
                if n >= 2:
                    act.wait_ge(group_done, FREED[n - 2])
                act.activation(upper(n, width_of(n)), chunk(n, width_of(n)), ACT.Copy).then_inc(upper_ready, 1)

            def split_after(group):
                if group[5] and group[1] + 2 < NCHUNK:
                    split_upper(group[1] + 2)

            split_upper(0)
            for n in range(2 * NT):
                act.wait_ge(group_done, n + 1)
                i, half = n // 2, n % 2
                act.activation(xh[:, 4 * half:4 * half + 4, i * P:(i + 1) * P],
                               group_bank(n)[:, :].rearrange("p (k t) -> p k t", k=4), ACT.Copy).then_inc(group_out, 1)

            def group_evac(n, group):
                form, _, _, dst, scale, _ = group
                src = group_bank(n)
                q = n - G1 - GATES
                if 2 <= q < SPILL:
                    act.wait_ge(spilled[q % 2], 16 * (q // 2))
                act.wait_ge(group_done, n + 1)
                if isinstance(dst, str):
                    w = 0 if dst == "kc" else 1
                    for kv in range(2):
                        for par in range(2):
                            last = act.activation(
                                KV[DH * par:DH * par + DH, w, :, 8 * kv:8 * kv + 8],
                                src[DH * kv:DH * kv + DH, :].rearrange(
                                    "p (n l two) -> p two l n", n=NBLK, two=2)[:, par], ACT.Copy)
                    last.then_inc(group_out, 1)
                elif form == "Q":
                    q_dst, m = dst
                    for half in range(2):
                        g, j = divmod(2 * m + half, 4)
                        last = act.activation(q_dst[DH * g:DH * g + DH, j, :], src[DH * half:DH * half + DH, :],
                                              ACT.Copy, scale=scale)
                    last.then_inc(group_out, 1)
                elif form == "V":
                    i = group[2]
                    act.activation(vs[:, i, :], src[:, 0:P], ACT.Copy)
                    act.activation(vw[:, i, :], src[:, P:2 * P], ACT.Copy)
                    act.activation(ga[:, i, :], src[:, 2 * P:2 * P + 24], ACT.Sigmoid).then_inc(group_out, 1)
                elif form == "N":
                    act.activation(dst, src[:, :].rearrange("p (i c) -> p i c", i=NT), ACT.Copy).then_inc(group_out, 1)
                elif form == "N2":
                    act.activation(dst, src[:, :].rearrange("p (i c) -> p i c", i=2), ACT.Copy).then_inc(group_out, 1)
                else:
                    act.activation(dst, src[:, :], ACT.Copy, scale=scale).then_inc(group_out, 1)

            split_upper(1)
            act.wait_ge(lam_dot, 1)
            act.activation(lamt[:, 2:4], lamt[:, 0:2], ACT.Exp).then_inc(lam_exp, 1)
            def first_evac(n):
                group_evac(G0 + n, FIRST[n])
                split_after(FIRST[n])

            for n in range(COMPRESS):
                if n == 4:
                    act.wait_ge(embed_done, 1)
                    act.activation(pe2, bank[5][:, 0:64].rearrange("p (w l) -> p w l", w=2),
                                   ACT.Copy).then_inc(embed_out, 1)
                first_evac(n)
            act.wait_ge(hc_done, 1)
            act.activation(hcx[0:16, :], bank[4][0:16, :], ACT.Copy).then_inc(hc_copied, 1)
            first_evac(COMPRESS)
            act.wait_ge(hc_cubic, 1)
            act.activation(hcu[0:16, :], hcu[0:16, :], ACT.Tanh, scale=math.sqrt(2 / math.pi)).then_inc(hc_tanh, 1)
            for n in range(COMPRESS + 1, len(FIRST) - 1):
                first_evac(n)
            act.wait_ge(hct_done, 1)
            act.activation(hcT, bank[5][:, 0:64].rearrange("p (f c) -> p f c", f=4), ACT.Copy,
                           scale=0.5).then_inc(hct_out, 1)
            first_evac(len(FIRST) - 1)
            act.wait_ge(cmp_done, 1)
            act.activation(kcmp, bank[4][:, 0:8], ACT.Copy)
            act.activation(vcmp[0:8, :], bank[4][0:8, 128:256], ACT.Copy).then_inc(cmp_out, 1)

            def exps(s):
                kind, g, i = JOBS[s]
                n = keys_of(kind, i)[1] + (kind == "swa")
                act.wait_ge(max_ready, s + 1)
                for j in range(4):
                    row = S[:, 4 * (s % 2) + j, 0:n]
                    last = act.activation(row, row, ACT.Exp, bias=negm[:, s % 2, j:j + 1],
                                          accum_out=esum[:, s % 2, j:j + 1])
                last.then_inc(exped, 1)

            def turned_evacs(s, part):
                first, last = TURN0[s], TURN0[s + 1]
                for n in range(first, last)[:2] if part == 0 else range(first, last)[2:]:
                    act.wait_ge(turned, n + 1)
                    if n >= 4:
                        act.wait_ge(pv_done, n - 3)
                    act.activation(PT[:, n % 4, :], bank[4 + n % 2][:, :], ACT.Copy).then_inc(turned_out, 1)
                if CLOSES[s] and part:
                    kind, g, i = JOBS[s]
                    act.wait_ge(pv_done, TURN0[s + 1])
                    rows = slice(DH * g, DH * g + DH)
                    if kind == "dif":
                        act.activation(odn[:, i, 256 * g:256 * g + 256], bank[6][:, 0:256], ACT.Copy).then_inc(o_out, 1)
                    else:
                        dst = ob if kind == "swa" else oa
                        act.activation(dst[rows, :, i * P:(i + 1) * P],
                                       bank[6][rows, :].rearrange("p (j t) -> p j t", j=4),
                                       ACT.Copy).then_inc(o_out, 1)

            for s in range(NJ + 1):
                if s < NJ:
                    exps(s)
                if s >= 1:
                    turned_evacs(s - 1, 0)
                if s < NJ:
                    for n in range(REST_AT[s], REST_AT[s + 1]):
                        group_evac(G1 + n, REST[n])
                if s >= 1:
                    turned_evacs(s - 1, 1)
                if s < NJ:
                    for n in range(REST_AT[s], REST_AT[s + 1]):
                        split_after(REST[n])
            act.wait_ge(o_out, OUT0[NJ])
            for n in range(16):
                row = odn[:, n // 4, P * (n % 4):P * (n % 4) + P]
                last = act.activation(S[:, n // 4, P * (n % 4):P * (n % 4) + P], row, ACT.Square, accum_out=ssq[:, n:n + 1])
            last.then_inc(sq_done, 1)
            act.wait_ge(rms_in, 1)
            act.activation(rms, ssq, ACT.Sqrt).then_inc(rms_root, 1)
            act.wait_ge(group_out, G1 + len(REST))
            for n in range(24):
                if n == 16:
                    for hd in range(4):
                        act.wait_ge(oct_done, hd + 1)
                        act.activation(oc[:, hd, :], bank[4 + hd % 2][:, :], ACT.Copy,
                                       scale=gcol).then_inc(oct_out, 1)
                if n >= ND and n % 4 == 0:
                    act.wait_ge(gates_in[n // 4 - 2], 16)
                act.activation(gates(n), gates(n), ACT.Sigmoid).then_inc(sig_done, 1)
            def x1t_evac(i):
                for half in range(2):
                    n = 2 * i + half
                    act.wait_ge(x1t_done, n + 1)
                    act.activation(x1T[:, 4 * half:4 * half + 4, i * P:(i + 1) * P],
                                   bank[4 + half][:, :].rearrange("p (k t) -> p k t", k=4), ACT.Copy).then_inc(x1t_out, 1)

            def residual(i):
                act.wait_ge(x1_ready, i + 1)
                act.activation(acc[:, i, :], x1[:, i, :], ACT.Copy, scale=ALPHA).then_inc(residual_in, 1)

            for i in range(NT):
                act.wait_ge(var_ready, i + 1)
                act.activation(rstd, var_e, ACT.Sqrt).then_inc(root_ready, 1)
                if i >= 1:
                    x1t_evac(i - 1)
                    residual(i - 1)
            for k in range(2):
                act.wait_ge(pt_done, k + 1)
                act.activation(pT[:, k, :], bank[4 + k][:, :], ACT.Copy).then_inc(pt_out, 1)
            x1t_evac(NT - 1)
            residual(NT - 1)
            act.wait_ge(route_done, 1)
            act.activation(sc, bank[6][:, 0:256].rearrange("p (i e) -> p i e", i=NT), ACT.Sigmoid).then_inc(route_sig, 1)
            for n in range(2 * NT):
                act.wait_ge(ple_done, n + 1)
                if n >= 2:
                    act.wait_ge(ple_used, n - 1)
                act.activation(ple_sg[:, n % 2, :], bank[n % 2][:, :], ACT.Sigmoid).then_inc(ple_sig, 1)
            for i in range(NT):
                act.wait_ge(sh_gu, i + 1)
                act.activation(sg[:, i % 2, :], bank[i % 2][:, 0:F], ACT.Sigmoid).then_inc(sh_sig, 1)

            def xgt_evac(b, it, r):
                n = turn(b, it, r)
                for half in range(2):
                    act.wait_ge(xgt_done, 2 * n + half + 1)
                    if half == 0 and not (isinstance(n, int) and n < 2):
                        act.wait_ge(gu_done, n - 1)
                    act.activation(xgT[:, r % 2, 4 * half:4 * half + 4, :],
                                   bank[half][:, :].rearrange("p (k s) -> p k s", k=4), ACT.Copy).then_inc(xgt_out, 1)

            def gate_sig(b, it, r):
                n = turn(b, it, r)
                act.wait_ge(gu_done, n + 1)
                if not (isinstance(n, int) and n < 2):
                    act.wait_ge(h_ready, n - 1)
                act.activation(sg[:, r % 2, :], bank[2 + r % 2][:, 0:F], ACT.Sigmoid).then_inc(e_sig, 1)

            def y_evac(b, it, r):
                n = turn(b, it, r)
                act.wait_ge(y_done, n + 1)
                act.wait_ge(ycol_ready, n + 1)
                for half in range(2):
                    act.activation(y[:, r, 512 * half:512 * half + 512], bank[5 + half][:, :],
                                   ACT.Copy, scale=wgr[:, r:r + 1]).then_inc(y_out, 1)

            def expert_acts(b):
                xgt_evac(b, 0, 0)

                def step(it, r, before):
                    gate_sig(b, it, r)
                    xgt_evac(b, it + (r + 1) // NR, (r + 1) % NR)
                    if before is not None:
                        y_evac(b, *before)

                for r in range(NR):
                    step(0, r, (0, r - 1) if r else None)
                last = NEXP // NR - 1
                with act.Fori(1, last) as it:
                    for r in range(NR):
                        step(it, r, (it, r - 1) if r else (it - 1, NR - 1))
                for r in range(NR - 1):
                    step(last, r, (last, r - 1) if r else (last - 1, NR - 1))
                gate_sig(b, last, NR - 1)
                y_evac(b, last, NR - 2)
                y_evac(b, last, NR - 1)

            expert_acts(0)
            act.wait_ge(cnt_ready, 1)
            most = act.value_load(cnt[0:1, 0:1], min_val=0, max_val=T)
            with act.If(most > CAP):
                expert_acts(1)
                with act.If(most > 2 * CAP):
                    expert_acts(2)
                    with act.If(most > 3 * CAP):
                        expert_acts(3)
                        act.nop()
                    act.nop()
                act.nop()
            for i in range(NT):
                act.wait_ge(var_ready, NT + i + 1)
                act.activation(rstd, var_e, ACT.Sqrt).then_inc(root_ready, 1)

        @block.vector
        def _(dve):
            links = [0]
            in_loop = [False]

            def link(ins):
                links[0] += 1
                ins.then_inc(chain, 1)
                dve.wait_ge(chain, links[0])

            dve.memset(vcmp, 0.0)
            dve.memset(esum[:, :, :].rearrange("p r j -> p (r j)"), 0.0)
            def split_lower(n):
                dve.wait_ge(upper_ready, n + 1)
                w = width_of(n)
                dve.tensor_tensor(lower(n, w), chunk(n, w), upper(n, w), ALU.subtract).then_inc(lower_ready, 1)

            split_lower(0)
            for n in range(2 * NT):
                i, half = n // 2, n % 2
                cut = (slice(None), slice(4 * half, 4 * half + 4), slice(i * P, (i + 1) * P))
                dve.wait_ge(group_out, n + 1)
                dve.tensor_tensor(xl[cut], group_bank(n)[:, :].rearrange("p (k t) -> p k t", k=4), xh[cut],
                                  ALU.subtract).then_inc(x_low, 1)

            dve.wait_ge(const_in, 16 * 10)
            link(dve.tensor_tensor(lq[:, 0:3:2, :], lq[:, 0:3:2, :], lq[:, 1:4:2, :], ALU.mult))
            dve.tensor_reduce(lamt[:, 0:2], lq[:, 0:3:2, :], axis=AXX, op=ALU.add).then_inc(lam_dot, 1)
            dve.wait_ge(lam_exp, 1)
            link(dve.tensor_tensor(lamt[:, 0:1], lamt[:, 3:4], lamt[:, 2:3], ALU.subtract))
            dve.memset(lamv, 1.0)
            link(dve.tensor_scalar(gcol, gcol, 1.0 - LAMBDA_INIT, None, ALU.mult))
            for j in (1, 3):
                last = dve.tensor_scalar(lamv[:, j:j + 1], lamt[:, 0:1], -LAMBDA_INIT, None, ALU.add)
            link(last)
            for n in range(1, 4):
                split_lower(n)
            dve.wait_ge(embed_out, 1)
            for w in range(2):
                dve.wait_ge(group_out, G0 + 4 + w + 1)
                dve.tensor_tensor(KV[:, w], KV[:, w], pe2[:, w, :].unsqueeze(2).to_broadcast([P, 32, 16]),
                                  ALU.add).then_inc(pe_added, 1)
            split_lower(4)
            dve.wait_ge(hc_copied, 1)
            link(dve.tensor_tensor(hcu[0:16, :], hcx[0:16, :], hcx[0:16, :], ALU.mult))
            link(dve.tensor_scalar(hcu[0:16, :], hcu[0:16, :], 0.044715, 1.0, ALU.mult, ALU.add))
            dve.tensor_tensor(hcu[0:16, :], hcu[0:16, :], hcx[0:16, :], ALU.mult).then_inc(hc_cubic, 1)
            dve.wait_ge(hc_tanh, 1)
            dve.scalar_tensor_tensor(hcu[0:16, :], hcu[0:16, :], 1.0, hcx[0:16, :], ALU.add,
                                     ALU.mult).then_inc(hc_ready, 1)
            split_lower(REST0)
            split_lower(REST0 + 1)
            dve.wait_ge(pool_const, 13)

            def bias_and_max(s):
                kind, g, i = JOBS[s]
                n = keys_of(kind, i)[1]
                rows = S[:, 4 * (s % 2):4 * (s % 2) + 4, :]
                if s >= 2:
                    dve.wait_ge(turned, TURN0[s - 1])
                if kind == "cmp":
                    dve.memset(rows[:, :, NBLK:P], 0.0)
                if kind == "swa":
                    dve.tensor_copy(rows[:, :, n:n + 1], sinks[:, 4 * g:4 * g + 4].unsqueeze(2))
                for j in range(4):
                    dve.wait_ge(scored, 4 * s + j + 1)
                    last = dve.scalar_tensor_tensor(rows[:, j, 0:n], distances(kind, i, n),
                                                    -slope_of(kind, g, j), bank[j][:, 0:n],
                                                    ALU.mult, ALU.add)
                    last.then_inc(biased, 1)
                dve.wait_ge(biased, 4 * s + 4)
                if s >= 2:
                    dve.wait_ge(exped, s - 1)
                m = dve.tensor_reduce(negm[:, s % 2, :], rows[:, :, 0:n + (kind == "swa")], axis=AXX,
                                      op=ALU.max, negate=True)
                if kind == "cmp":
                    link(m)
                    m = dve.tensor_scalar(negm[:, s % 2, :], negm[:, s % 2, :], 1e29, None, ALU.min)
                m.then_inc(max_ready, 1)

            def weigh(s):
                kind, g, i = JOBS[s]
                n = keys_of(kind, i)[1]
                f = fac[:, s % 2, :]
                dve.wait_ge(exped, s + 1)
                e = esum[:, s % 2, :]
                if kind == "cmp":
                    link(dve.tensor_scalar(e, e, 1e-30, None, ALU.max))
                link(dve.reciprocal(f, e))
                if kind in ("slc", "win", "cmp"):
                    br = ("cmp", "slc", "win").index(kind)
                    gates = ga[:, i, 12 * g + br:12 * g + br + 10:3]
                    link(dve.tensor_tensor(f, f, gates, ALU.mult))
                if kind == "dif":
                    link(dve.tensor_tensor(f, f, lamv, ALU.mult))
                    for hh in range(2):
                        a, b = (S[:, 4 * (s % 2) + 2 * hh + r, 0:n] for r in range(2))
                        link(dve.tensor_scalar(b, b, f[:, 2 * hh + 1:2 * hh + 2], None, ALU.mult))
                        last = dve.scalar_tensor_tensor(a, a, f[:, 2 * hh:2 * hh + 1], b, ALU.mult, ALU.add)
                else:
                    for j in range(4):
                        row = S[:, 4 * (s % 2) + j, 0:n]
                        last = dve.tensor_scalar(row, row, f[:, j:j + 1], None, ALU.mult)
                last.then_inc(probs, 1)

            for s in range(NJ):
                bias_and_max(s)
                if s >= 1:
                    for n in range(REST_AT[s - 1], REST_AT[s]):
                        if REST[n][5] and REST[n][1] + 2 < NCHUNK:
                            split_lower(REST[n][1] + 2)
                weigh(s)
            dve.wait_ge(sq_done, 1)
            dve.tensor_scalar(ssq, ssq, 1.0 / (2 * DH), EPS, ALU.mult, ALU.add).then_inc(rms_in, 1)
            dve.wait_ge(rms_root, 1)
            link(dve.reciprocal(rms, rms))
            for n in range(16):
                row = odn[:, n // 4, P * (n % 4):P * (n % 4) + P]
                last = dve.tensor_scalar(row, row, rms[:, n:n + 1], None, ALU.mult)
            last.then_inc(od_ready, 1)
            for n in range(24):
                m = n % 8
                dve.wait_ge(sig_done, n + 1)
                dve.wait_ge(branch_done, n + 1)
                dst = merged[:, m, :] if n < 8 else mtmp[:, n % 2, :]
                ins = dve.tensor_tensor(dst, bank[n % 4][:, :], gates(n), ALU.mult)
                ins.then_inc(branch_used, 1)
                if n >= 8:
                    dve.wait_ge(branch_used, n + 1)
                    last = dve.tensor_tensor(merged[:, m, :], merged[:, m, :], mtmp[:, n % 2, :], ALU.add)
                    if n == 23:
                        last.then_inc(merged_ready, 1)

            def layer_norm(src, dst, w, root):
                for c in range(2):
                    last = dve.bn_stats(stats[:, c, :], src[:, 512 * c:512 * c + 512])
                link(last)
                link(dve.bn_aggr(mv, stats))
                if root > 1:
                    dve.wait_ge(root_ready, root - 1)
                dve.tensor_scalar(var_e, mv[:, 1:2], EPS, None, ALU.add).then_inc(var_ready, 1)
                dve.wait_ge(root_ready, root)
                link(dve.reciprocal(rstd, rstd))
                link(dve.tensor_scalar(dst, src, mv[:, 0:1], rstd, ALU.subtract, ALU.mult))
                link(dve.tensor_tensor(dst, dst, lnp[:, w, :], ALU.mult))
                return dve.tensor_tensor(dst, dst, lnp[:, w + 1, :], ALU.add)

            dve.wait_ge(xr_in, 16)
            for i in range(NT):
                for half in range(2):
                    cols = slice(512 * half, 512 * half + 512)
                    dve.wait_ge(att_done, 2 * i + half + 1)
                    last = dve.scalar_tensor_tensor(z[:, i % 2, cols], xr[:, i, cols], ALPHA,
                                                    bank[2 * (i % 2) + half][:, :], ALU.mult, ALU.add)
                    last.then_inc(att_used, 1)
                dve.wait_ge(att_used, 2 * i + 2)
                if i == 0:
                    dve.wait_ge(late_in, 16 * 7)
                layer_norm(z[:, i % 2, :], x1[:, i, :], 0, i + 1).then_inc(x1_ready, 1)

            dve.wait_ge(route_sig, 1)
            dve.memset(gs[:, :, NGRP:NGRP + 4], -1e30)
            link(dve.tensor_tensor(bi, sc, rbias.unsqueeze(1).to_broadcast([P, NT, NEXP]), ALU.add))
            for i in range(NT):
                for g in range(NGRP):
                    last = dve.max(g8[:, i, g, :], bi[:, i, GSZ * g:GSZ * g + GSZ])
            link(last)
            link(dve.tensor_tensor(gs[:, :, 0:NGRP], g8[:, :, :, 0], g8[:, :, :, 1], ALU.add))
            for i in range(NT):
                last = dve.max(gt8[:, i, :], gs[:, i, 0:NGRP])
            link(last)
            link(dve.memset(gt8[:, :, TOPG:8], -1e30))
            for i in range(NT):
                last = dve.match_replace(gr[:, i, :], gt8[:, i, :], gs[:, i, :], -2e30)
            link(last)
            link(dve.tensor_scalar(gmask, gr[:, :, 0:NGRP], -1.5e30, None, ALU.is_lt))
            link(dve.tensor_scalar(gneg, gmask, -1.0, 1e30, ALU.add, ALU.mult))

            def by_expert(t):
                return t.rearrange("p i (g c) -> p i g c", g=NGRP)

            for i in range(NT):
                gb = gmask[:, i, :].unsqueeze(2).to_broadcast([P, NGRP, GSZ])
                last = dve.tensor_tensor(by_expert(m1)[:, i], by_expert(bi)[:, i], gb, ALU.mult)
            link(last)
            for i in range(NT):
                gb = gneg[:, i, :].unsqueeze(2).to_broadcast([P, NGRP, GSZ])
                last = dve.tensor_tensor(by_expert(m1)[:, i], by_expert(m1)[:, i], gb, ALU.add)
            link(last)
            for i in range(NT):
                last = dve.max(v8[:, i, :], m1[:, i, :])
            link(last)
            for i in range(NT):
                last = dve.match_replace(rep[:, i, :], v8[:, i, :], m1[:, i, :], -3e30)
            link(last)
            link(dve.tensor_scalar(sel, rep, -2e30, None, ALU.is_lt))
            dve.tensor_copy(selb, sel).then_inc(sel_ready, 1)
            link(dve.tensor_tensor(ws, sc, sel, ALU.mult))
            link(dve.tensor_reduce(wsum, ws, axis=AXX, op=ALU.add))
            link(dve.reciprocal(wrec, wsum))
            for i in range(NT):
                last = dve.tensor_scalar(ws[:, i, :], ws[:, i, :], wrec[:, i:i + 1], ROUTED_SCALE,
                                         ALU.mult, ALU.mult)
            link(last)
            dve.wait_ge(xg_zero, 1)

            def part(c):
                return RW5[:, :, :, c].rearrange("p e i -> p i e")

            link(dve.tensor_copy(part(2), ws))
            link(dve.tensor_tensor(wr1, ws, part(2), ALU.subtract))
            link(dve.tensor_copy(part(3), wr1))
            link(dve.tensor_tensor(part(4), wr1, part(3), ALU.subtract))

            def ple(n):
                half, i = n // NT, n % NT
                cols = slice(512 * half, 512 * half + 512)
                dve.wait_ge(ple_sig, n + 1)
                ins = dve.tensor_tensor(ple_sg[:, n % 2, :], ple_sg[:, n % 2, :], bank[2 + n % 2][:, :], ALU.mult)
                link(ins)
                dve.tensor_tensor(acc[:, i, cols], acc[:, i, cols], ple_sg[:, n % 2, :],
                                  ALU.add).then_inc(ple_used, 1)

            dve.wait_ge(residual_in, NT)
            for n in range(NT):
                ple(n)
            dve.wait_ge(pos_done, 1)
            posp = bank[7][:, 0:256].rearrange("p (i e) -> p i e", i=NT)
            link(dve.scalar_tensor_tensor(pos1, posp, 1.0, sel, ALU.add, ALU.mult))
            count = bank[7][:, 256:320]
            link(dve.tensor_copy(before[0], count))
            link(dve.tensor_scalar(minus_p, slot_row[:, 0:1], -1.0, None, ALU.mult))
            for step in range(6):
                a, b, w = before[step % 2], before[(step + 1) % 2], 1 << step
                dve.tensor_copy(b[:, 0:w], a[:, 0:w])
                link(dve.tensor_tensor(b[:, w:], a[:, w:], a[:, 0:NEXP - w], ALU.add))
            link(dve.tensor_tensor(slot_row, slot_row, before[0], ALU.add))
            link(dve.tensor_tensor(slot_row, slot_row, count, ALU.subtract))
            dve.tensor_scalar(posE.rearrange("p e i -> p i e"), pos1, -1.0, None, ALU.add)
            for i in range(NT):
                last = dve.tensor_tensor(dd[:, i, :], sel[:, i, :], slot_row, ALU.mult)
            link(last)
            link(dve.tensor_tensor(dd, dd, pos1, ALU.add))
            for i in range(NT):
                last = dve.max(d8[:, i, :], dd[:, i, :])
            link(last)
            link(dve.tensor_scalar(d8, d8, minus_p, -1.0, ALU.add, ALU.add))
            link(dve.tensor_copy(dest, d8))
            link(dve.tensor_reduce(cmax, bank[7][:, 256:320], axis=AXX, op=ALU.max))
            dve.tensor_copy(cnt, cmax).then_inc(cnt_ready, 1)
            dve.nop().then_inc(pos_used, 1)

            def hot(r, e, n):
                if not (isinstance(n, int) and n < NHOT):
                    dve.wait_ge(hot_used, n - NHOT + 1)
                for i in range(NT):
                    last = dve.tensor_scalar(onehot[:, r, i, :], iota_s, posE[:, bass.ds(e, 1), i], None,
                                             ALU.is_equal)
                last.then_inc(hot_ready, 1)

            def index_tables(b):
                dve.wait_ge(idx_done, b + 1)
                t5 = bank[7][:, 0:320].rearrange("p (e c) -> p e c", c=5)
                dve.tensor_copy(IDX, t5[:, :, 0]).then_inc(index_chain, 1)
                dve.wait_ge(index_chain, 7 * b + 1)
                dve.tensor_tensor(IDX, IDX, t5[:, :, 1], ALU.add).then_inc(index_chain, 1)
                dve.tensor_reduce(WG, t5[:, :, 2:5], axis=AXX, op=ALU.add)
                dve.wait_ge(index_chain, 7 * b + 2)
                dve.tensor_scalar(IDX, IDX, 1024.0, None, ALU.add).then_inc(index_chain, 1)
                dve.wait_ge(index_chain, 7 * b + 3)
                dve.tensor_scalar(IDY, IDX, float(T), 65536.0, ALU.is_ge, ALU.mult).then_inc(index_chain, 1)
                dve.wait_ge(index_chain, 7 * b + 4)
                dve.tensor_tensor(IDY, IDY, slot_row, ALU.add).then_inc(index_chain, 1)
                dve.wait_ge(index_chain, 7 * b + 5)
                dve.tensor_scalar(IDY, IDY, float(CAP * b), None, ALU.add).then_inc(index_chain, 1)
                dve.wait_ge(index_chain, 7 * b + 6)
                dve.tensor_scalar(posE, posE, -float(CAP), None, ALU.add).then_inc(index_chain, 1)
                dve.wait_ge(index_chain, 7 * b + 7)
                dve.nop().then_inc(idx_used, 1)

            def index_pass(b):
                with dve.Fori(0, NEXP // 4) as it:
                    for r in range(4):
                        n = turn(b, it, r)
                        hot_loop(r, 4 * it + r, n)
                index_tables(b)

            def hot_loop(r, e, n):
                dve.wait_ge(hot_used, n - 3)
                for i in range(NT):
                    last = dve.tensor_scalar(onehot[:, r, i, :], iota_s, posE[:, bass.ds(e, 1), i], None,
                                             ALU.is_equal)
                last.then_inc(hot_ready, 1)

            def hots(batch):
                for n in range(HOT0[batch], HOT0[batch + 1]):
                    hot(n % NHOT, n, n)

            def tokens_of(it, r):
                e = NR * it + r
                dve.tensor_copy(idxr[:, r:r + 1], IDX[:, bass.ds(e, 1)]).then_inc(col_ready, 1)

            dve.wait_ge(x1_stored, 16 * NT)
            for n in range(NT, 2 * NT):
                ple(n)
                hots(n - NT)
            for i in range(NT):
                dve.wait_ge(sh_sig, i + 1)
                if i >= 2:
                    dve.wait_ge(sh_ht, i - 1)
                link(dve.tensor_tensor(sg[:, i % 2, :], sg[:, i % 2, :], bank[i % 2][:, 0:F], ALU.mult))
                dve.tensor_tensor(h[:, i % 2, :], sg[:, i % 2, :], bank[i % 2][:, F:2 * F], ALU.mult).then_inc(sh_h, 1)
                if i < 2:
                    hots(NT + 2 * i)
                dve.wait_ge(sh_ht, i + 1)
                dve.tensor_copy(hT[:, i % 2], bank[4][:, 0:256].rearrange("p (k s) -> p k s", k=NF)).then_inc(sh_hto, 1)
                if i < 2:
                    hots(NT + 2 * i + 1)
                for half in range(2):
                    cols = slice(512 * half, 512 * half + 512)
                    dve.wait_ge(sh_y, i + 1)
                    last = dve.tensor_tensor(acc[:, i, cols], acc[:, i, cols], bank[2 + half][:, :], ALU.add)
                last.then_inc(sh_used, 1)
                if i == 1:
                    index_tables(0)
                    for r in range(NR):
                        tokens_of(0, r)

            def rows_of(b, it, r):
                n = turn(b, it, r)
                e = NR * it + r
                if not (isinstance(n, int) and n < NR):
                    dve.wait_ge(scattered[r], 16 * (NEXP // NR * b + it))
                dve.tensor_copy(idyr[:, r:r + 1], IDY[:, bass.ds(e, 1)])
                dve.tensor_copy(wgr[:, r:r + 1], WG[:, bass.ds(e, 1)]).then_inc(ycol_ready, 1)

            silu = sem("silu")

            def hidden_all(b, it, r):
                n = turn(b, it, r)
                dve.wait_ge(e_sig, n + 1)
                if not (isinstance(n, int) and n < 2):
                    dve.wait_ge(ht_done, n - 1)
                dve.tensor_tensor(sg[:, r % 2, :], sg[:, r % 2, :], bank[2 + r % 2][:, 0:F],
                                  ALU.mult).then_inc(silu, 1)
                dve.wait_ge(silu, n + 1)
                dve.tensor_tensor(h[:, r % 2, :], sg[:, r % 2, :], bank[2 + r % 2][:, F:2 * F],
                                  ALU.mult).then_inc(h_ready, 1)

            def hidden_evac(b, it, r):
                n = turn(b, it, r)
                dve.wait_ge(ht_done, n + 1)
                if not (isinstance(n, int) and n < 2):
                    dve.wait_ge(y_done, n - 1)
                dve.tensor_copy(hT[:, r % 2], bank[4][:, 0:256].rearrange("p (k s) -> p k s", k=NF)).then_inc(ht_out, 1)

            def expert_vectors(b):
                if b:
                    index_pass(b)
                    for r in range(NR):
                        tokens_of(0, r)

                def step(it, r, before, after=True):
                    if before is not None:
                        hidden_evac(b, *before)
                    hidden_all(b, it, r)
                    if after:
                        tokens_of(it + 1, r)
                    rows_of(b, it, r)

                for r in range(NR):
                    step(0, r, (0, r - 1) if r else None)
                last = NEXP // NR - 1
                with dve.Fori(1, last) as it:
                    for r in range(NR):
                        step(it, r, (it, r - 1) if r else (it - 1, NR - 1))
                for r in range(NR):
                    step(last, r, (last, r - 1) if r else (last - 1, NR - 1), after=False)
                hidden_evac(b, last, NR - 1)

            expert_vectors(0)
            after_first = links[0]
            dve.wait_ge(cnt_ready, 1)
            most = dve.value_load(cnt[0:1, 0:1], min_val=0, max_val=T)
            with dve.If(most > CAP):
                expert_vectors(1)
                with dve.If(most > 2 * CAP):
                    expert_vectors(2)
                    with dve.If(most > 3 * CAP):
                        expert_vectors(3)
                        dve.nop()
                    dve.nop()
                dve.nop()
            final = sem("final_chain")
            links_f = [0]

            def flink(ins):
                links_f[0] += 1
                ins.then_inc(final, 1)
                dve.wait_ge(final, links_f[0])

            for i in range(NT):
                for k in range(TOPK):
                    n = i * TOPK + k
                    dve.wait_ge(row_in[n % NROW], 16 * (n // NROW + 1))
                    dve.tensor_tensor(acc[:, i, :], acc[:, i, :], last_rows(n), ALU.add).then_inc(row_added, 1)
                    dve.wait_ge(row_added, n + 1)
                for c in range(2):
                    last = dve.bn_stats(stats[:, c, :], acc[:, i, 512 * c:512 * c + 512])
                flink(last)
                flink(dve.bn_aggr(mv, stats))
                dve.tensor_scalar(var_e, mv[:, 1:2], EPS, None, ALU.add).then_inc(var_ready, 1)
                dve.wait_ge(root_ready, NT + i + 1)
                flink(dve.reciprocal(rstd, rstd))
                flink(dve.tensor_scalar(acc[:, i, :], acc[:, i, :], mv[:, 0:1], rstd, ALU.subtract, ALU.mult))
                flink(dve.tensor_tensor(acc[:, i, :], acc[:, i, :], lnp[:, 2, :], ALU.mult))
                dve.tensor_tensor(acc[:, i, :], acc[:, i, :], lnp[:, 3, :], ALU.add).then_inc(out_ready, 1)

        @block.tensor
        def _(pe):
            mm = pe.matmul
            pe.wait_ge(pool_const, 13)
            for n in range(2 * NT):
                i, half = n // 2, n % 2
                if half == 0:
                    pe.wait_ge(x_in[i], 16)
                if n >= 4:
                    pe.wait_ge(x_low, n - 3)
                for k in range(4):
                    last = pe.transpose(group_bank(n)[:, k * P:(k + 1) * P],
                                        x0[:, i, (4 * half + k) * P:(4 * half + k + 1) * P], ident)
                last.then_inc(group_done, 1)
            def products(dst, stationary, moving):
                (sh, sl), (mh, ml) = stationary, moving
                for k in range(ND):
                    mm(dst, sh(k), mh(k), start=(k == 0), stop=False)
                    mm(dst, sh(k), ml(k), start=False, stop=False)
                    last = mm(dst, sl(k), mh(k), start=False, stop=(k == ND - 1))
                return last

            def group(n, desc):
                form, c, col, _, _, _ = desc
                dstb = group_bank(n)
                pe.wait_ge(lower_ready, c + 1)
                pe.wait_ge(group_out, n - 1 if n < G1 else n)
                w_halves = upper(c, width_of(c)), lower(c, width_of(c))
                if form in ("T", "Q"):
                    last = products(dstb[:, :], [lambda k, a=a: a[:, k, col:col + P] for a in w_halves],
                                    [lambda k, a=a: a[:, k, :] for a in (xh, xl)])
                else:
                    tiles, c0, width = {"N": (range(NT), col, P), "N2": (range(col, col + 2), 0, 2 * P),
                                        "V": (range(col, col + 1), 0, width_of(c))}[form]
                    for a, i in enumerate(tiles):
                        last = products(dstb[:, a * width:(a + 1) * width],
                                        [lambda k, a=a, i=i: a[:, k, i * P:(i + 1) * P] for a in (xh, xl)],
                                        [lambda k, a=a: a[:, k, c0:c0 + width] for a in w_halves])
                last.then_inc(group_done, 1)

            pe.wait_ge(x_low, 2 * NT)
            for n in range(COMPRESS):
                if n == 4:
                    pe.wait_ge(const_in, 16 * 10)
                    for w in range(2):
                        last = pe.transpose(bank[5][:, 32 * w:32 * w + 32], pe_raw[0:32, w, :], ident[0:32, 0:32])
                    last.then_inc(embed_done, 1)
                group(G0 + n, FIRST[n])
            for w in range(2):
                pe.wait_ge(pe_added, w + 1)
                pe.wait_ge(w1_in[w], 16 * NW1)
                for c in range(NW1):
                    for a in range(ND):
                        la = c * ND + a
                        last = mm(bank[4][0:16, 256 * w:256 * w + 256], KV[:, w, la, :], w1_chunk(w, c)[:, a, :],
                                  start=(la == 0), stop=(la == NW1 * ND - 1))
            last.then_inc(hc_done, 1)
            for n in range(COMPRESS, len(FIRST) - 1):
                group(G0 + n, FIRST[n])
            pe.wait_ge(hc_ready, 1)
            for f in range(4):
                last = pe.transpose(bank[5][:, 16 * f:16 * f + 16], hcu[0:16, P * f:P * f + P], ident[0:16, 0:16])
            last.then_inc(hct_done, 1)
            group(G1 - 1, FIRST[-1])
            pe.wait_ge(hct_out, 1)
            w2k = w2[:, 0:128].rearrange("p (f d) -> p f d", f=2)
            w2v = w2[:, 128:256].rearrange("p (f d) -> p f d", f=2)
            for g in range(2):
                for f in range(2):
                    mm(bank[4][DH * g:DH * g + DH, 0:8], w2k[:, f, :], hcT[:, f, 8 * g:8 * g + 8],
                       start=(f == 0), stop=(f == 1))
            for g in range(2):
                for f in range(2):
                    last = mm(bank[4][0:8, 128 + DH * g:128 + DH * g + DH], hcT[:, 2 + f, 8 * g:8 * g + 8],
                              w2v[:, f, :], start=(f == 0), stop=(f == 1))
            last.then_inc(cmp_done, 1)
            pe.wait_ge(cmp_out, 1)

            def scores(s):
                kind, g, i = JOBS[s]
                n = keys_of(kind, i)[1]
                pe.wait_ge(group_out, need_group(kind))
                for j in range(4):
                    if s >= 1:
                        pe.wait_ge(biased, 4 * (s - 1) + j + 1)
                    q, k = unit_operands(kind, g, i, j)
                    mm(bank[j][:, 0:n], q, k, start=True, stop=True).then_inc(scored, 1)

            opened = {}

            def turn_and_value(s, between):
                kind, g, i = JOBS[s]
                lo = keys_of(kind, i)[0]
                nb = blocks_of(kind, i)
                pe.wait_ge(probs, s + 1)
                first_of_out = s == 0 or CLOSES[s - 1]

                def transposes(n, a):
                    if n >= 2:
                        pe.wait_ge(turned_out, n - 1)
                    for q in range(nb if kind == "dif" else 4):
                        if kind == "dif":
                            src = S[:, 4 * (s % 2) + 2 * a, q * P:(q + 1) * P]
                        else:
                            src = S[:, 4 * (s % 2) + q, a * P:(a + 1) * P]
                        last = pe.transpose(bank[4 + n % 2][:, q * P:(q + 1) * P], src, ident)
                    last.then_inc(turned, 1)

                def values(n, a):
                    pe.wait_ge(turned_out, n + 1)
                    if first_of_out and a == 0 and OUT0[s] >= 1:
                        pe.wait_ge(o_out, OUT0[s])
                    rows = slice(DH * g, DH * g + DH)
                    if kind == "dif":
                        hd = 2 * g + a
                        for q in range(nb):
                            last = mm(bank[6][:, P * a:P * a + P], PT[:, n % 4, q * P:(q + 1) * P],
                                      vd[:, q, P * hd:P * hd + P], start=(q == 0), stop=(q == nb - 1))
                    else:
                        v = {"slc": lambda: vs[:, a, rows], "win": lambda: vw[:, a, rows],
                             "swa": lambda: vb[:, lo + a, rows], "cmp": lambda: vcmp[:, rows]}[kind]()
                        last = mm(bank[6][rows, :], v, PT[:, n % 4, :], start=first_of_out and a == 0,
                                  stop=CLOSES[s] and a == turns - 1)
                    last.then_inc(pv_done, 1)

                turns = turns_of(kind, i)
                t0 = TURN0[s]
                ahead = min(2, turns)
                for a in range(ahead):
                    transposes(t0 + a, a)
                between()
                for a in range(turns):
                    values(t0 + a, a)
                    if a + ahead < turns:
                        transposes(t0 + a + ahead, a + ahead)

            for s in range(NJ + 1):
                def project():
                    if s < NJ:
                        for n in range(REST_AT[s], REST_AT[s + 1]):
                            group(G1 + n, REST[n])

                if s < NJ:
                    scores(s)
                if s >= 1:
                    turn_and_value(s - 1, project)
                else:
                    project()

            pe.wait_ge(o_out, OUT0[NJ])
            for n in range(24):
                b, m = n // 8, n % 8
                if m == 0:
                    pe.wait_ge(big_in[b % 2], big_count(B_BR + b))
                if n == 16:
                    pe.wait_ge(od_ready, 1)
                    for hd in range(4):
                        if hd >= 2:
                            pe.wait_ge(oct_out, hd - 1)
                        for i in range(NT):
                            last = pe.transpose(bank[4 + hd % 2][:, i * P:(i + 1) * P],
                                                odn[:, i, P * hd:P * hd + P], ident)
                        last.then_inc(oct_done, 1)
                    pe.wait_ge(oct_out, 4)
                if n >= 4:
                    pe.wait_ge(branch_used, n - 3)
                src = (oa, ob, oc)[b]
                for j in range(4):
                    last = mm(bank[n % 4][:, :], wb[b][:, j, m * P:(m + 1) * P], src[:, j, :],
                              start=(j == 0), stop=(j == 3))
                last.then_inc(branch_done, 1)

            pe.wait_ge(merged_ready, 1)

            def att_out(i):
                for half in range(2):
                    if i == 0:
                        pe.wait_ge(big_in[(B_WO + half) % 2], big_count(B_WO + half))
                    if i >= 2:
                        pe.wait_ge(att_used, 2 * (i - 2) + half + 1)
                    for m in range(ND):
                        last = mm(bank[2 * (i % 2) + half][:, :], merged[:, m, i * P:(i + 1) * P],
                                  wo_h[half][:, m, :], start=(m == 0), stop=(m == ND - 1))
                    last.then_inc(att_done, 1)

            def x1_turn(i):
                pe.wait_ge(x1_ready, i + 1)
                for half in range(2):
                    if i == NT - 1:
                        pe.wait_ge(pt_out, half + 1)
                    elif i >= 1:
                        pe.wait_ge(x1t_out, 2 * (i - 1) + half + 1)
                    for k in range(4):
                        last = pe.transpose(bank[4 + half][:, k * P:(k + 1) * P],
                                            x1[:, i, (4 * half + k) * P:(4 * half + k + 1) * P], ident)
                    last.then_inc(x1t_done, 1)

            for i in range(NT):
                att_out(i)
                if i >= 1:
                    x1_turn(i - 1)
            pe.wait_ge(late_in, 16 * 7)
            for k in range(2):
                pe.wait_ge(x1t_out, 2 * (NT - 2) + k + 1)
                for i in range(NT):
                    last = pe.transpose(bank[4 + k][:, i * P:(i + 1) * P], pn[:, i, k * P:(k + 1) * P], ident)
                last.then_inc(pt_done, 1)

            def route(i):
                for k in range(ND):
                    last = mm(bank[6][:, NEXP * i:NEXP * i + NEXP], x1T[:, k, i * P:(i + 1) * P], rw[:, k, :],
                              start=(k == 0), stop=(k == ND - 1))
                return last

            for i in range(NT - 1):
                route(i)
            x1_turn(NT - 1)
            pe.wait_ge(x1t_out, 2 * NT)
            route(NT - 1).then_inc(route_done, 1)

            def places():
                pe.wait_ge(sel_ready, 1)
                for i in range(NT):
                    for a in range(i):
                        mm(bank[7][:, NEXP * i:NEXP * i + NEXP], ones, selb[:, a, :], start=(a == 0), stop=False)
                    mm(bank[7][:, NEXP * i:NEXP * i + NEXP], tri, selb[:, i, :], start=(i == 0), stop=True)
                for i in range(NT):
                    last = mm(bank[7][:, 256:320], ones, selb[:, i, :], start=(i == 0), stop=(i == NT - 1))
                last.then_inc(pos_done, 1)

            def index_of(r, e, n):
                pe.wait_ge(hot_ready, n + 1)
                for i in range(NT):
                    last = mm(bank[7][:, bass.ds(5 * e, 5)], onehot[:, r, i, :],
                              RW5[:, bass.ds(e, 1), i, :].rearrange("p e c -> p (e c)"),
                              start=(i == 0), stop=(i == NT - 1))
                last.then_inc(hot_used, 1)

            def indices(batch):
                if batch == 0:
                    pe.wait_ge(pos_used, 1)
                for n in range(HOT0[batch], HOT0[batch + 1]):
                    index_of(n % NHOT, n, n)

            pe.wait_ge(pt_out, 2)
            pe.wait_ge(ppw_in, 16)
            for n in range(2 * NT):
                half, i = n // NT, n % NT
                if n == NT:
                    places()
                if n >= 2:
                    pe.wait_ge(ple_used, n - 1)
                else:
                    pe.wait_ge(att_used, 2 * NT)
                if i == 0:
                    pe.wait_ge(big_in[(B_PG + half) % 2], big_count(B_PG + half))
                for k in range(ND):
                    mm(bank[n % 2][:, :], x1T[:, k, i * P:(i + 1) * P], pg_h[half][:, k, :],
                       start=(k == 0), stop=(k == ND - 1))
                for k in range(2):
                    last = mm(bank[2 + n % 2][:, :], pT[:, k, i * P:(i + 1) * P],
                              ppw[:, k, 512 * half:512 * half + 512], start=(k == 0), stop=(k == 1))
                last.then_inc(ple_done, 1)
                if n > NT:
                    indices(n - NT - 1)
            pe.wait_ge(ple_used, 2 * NT)

            def shared_up(i):
                if i == 0:
                    pe.wait_ge(big_in[B_SG % 2], big_count(B_SG))
                if i >= 2:
                    pe.wait_ge(sh_h, i - 1)
                for k in range(ND):
                    last = mm(bank[i % 2][:, :].rearrange("p (w f) -> p w f", w=2), x1T[:, k, i * P:(i + 1) * P],
                              sgu[:, :, k, :], start=(k == 0), stop=(k == ND - 1))
                last.then_inc(sh_gu, 1)

            shared_up(0)
            indices(NT - 1)
            for i in range(NT):
                if i + 1 < NT:
                    shared_up(i + 1)
                pe.wait_ge(sh_h, i + 1)
                if i >= 1:
                    pe.wait_ge(sh_hto, i)
                for k in range(NF):
                    last = pe.transpose(bank[4][:, k * P:(k + 1) * P], h[:, i % 2, k * P:(k + 1) * P], ident)
                last.then_inc(sh_ht, 1)
                pe.wait_ge(sh_hto, i + 1)
                if i == 0:
                    pe.wait_ge(big_in[B_SD % 2], big_count(B_SD))
                else:
                    pe.wait_ge(sh_used, i)
                for half in range(2):
                    for k in range(NF):
                        last = mm(bank[2 + half][:, :], hT[:, i % 2, k, :], sdn[:, k, 512 * half:512 * half + 512],
                                  start=(k == 0), stop=(k == NF - 1))
                last.then_inc(sh_y, 1)
                if i < 2:
                    indices(NT + 2 * i)
                    indices(NT + 2 * i + 1)
                if i == 1:
                    pe.wait_ge(hot_used, NEXP)
                    pe.sem_inc(idx_done, 1)
            pe.wait_ge(sh_used, NT)

            def index_pass(b):
                pe.wait_ge(idx_used, b)
                with pe.Fori(0, NEXP // 4) as it:
                    for r in range(4):
                        index_of(r, 4 * it + r, turn(b, it, r))
                pe.wait_ge(hot_used, NEXP * (b + 1))
                pe.sem_inc(idx_done, 1)

            def rows_turn(b, it, r):
                n = turn(b, it, r)
                pe.wait_ge(gathered[r], 16 * (NEXP // NR * b + it + 1))
                for half in range(2):
                    if not (isinstance(n, int) and n < 1):
                        pe.wait_ge(xgt_out, 2 * n - 1 + half)
                    for k in range(4):
                        kk = 4 * half + k
                        last = pe.transpose(bank[half][:, k * P:(k + 1) * P], xg[:, r, kk:D:ND], ident)
                    last.then_inc(xgt_done, 1)

            def up(b, it, r, ks_):
                n = turn(b, it, r)
                gu, _ = eslot(r)
                if ks_[0] == 0:
                    pe.wait_ge(xgt_out, 2 * n + 2)
                    pe.wait_ge(wgu_in[r], 32 * (NEXP // NR * b + it + 1))
                    if not (isinstance(n, int) and n < 2):
                        pe.wait_ge(h_ready, n - 1)
                for k in ks_:
                    last = mm(bank[2 + r % 2][:, :].rearrange("p (w f) -> p w f", w=2), xgT[:, r % 2, k, :],
                              gu[:, :, k, :], start=(k == 0), stop=(k == ND - 1))
                if ks_[-1] == ND - 1:
                    last.then_inc(gu_done, 1)

            def hidden_turn(b, it, r):
                n = turn(b, it, r)
                pe.wait_ge(h_ready, n + 1)
                if not (isinstance(n, int) and n < 1):
                    pe.wait_ge(ht_out, n)
                for k in range(NF):
                    last = pe.transpose(bank[4][:, k * P:(k + 1) * P], h[:, r % 2, k:F:NF], ident)
                last.then_inc(ht_done, 1)

            def down(b, it, r):
                n = turn(b, it, r)
                _, dn = eslot(r)
                pe.wait_ge(ht_out, n + 1)
                pe.wait_ge(wd_in[r], 16 * (NEXP // NR * b + it + 1))
                if not (isinstance(n, int) and n < 1):
                    pe.wait_ge(y_out, 2 * n)
                for half in range(2):
                    for k in range(NF):
                        last = mm(bank[5 + half][:, :], hT[:, r % 2, k, :], dn[:, k, 512 * half:512 * half + 512],
                                  start=(k == 0), stop=(k == NF - 1))
                last.then_inc(y_done, 1)

            def expert_products(b):
                if b:
                    index_pass(b)
                rows_turn(b, 0, 0)

                def step(it, r, before, after=True):
                    up(b, it, r, range(0, 4))
                    if before is not None:
                        hidden_turn(b, *before)
                    up(b, it, r, range(4, ND))
                    if after:
                        rows_turn(b, it + (r + 1) // NR, (r + 1) % NR)
                    if before is not None:
                        down(b, *before)

                for r in range(NR):
                    step(0, r, (0, r - 1) if r else None)
                last = NEXP // NR - 1
                with pe.Fori(1, last) as it:
                    for r in range(NR):
                        step(it, r, (it, r - 1) if r else (it - 1, NR - 1))
                for r in range(NR):
                    step(last, r, (last, r - 1) if r else (last - 1, NR - 1), after=r < NR - 1)
                hidden_turn(b, last, NR - 1)
                down(b, last, NR - 1)

            expert_products(0)
            pe.wait_ge(cnt_ready, 1)
            most = pe.value_load(cnt[0:1, 0:1], min_val=0, max_val=T)
            with pe.If(most > CAP):
                expert_products(1)
                with pe.If(most > 2 * CAP):
                    expert_products(2)
                    with pe.If(most > 3 * CAP):
                        expert_products(3)
                        pe.nop()
                    pe.nop()
                pe.nop()


_INS = ["x", "p", "w_in", "nsa_pe_k", "nsa_w1_k", "nsa_w2_k", "nsa_pe_v", "nsa_w1_v", "nsa_w2_v", "swa_sinks",
        "diff_lq1", "diff_lk1", "diff_lq2", "diff_lk2", "diff_norm_g", "w_branch_a", "w_branch_b", "w_branch_c",
        "w_out", "ln1_g", "ln1_b", "router_w", "router_bias", "exp_w_gate", "exp_w_up", "exp_w_down",
        "sh_w_gate", "sh_w_up", "sh_w_down", "ple_w_proj", "ple_w_gate", "ln2_g", "ln2_b"]


def kernel(**inputs):
    import numpy as _np
    import concourse.bacc as _bacc
    from concourse import mybir as _mybir
    from concourse.bass_utils import run_bass_kernel_spmd as _run

    nc = _bacc.Bacc("TRN2", target_bir_lowering=False, num_devices=1)
    arrays, aps = {}, {}
    for name in _INS:
        a = _np.ascontiguousarray(inputs[name])
        arrays[f"in_{name}_dram"] = a
        aps[name] = nc.dram_tensor(f"in_{name}_dram", a.shape, _mybir.dt.from_np(a.dtype), kind="ExternalInput").ap()
    out = nc.dram_tensor("out_0_dram", (1, T, D), F32, kind="ExternalOutput").ap()
    build(nc, aps, out)
    r = _run(nc, [arrays], core_ids=[0])
    return r.results[0]["out_0_dram"]
```

```python
import math

import numpy as np

import concourse.bass as bass
from concourse import mybir
from contextlib import ExitStack

F32 = mybir.dt.float32
F32R = mybir.dt.float32r
BF16 = mybir.dt.bfloat16
I32 = mybir.dt.int32
U32 = mybir.dt.uint32
ALU = mybir.AluOpType
ACT = mybir.ActivationFunctionType
AXX = mybir.AxisListType.X

P = 128
T, D = 512, 1024
NT, ND = T // P, D // P
DH = 64
SCALE = DH ** -0.5
NEXP, TOPK, NGRP, TOPG = 64, 8, 8, 4
GSZ = NEXP // NGRP
F = 256
NF = F // P
ROUTED_SCALE = 2.5
ALPHA = 2 ** 0.25
EPS = 1e-5
LAMBDA_INIT = 0.8 - 0.6 * math.exp(0.0)
NBLK = T // 64
HUGE = 3e32
CAP = 112
YROWS = TOPK * T

C_QA, C_KC, C_VC, C_KS, C_VS, C_KW, C_VW, C_GA = 0, 512, 640, 768, 896, 1024, 1152, 1280
C_QB, C_KB, C_VB, C_QC, C_KD, C_VD, C_GM = 1304, 1816, 1944, 2072, 2584, 3096, 3608
IN_CHUNKS_FIRST = [[(C_QA, C_QA + 256)], [(C_QA + 256, C_KC)], [(C_KC, C_KS)],
                   [(C_KS, C_VS), (C_KW, C_VW)], [(C_VS, C_KW), (C_VW, C_QB)]]
IN_CHUNKS_REST = [[(c, c + 256)] for c in range(C_QB, 6680, 256)]
NGATE0 = 9
IN_CHUNKS_REST = IN_CHUNKS_REST[:NGATE0] + IN_CHUNKS_REST[NGATE0 + 4:] + IN_CHUNKS_REST[NGATE0:NGATE0 + 4]
NW1 = 4
IN_CHUNKS = IN_CHUNKS_FIRST + IN_CHUNKS_REST
REST0 = len(IN_CHUNKS_FIRST)
NSLOT, SLOT = 3, 2240
BIG = 2 * SLOT

JOBS = [(kind, g, i) for i in range(NT) for g in range(2) for kind in ("slc", "win", "cmp")]
JOBS += [("swa", g, i) for i in range(NT) for g in range(2)]
JOBS += [("dif", g, i) for i in range(NT) for g in range(2)]
NJ = len(JOBS)


def keys_of(kind, i):
    if kind == "cmp":
        return 0, NBLK
    lo = max(0, i - 1) if kind == "swa" else 0
    return lo, (i + 1 - lo) * P


def blocks_of(kind, i):
    return 1 if kind == "cmp" else keys_of(kind, i)[1] // P


def turns_of(kind, i):
    return 2 if kind == "dif" else blocks_of(kind, i)


TURN0 = np.cumsum([0] + [turns_of(k, i) for k, g, i in JOBS]).tolist()
CLOSES = [k != "slc" and k != "win" for k, g, i in JOBS]
OUT0 = np.cumsum([0] + [int(c) for c in CLOSES]).tolist()


def build(nc, A, out):
    ctx = ExitStack()
    with ctx:
        def sem(name):
            return ctx.enter_context(nc.semaphore(name))

        ARENA = 52000
        small = ctx.enter_context(nc.sbuf_tensor("small", [P, 1024], F32))
        small2 = ctx.enter_context(nc.sbuf_tensor("small2", [P, 128], F32))
        places = {}

        def place(off, n, dtype):
            assert off + n <= ARENA
            key = (off, n, dtype == F32R)
            if key not in places:
                name = f"{'halves' if dtype == F32R else 'floats'}_{off}_{n}"
                if off == 0:
                    with nc.sbuf_tensor(name, [P, n], dtype) as places[key]:
                        pass
                else:
                    with nc.sbuf_tensor(f"before_{name}", [P, off], F32):
                        with nc.sbuf_tensor(name, [P, n], dtype) as places[key]:
                            pass
            return places[key][:, :]

        def at(off, n):
            return place(off, n, F32)

        def half_at(off, n):
            return place(off, n, F32R)

        W = at(0, 4 * SLOT)
        upper_at = [NSLOT * SLOT, 37888]
        qa = at(8960, 2048).rearrange("p (j t) -> p j t", t=T)
        qb = at(11008, 2048).rearrange("p (j t) -> p j t", t=T)
        qc = at(13056, 2048).rearrange("p (j t) -> p j t", t=T)
        kd = at(15104, 2048).rearrange("p (j t) -> p j t", t=T)
        vd = at(17152, 2048).rearrange("p (i c) -> p i c", i=NT)
        ks, kw = at(19200, 512), at(19712, 512)
        vs = at(20224, 512).rearrange("p (i c) -> p i c", i=NT)
        vw = at(20736, 512).rearrange("p (i c) -> p i c", i=NT)
        kb = at(21248, 512)
        vb = at(21760, 512).rearrange("p (i c) -> p i c", i=NT)
        KV = at(22272, 1024).rearrange("p (w l c) -> p w l c", w=2, c=16)
        hcx, hcu, hct = at(23296, 512), at(23808, 512), at(24320, 256)
        xh = half_at(24576, 4096).rearrange("p (k t) -> p k t", t=T)
        xl = half_at(28672, 4096).rearrange("p (k t) -> p k t", t=T)
        gates_kept = at(32768, 4096).rearrange("p (m t) -> p m t", t=T)
        gates_ring = at(36864, 1024).rearrange("p (r t) -> p r t", t=T)
        gates_back = at(24576, 8192).rearrange("p (m t) -> p m t", t=T)
        S = at(40960, 4096).rearrange("p (u n) -> p u n", n=T)
        PT = at(45056, 2048).rearrange("p (u n) -> p u n", n=T)
        oa = at(47104, 2048).rearrange("p (j t) -> p j t", t=T)
        ob = at(49152, 2048).rearrange("p (j t) -> p j t", t=T)
        dist = at(51200, T)
        distw = at(51712, 2 * P)
        distc = at(51968, NT * NBLK).rearrange("p (i n) -> p i n", i=NT)
        x0 = at(32768, 4096).rearrange("p (i d) -> p i d", i=NT)
        odn = at(19200, 2048).rearrange("p (i c) -> p i c", i=NT)
        merged = at(11008, 4096).rearrange("p (m t) -> p m t", t=T)
        xr = at(15104, 4096).rearrange("p (i d) -> p i d", i=NT)
        x1 = at(28672, 4096).rearrange("p (i d) -> p i d", i=NT)
        acc = at(32768, 4096).rearrange("p (i d) -> p i d", i=NT)
        ob_halves = [half_at(o, 2048).rearrange("p (j t) -> p j t", t=T) for o in (22272, 49152)]
        oc_halves = [half_at(o, 2048).rearrange("p (j t) -> p j t", t=T) for o in (8960, 45056)]
        merged_l = half_at(11008, 4096).rearrange("p (m t) -> p m t", t=T)
        merged_h = half_at(47104, 4096).rearrange("p (m t) -> p m t", t=T)
        ln1 = at(8960, 2048).rearrange("p (w d) -> p w d", w=2)
        ln2 = at(38912, 2048).rearrange("p (w d) -> p w d", w=2)
        x1T = at(24576, 4096).rearrange("p (k t) -> p k t", t=T)
        z = at(40960, 2048).rearrange("p (r d) -> p r d", r=2)
        mtmp = at(43008, 1024).rearrange("p (r t) -> p r t", r=2)
        ppw = at(45056, 2048).rearrange("p (k d) -> p k d", k=2)
        pn = at(19200, 1024).rearrange("p (i c) -> p i c", i=NT)
        pT = at(49152, 1024).rearrange("p (k t) -> p k t", k=2)
        rw = at(44032, 512).rearrange("p (k e) -> p k e", k=ND)
        NR = 4
        gu_at, gu_upper_at, down_at = [12288, 16384, 0, 4096], [20480, 24576], [10240, 8192]

        def gu_raw(r):
            return at(gu_at[r], 2 * ND * F)

        def gu_lower(r):
            return half_at(gu_at[r], 2 * ND * F)

        def gu_upper(r):
            return half_at(gu_upper_at[r % 2], 2 * ND * F)

        def gate_up(v):
            return v.rearrange("p (w k f) -> p w k f", w=2, k=ND)

        def down_w(r):
            return at(down_at[r % 2], NF * D).rearrange("p (k d) -> p k d", k=NF)

        xg = at(40960, 4096).rearrange("p (r d) -> p r d", r=NR)
        xgh = half_at(49152, 2048).rearrange("p (r k s) -> p r k s", r=2, k=ND)
        xgl = half_at(36864, 2048).rearrange("p (r k s) -> p r k s", r=2, k=ND)
        y = at(30720, 2048).rearrange("p (r d) -> p r d", r=2)
        sg = at(48128, 512).rearrange("p (r f) -> p r f", r=2)
        h = at(48640, 512).rearrange("p (r f) -> p r f", r=2)
        NHOT = 16
        HOT0 = [0, 10, 20, 30, 40, 46, 52, 58, NEXP]
        onehot = at(28672, 4096).bitcast(BF16).rearrange("p (r i s) -> p r i s", r=NHOT, i=NT)
        ple_sg = at(43008, 1024).rearrange("p (r t) -> p r t", r=2)
        RW5 = at(47104, 640).bitcast(BF16).rearrange("p (e i c) -> p e i c", e=NEXP, c=5)
        posE = at(47744, 256).rearrange("p (e i) -> p e i", i=NT)
        hT = at(51200, 512).rearrange("p (r k s) -> p r k s", r=2, k=NF)
        dest = at(51712, 32).bitcast(U32).rearrange("p (i k) -> p i k", i=NT)
        def last_rows(n):
            return at(n * D, D) if n < NT * TOPK - 4 else at(40960 + (n - NT * TOPK + 4) * D, D)


        def rt(n, w=256):
            return at(8960 + 256 * n, w)

        sc, bi, m1, rep, sel, ws = [rt(n).rearrange("p (i e) -> p i e", i=NT) for n in range(6)]
        g8 = rt(6).rearrange("p (i g c) -> p i g c", i=NT, g=NGRP)
        selb = at(8960 + 1792, 128).bitcast(BF16).rearrange("p (i e) -> p i e", i=NT)
        gs = at(10880, 48).rearrange("p (i g) -> p i g", i=NT)
        gr = at(10928, 48).rearrange("p (i g) -> p i g", i=NT)
        gt8 = at(10976, 32).rearrange("p (i g) -> p i g", i=NT)
        gmask = at(11008, 32).rearrange("p (i g) -> p i g", i=NT)
        gneg = at(11040, 32).rearrange("p (i g) -> p i g", i=NT)
        v8 = at(11072, 32).rearrange("p (i g) -> p i g", i=NT)
        dd = at(11136, 256).rearrange("p (i e) -> p i e", i=NT)
        d8 = at(11392, 32).rearrange("p (i g) -> p i g", i=NT)
        wr1 = at(11424, 256).rearrange("p (i e) -> p i e", i=NT)
        wsum = at(11680, 4)
        wrec = at(11684, 4)
        cmax = at(11688, 1)
        before = [at(11968, 64), at(12032, 64)]
        minus_p = at(12096, 1)
        pos1 = at(11712, 256).rearrange("p (i e) -> p i e", i=NT)

        def sm(o, n):
            return small[:, o:o + n]

        ident = sm(0, 128)
        iota_s = sm(128, 64).bitcast(BF16)
        tri = sm(192, 64).bitcast(BF16)
        ones = sm(256, 64).bitcast(BF16)
        slot_row = sm(320, 64)
        negm = sm(384, 8).rearrange("p (r j) -> p r j", r=2)
        esum = sm(392, 8).rearrange("p (r j) -> p r j", r=2)
        fac = sm(400, 8).rearrange("p (r j) -> p r j", r=2)
        sinks = sm(408, 8)
        lamv = sm(416, 4)
        ga = sm(420, 96).rearrange("p (i c) -> p i c", i=NT)
        kcmp = sm(516, 8)
        pe2 = sm(524, 64).rearrange("p (w l) -> p w l", w=2)
        gcol = sm(588, 1)
        ssq, rms = sm(592, 16), sm(608, 16)
        stats = sm(624, 12).rearrange("p (c s) -> p c s", c=2)
        mv, var_e, rstd = sm(636, 2), sm(638, 1), sm(639, 1)
        vcmp = sm(640, 128)
        hcT = sm(768, 64).rearrange("p (f c) -> p f c", f=4)
        IDX = sm(832, 64)
        WG = sm(896, 64)
        cnt = sm(960, 1).bitcast(I32)
        lamt = sm(961, 4)
        idxr = sm(965, 4).bitcast(U32)
        idyr = sm(969, 4).bitcast(U32)
        wgr = sm(973, 4)
        rbias = small2[:, 64:128]
        IDY = small2[:, 0:64]
        w2 = hct
        pe_raw = at(45056, 256).rearrange("p (w l) -> p w l", w=2)
        lq = at(45312, 256).rearrange("p (w d) -> p w d", w=4)

        bank = [ctx.enter_context(nc.psum_tensor(f"bank{n}", [P, 512], F32)) for n in range(8)]
        x1_dram = nc.dram_tensor("x1_rows", (T, D), F32, kind="Internal").ap()
        gates_dram = nc.dram_tensor("gate_rows", (2 * D, T), F32, kind="Internal").ap()
        y_dram = nc.dram_tensor("y_rows", (YROWS, D), F32, kind="Internal").ap()

        x_in = [sem(f"x_in{i}") for i in range(NT)]
        const_in = sem("const_in")
        w_in = [sem(f"w_in{s}") for s in range(NSLOT)]
        w1_in = [sem(f"w1_in{w}") for w in range(2)]
        x_low, upper_ready, lower_ready = sem("x_low"), sem("upper_ready"), sem("lower_ready")
        spilled = [sem(f"spilled{s}") for s in range(2)]
        gates_in = [sem(f"gates_in{s}") for s in range(4)]
        pool_const = sem("pool_const")
        group_done = sem("group_done")
        group_out = sem("group_out")
        embed_done, embed_out, pe_added = sem("embed_done"), sem("embed_out"), sem("pe_added")
        chain = sem("vector_chain")
        hc_done, hc_copied, hc_cubic, hc_tanh, hc_ready = (sem(n) for n in (
            "hc_done", "hc_copied", "hc_cubic", "hc_tanh", "hc_ready"))
        hct_done, hct_out, cmp_done, cmp_out = (sem(n) for n in (
            "hct_done", "hct_out", "cmp_done", "cmp_out"))
        lam_dot, lam_exp = sem("lam_dot"), sem("lam_exp")
        scored, biased, max_ready, exped, probs = (sem(n) for n in (
            "scored", "biased", "max_ready", "exped", "probs"))
        turned, turned_out, pv_done, o_out = (sem(n) for n in (
            "turned", "turned_out", "pv_done", "o_out"))
        sq_done, rms_in, rms_root, od_ready, oct_done, oct_out = (sem(n) for n in (
            "sq_done", "rms_in", "rms_root", "od_ready", "oct_done", "oct_out"))
        big_in = [sem(f"big_in{s}") for s in range(2)]
        sig_done, branch_done, branch_used, merged_ready = (sem(n) for n in (
            "sig_done", "branch_done", "branch_used", "merged_ready"))
        xr_in, late_in, ppw_in = sem("xr_in"), sem("late_in"), sem("ppw_in")
        sgu_in, sdn_in, ln2_in = sem("sgu_in"), sem("sdn_in"), sem("ln2_in")
        att_done, att_used, var_ready, root_ready, x1_ready = (sem(n) for n in (
            "att_done", "att_used", "var_ready", "root_ready", "x1_ready"))
        residual_in = sem("residual_in")
        wb_upper, wb_lower, ob_upper, ob_lower, oc_lower = (sem(n) for n in (
            "wb_upper", "wb_lower", "ob_upper", "ob_lower", "oc_lower"))
        wo1_in, wo_upper, wo_lower, merged_upper, merged_lower = (sem(n) for n in (
            "wo1_in", "wo_upper", "wo_lower", "merged_upper", "merged_lower"))
        x1t_done, x1t_out, x1_stored = sem("x1t_done"), sem("x1t_out"), sem("x1_stored")
        pt_done, pt_out = sem("pt_done"), sem("pt_out")
        route_done, route_sig, sel_ready, pos_done, pos_used = (sem(n) for n in (
            "route_done", "route_sig", "sel_ready", "pos_done", "pos_used"))
        ple_done, ple_sig, ple_used = sem("ple_done"), sem("ple_sig"), sem("ple_used")
        sh_gu, sh_sig, sh_h, sh_ht, sh_hto, sh_y, sh_used = (sem(n) for n in (
            "sh_gu", "sh_sig", "sh_h", "sh_ht", "sh_hto", "sh_y", "sh_used"))
        index_chain = sem("index_chain")
        cnt_ready, hot_ready, hot_used, idx_done, idx_used = (sem(n) for n in (
            "cnt_ready", "hot_ready", "hot_used", "idx_done", "idx_used"))
        xg_zero = sem("xg_zero")
        pool_turn = sem("pool_turn")
        wgu_in = [sem(f"wgu_in{s}") for s in range(NR)]
        wd_in = [sem(f"wd_in{s}") for s in range(2)]
        e_upper, e_lower, xgl_out = sem("e_upper"), sem("e_lower"), sem("xgl_out")
        col_ready = sem("col_ready")
        ycol_ready = sem("ycol_ready")
        gathered = [sem(f"gathered{s}") for s in range(NR)]
        scattered = [sem(f"scattered{s}") for s in range(2)]
        xgt_done, xgt_out, gu_done, e_sig, h_ready, ht_done, ht_out, y_done, y_out = (
            sem(n) for n in ("xgt_done", "xgt_out", "gu_done", "e_sig", "h_ready", "ht_done",
                             "ht_out", "y_done", "y_out"))
        NROW = 12
        PE_ROWS = 5
        rows_summed, sums_used = sem("rows_summed"), sem("sums_used")
        row_in = [sem(f"row_in{s}") for s in range(NROW)]
        out_ready, stored = sem("out_ready"), sem("stored")

        w_rows = A["w_in"][0].rearrange("(k p) c -> p k c", p=P)
        w1k = A["nsa_w1_k"][0].rearrange("(a p) f -> p a f", p=P)
        w1v = A["nsa_w1_v"][0].rearrange("(a p) f -> p a f", p=P)

        def slot_of(n):
            return n % NSLOT

        def chunk(n, width=256):
            o = slot_of(n) * SLOT
            return W[:, o:o + ND * width].rearrange("p (k c) -> p k c", k=ND)

        def upper(n, width=256):
            o = upper_at[n % 2]
            return half_at(o, ND * width).rearrange("p (k c) -> p k c", k=ND)

        def lower(n, width=256):
            return half_at(slot_of(n) * SLOT, ND * width).rearrange("p (k c) -> p k c", k=ND)

        def w_count(n):
            return 16 * sum(len(IN_CHUNKS[m]) for m in range(n % NSLOT, n + 1, NSLOT))

        w1_at = [11008, 13056, 15104, 17152, 40960, 43008, 47104, 49152]

        def w1_chunk(w, c):
            return at(w1_at[NW1 * w + c], 2048).rearrange("p (a f) -> p a f", a=ND)

        def query_groups(n, dst):
            return [("Q", n + j // 2, (j % 2) * P, (dst, j), SCALE, j % 2) for j in range(4)]

        FIRST = query_groups(0, qa)
        FIRST += [("T", 2, 0, "kc", 1.0, 0), ("T", 2, P, "vc", 1.0, 1)]
        COMPRESS = len(FIRST)
        FIRST += [("T", 3, 0, ks, 1.0, 0), ("T", 3, P, kw, 1.0, 1)]
        FIRST += [("V", 4, i, None, 1.0, i == NT - 1) for i in range(NT)]
        REST = query_groups(REST0, qb)
        REST += [("T", REST0 + 2, 0, kb, 1.0, 0), ("N", REST0 + 2, P, vb, 1.0, 1)]
        for base, dst, scale in ((3, qc, SCALE), (5, kd, 1.0)):
            REST += [("T", REST0 + base + j // 2, (j % 2) * P, dst[:, j, :], scale, j % 2)
                     for j in range(4)]
        for c in range(2):
            REST += [("N2", REST0 + 7 + c, 2 * i, vd[:, 2 * i:2 * i + 2, 256 * c:256 * c + 256], 1.0, i)
                     for i in range(2)]
        GATES = len(REST)
        SPILL = 2 * ND
        REST += [("T", REST0 + NGATE0 + q // 2, (q % 2) * P,
                  gates_ring[:, q % 2, :] if q < SPILL else gates_kept[:, q - SPILL, :], 1.0, q % 2)
                 for q in range(3 * ND)]
        NCHUNK = len(IN_CHUNKS)

        def gates(n):
            return gates_kept[:, n, :] if n < ND else gates_back[:, n - ND, :]

        NXG = 2 * NT
        G0, G1 = NXG, NXG + len(FIRST)
        FREED = {desc[1]: G0 + n + 1 for n, desc in enumerate(FIRST + REST)}
        N_STEPS = NJ
        PER_STEP = [2 if s in (3, 9) else 1 for s in range(N_STEPS)]
        assert sum(PER_STEP) == len(REST)
        REST_AT = np.cumsum([0] + PER_STEP).tolist()

        def group_bank(n):
            return bank[n % 4] if n < G0 else bank[6 + n % 2] if n < G1 else bank[7]

        def need_group(kind):
            return {"slc": G1, "win": G1, "cmp": G1, "swa": G1 + 6, "dif": G1 + 18}[kind]

        def width_of(n):
            return sum(b - a for a, b in IN_CHUNKS[n])

        def unit_operands(kind, g, i, j):
            lo, n = keys_of(kind, i)
            tq = slice(i * P, (i + 1) * P)
            if kind == "dif":
                r, hd = j % 2, 2 * g + j // 2
                rows = slice(DH * r, DH * r + DH)
                return qc[rows, hd, tq], kd[rows, hd, 0:n]
            rows = slice(DH * g, DH * g + DH)
            q = (qb if kind == "swa" else qa)[rows, j, tq]
            k = {"slc": ks, "win": kw, "swa": kb, "cmp": kcmp}[kind]
            return q, k[rows, lo * P:lo * P + n]

        def slope_of(kind, g, j):
            return 2.0 ** (-2.0 * (2 * g + j // 2 + 1)) if kind == "dif" else 2.0 ** -(4 * g + j + 1)

        def distances(kind, i, n):
            if kind == "cmp":
                return distc[:, i, :]
            if kind == "swa":
                return distw[:, 2 * P - n:2 * P]
            return dist[:, T - n:T]

        big0 = W[:, 0:4096]
        big1 = W[:, BIG:BIG + 4096]
        bigs = [big0, big1]
        wb = [bigs[b % 2].rearrange("p (j d) -> p j d", j=4) for b in range(3)]
        wb_halves = [[half_at(o, 4096).rearrange("p (j d) -> p j d", j=4) for o in offs]
                     for offs in ((36864, BIG), (15104, 0))]
        wo_at = [(BIG, 32768), (36864, 20480)]
        wo_raw, wo_l, wo_h = ([kind(offs[which], 4096).rearrange("p (k d) -> p k d", k=ND) for offs in wo_at]
                              for kind, which in ((at, 0), (half_at, 0), (half_at, 1)))
        pg_h = [bigs[0].rearrange("p (k d) -> p k d", k=ND), bigs[1].rearrange("p (k d) -> p k d", k=ND)]
        sgu = at(36864, 4096).rearrange("p (w k f) -> p w k f", w=2, k=ND)
        sdn = at(45056, 2048).rearrange("p (k d) -> p k d", k=NF)
        B_BR, B_WO, B_PG = 0, 3, 4
        BIG_DMAS = [2, 2, 1, 1, 1, 1, 1, 2, 1]

        def big_count(n):
            return 16 * sum(BIG_DMAS[m] for m in range(n % 2, n + 1, 2))

        def second(b, it, r):
            return NEXP // 2 * b + 2 * it + r // 2

        def turn(b, it, r):
            return NEXP * b + NR * it + r

        block = ctx.enter_context(nc.Block())

        @block.sync
        def _(sp):
            def load_chunk(n):
                if n >= NSLOT:
                    sp.wait_ge(group_done, FREED[n - NSLOT])
                c0 = 0
                for a, b in IN_CHUNKS[n]:
                    sp.dma_start(chunk(n, width_of(n))[:, :, c0:c0 + b - a],
                                 w_rows[:, :, a:b]).then_inc(w_in[slot_of(n)], 16)
                    c0 += b - a

            load_chunk(0)
            for i in range(NT):
                sp.dma_start(x0[:, i, :], A["x"][0, i * P:(i + 1) * P, :]).then_inc(x_in[i], 16)
            for n in range(1, NSLOT):
                load_chunk(n)
            for w, src in enumerate((w1k, w1v)):
                for c in range(NW1):
                    sp.dma_start(w1_chunk(w, c), src[:, ND * c:ND * c + ND, :]).then_inc(w1_in[w], 16)
                load_chunk(NSLOT + w)
            for n in range(NSLOT + 2, NCHUNK):
                load_chunk(n)

            BIG_FREED = [(branch_done, 8), (branch_done, 16), (branch_done, 24), (att_done, 2 * NT)]

            def big_load(n, parts):
                if n < 2:
                    sp.wait_ge(group_done, G1 + len(REST))
                else:
                    sp.wait_ge(*BIG_FREED[n - 2])
                for dst, src in parts:
                    sp.dma_start(dst, src).then_inc(big_in[n % 2], 16)

            wo = A["w_out"][0].rearrange("(k p) d -> p k d", p=P)
            for b, name in enumerate(("w_branch_a", "w_branch_b", "w_branch_c")):
                src = A[name][0]
                if b < 2:
                    src = src.rearrange("(two j d) n -> two d j n", two=2, j=4)
                    parts = [(wb[b][DH * s:DH * s + DH], src[s]) for s in range(2)]
                else:
                    parts = [(wb[b], src.rearrange("(j p) n -> p j n", p=P))]
                big_load(B_BR + b, parts)
                if b == 1:
                    for r in range(2):
                        sp.wait_ge(spilled[r], 16 * (SPILL // 2))
                    for q in range(4):
                        sp.dma_start(gates_back[:, 4 * q:4 * q + 4, :], gates_dram[
                            4 * q * P:4 * (q + 1) * P, :].rearrange("(m p) t -> p m t", p=P)).then_inc(gates_in[q], 16)
            big_load(B_WO, [(wo_raw[0], wo[:, :, 0:512])])
            sp.dma_start(wo_raw[1], wo[:, :, 512:1024]).then_inc(wo1_in, 16)
            sp.wait_ge(branch_done, 24)
            sp.dma_start(xr, A["x"][0].rearrange("(i p) d -> p i d", p=P)).then_inc(xr_in, 16)
            for n, name in enumerate(("ln1_g", "ln1_b")):
                sp.dma_start(ln1[:, n, :], A[name][0:1, :].to_broadcast([P, D])).then_inc(late_in, 16)
            sp.dma_start(pn, A["p"][0, 0].rearrange("(i p) c -> p i c", p=P)).then_inc(late_in, 16)
            sp.dma_start(rw, A["router_w"][0].rearrange("(k p) e -> p k e", p=P)).then_inc(late_in, 16)
            sp.dma_start(rbias, A["router_bias"][0:1, :].to_broadcast([P, NEXP])).then_inc(late_in, 16)
            sp.dma_start(ppw, A["ple_w_proj"][0].rearrange("(k p) d -> p k d", p=P)).then_inc(ppw_in, 16)
            pg = A["ple_w_gate"][0].rearrange("(k p) d -> p k d", p=P)
            big_load(B_PG, [(pg_h[0], pg[:, :, 0:512])])
            big_load(B_PG + 1, [(pg_h[1], pg[:, :, 512:1024])])
            sp.wait_ge(x1_ready, NT)
            for w, name in enumerate(("sh_w_gate", "sh_w_up")):
                sp.dma_start(sgu[:, w], A[name][0].rearrange("(k p) f -> p k f", p=P)).then_inc(sgu_in, 16)

            def load_gate_up(b, it, r):
                n = turn(b, it, r)
                e = NR * it + r
                if not (isinstance(n, int) and n < NR):
                    sp.wait_ge(gu_done, n - NR + 1)
                for w, name in enumerate(("exp_w_gate", "exp_w_up")):
                    sp.dma_start(gate_up(gu_raw(r))[:, w], A[name][0, bass.ds(e, 1)].rearrange(
                        "e (p k) f -> p (e k) f", p=P)).then_inc(wgu_in[r], 16)

            def load_down(b, it, r):
                n = turn(b, it, r)
                e = NR * it + r
                if not (isinstance(n, int) and n < 2):
                    sp.wait_ge(y_done, n - 1)
                sp.dma_start(down_w(r), A["exp_w_down"][0, bass.ds(e, 1)].rearrange(
                    "e (p k) d -> p (e k) d", p=P)).then_inc(wd_in[r % 2], 16)

            sp.wait_ge(route_done, 1)
            load_gate_up(0, 0, 0)
            load_gate_up(0, 0, 1)
            sp.wait_ge(cnt_ready, 1)
            load_down(0, 0, 0)
            sp.wait_ge(ple_done, NT)
            load_gate_up(0, 0, 2)
            sp.wait_ge(ple_done, 2 * NT)
            sp.dma_start(sdn, A["sh_w_down"][0].rearrange("(k p) d -> p k d", p=P)).then_inc(sdn_in, 16)
            load_down(0, 0, 1)
            load_gate_up(0, 0, 3)
            sp.wait_ge(sh_gu, NT)
            for n, name in enumerate(("ln2_g", "ln2_b")):
                sp.dma_start(ln2[:, n, :], A[name][0:1, :].to_broadcast([P, D])).then_inc(ln2_in, 16)

            def expert_loads(b):
                if b:
                    for r in range(NR):
                        load_gate_up(b, 0, r)
                for r in range(NR):
                    if b or r >= 2:
                        load_down(b, 0, r)
                    load_gate_up(b, 1, r)
                last = NEXP // NR - 1
                with sp.Fori(1, last) as it:
                    for r in range(NR):
                        load_down(b, it, r)
                        load_gate_up(b, it + 1, r)
                for r in range(NR):
                    load_down(b, last, r)

            expert_loads(0)
            sp.wait_ge(cnt_ready, 1)
            most = sp.value_load(cnt[0:1, 0:1], min_val=0, max_val=T)
            with sp.If(most > CAP):
                expert_loads(1)
                with sp.If(most > 2 * CAP):
                    expert_loads(2)
                    with sp.If(most > 3 * CAP):
                        expert_loads(3)
                        with sp.If(most > 4 * CAP):
                            expert_loads(4)
                            sp.nop()
                        sp.nop()
                    sp.nop()
                sp.nop()
            for i in range(NT):
                sp.wait_ge(out_ready, i + 1)
                sp.dma_start(out[0, i * P:(i + 1) * P, :], acc[:, i, :]).then_inc(stored, 16)
            sp.wait_ge(stored, 16 * NT)

        @block.gpsimd
        def _(pool):
            n_const = [0]

            def made(ins):
                n_const[0] += 1
                ins.then_inc(pool_const, 1)
                pool.wait_ge(pool_const, n_const[0])

            made(pool.memset(ident, 0.0))
            made(pool.affine_select(out=ident, in_=ident, compare_op=ALU.not_equal, fill=1.0, base=0,
                                    pattern=[[-1, P]], channel_multiplier=1))
            made(pool.memset(ones, 1.0))
            made(pool.affine_select(out=tri, in_=ones, compare_op=ALU.is_gt, fill=0.0, base=0,
                                    pattern=[[1, P]], channel_multiplier=-1))
            made(pool.iota(iota_s, pattern=[[1, P]], base=0, channel_multiplier=0,
                           allow_small_or_imprecise_dtypes=True))
            made(pool.iota(slot_row, pattern=[[0, NEXP]], base=0, channel_multiplier=1,
                           allow_small_or_imprecise_dtypes=True))
            made(pool.iota(dist, pattern=[[-1, T]], base=T - P, channel_multiplier=1,
                           allow_small_or_imprecise_dtypes=True))
            made(pool.affine_select(out=dist, in_=dist, compare_op=ALU.is_ge, fill=HUGE, base=T - P,
                                    pattern=[[-1, T]], channel_multiplier=1))
            made(pool.iota(distw, pattern=[[-1, 2 * P]], base=P, channel_multiplier=1,
                           allow_small_or_imprecise_dtypes=True))
            made(pool.affine_select(out=distw, in_=distw, compare_op=ALU.is_ge, fill=HUGE, base=P,
                                    pattern=[[-1, 2 * P]], channel_multiplier=1))
            made(pool.affine_select(out=distw, in_=distw, compare_op=ALU.is_gt, fill=HUGE, base=0,
                                    pattern=[[1, 2 * P]], channel_multiplier=-1))
            made(pool.iota(distc, pattern=[[P, NT], [-64, NBLK]], base=-63, channel_multiplier=1,
                           allow_small_or_imprecise_dtypes=True))
            made(pool.affine_select(out=distc, in_=distc, compare_op=ALU.is_ge, fill=HUGE, base=-63,
                                    pattern=[[P, NT], [-64, NBLK]], channel_multiplier=1))
            assert n_const[0] == 13
            for q in range(SPILL):
                pool.wait_ge(group_out, G1 + GATES + q + 1)
                pool.dma_start(gates_dram[q * P:(q + 1) * P, :], gates_ring[:, q % 2, :]).then_inc(spilled[q % 2], 16)
            for i in range(NT):
                pool.wait_ge(x1_ready, i + 1)
                pool.dma_start(x1_dram[i * P:(i + 1) * P, :], x1[:, i, :]).then_inc(x1_stored, 16)
            pool.wait_ge(pt_done, 2)
            pool.iota(RW5[:, :, :, 0], pattern=[[0, NEXP], [0, NT]], base=0, channel_multiplier=1,
                      allow_small_or_imprecise_dtypes=True)
            pool.iota(RW5[:, :, :, 1], pattern=[[0, NEXP], [P, NT]], base=-1024, channel_multiplier=0,
                      allow_small_or_imprecise_dtypes=True).then_inc(xg_zero, 1)
            pool.wait_ge(ple_used, 2 * NT)
            pool.memset(xg, 0.0).then_inc(xg_zero, 1)
            pool.wait_ge(xg_zero, 2)
            pool.wait_ge(x1_stored, 16 * NT)

            last_token = pool.to_reg(T - 1)
            last_row = pool.to_reg(YROWS - 1)

            def gather(b, it, r):
                n = turn(b, it, r)
                pool.wait_ge(col_ready, n + 1)
                if not (isinstance(n, int) and n < NR):
                    pool.wait_ge(xgt_done, 2 * (n - NR) + 2)
                pool.sem_inc(pool_turn, 1)
                pool.indirect_dma_start(
                    xg[0:CAP, r, :], None, x1_dram,
                    bass.IndirectOffsetOnAxis(ap=idxr[0:CAP, r:r + 1], axis=0),
                    bounds_check=last_token, oob_is_err=False).then_inc(gathered[r], 16)

            def scatter(b, it, r):
                n = turn(b, it, r)
                pool.wait_ge(y_out, 2 * n + 2)
                pool.sem_inc(pool_turn, 1)
                pool.indirect_dma_start(
                    y_dram, bass.IndirectOffsetOnAxis(ap=idyr[0:CAP, r:r + 1], axis=0),
                    y[0:CAP, r % 2, :], None,
                    bounds_check=last_row, oob_is_err=False).then_inc(scattered[r % 2], 16)

            def expert_rows(b):
                for r in range(NR):
                    gather(b, 0, r)
                last = NEXP // NR - 1
                with pool.Fori(0, last) as it:
                    for r in range(NR):
                        gather(b, it + 1, r)
                        scatter(b, it, r)
                for r in range(NR):
                    scatter(b, last, r)
                for s in range(2):
                    pool.wait_ge(scattered[s], 16 * (NEXP // 2) * (b + 1))

            expert_rows(0)
            pool.wait_ge(cnt_ready, 1)
            most = pool.value_load(cnt[0:1, 0:1], min_val=0, max_val=T)
            with pool.If(most > CAP):
                expert_rows(1)
                with pool.If(most > 2 * CAP):
                    expert_rows(2)
                    with pool.If(most > 3 * CAP):
                        expert_rows(3)
                        with pool.If(most > 4 * CAP):
                            expert_rows(4)
                            pool.nop()
                        pool.nop()
                    pool.nop()
                pool.nop()
            for i in range(NT):
                for k in range(TOPK):
                    n = i * TOPK + k
                    if n >= NROW:
                        pool.wait_ge(row_in[n % NROW], 16 * (n // NROW))
                    pool.indirect_dma_start(
                        last_rows(n), None, y_dram,
                        bass.IndirectOffsetOnAxis(ap=dest[:, i, k:k + 1], axis=0),
                        bounds_check=last_row, oob_is_err=False).then_inc(row_in[n % NROW], 16)

        @block.scalar
        def _(act):
            act.dma_start(pe_raw[0:32, 0, :], A["nsa_pe_k"][0].rearrange("(l two) d -> l (two d)", two=2)).then_inc(const_in, 16)
            act.dma_start(pe_raw[0:32, 1, :], A["nsa_pe_v"][0].rearrange("(l two) d -> l (two d)", two=2)).then_inc(const_in, 16)
            act.dma_start(w2[:, 0:128].rearrange("p (f d) -> p f d", f=2),
                          A["nsa_w2_k"][0].rearrange("(f p) d -> p f d", p=P)).then_inc(const_in, 16)
            act.dma_start(w2[:, 128:256].rearrange("p (f d) -> p f d", f=2),
                          A["nsa_w2_v"][0].rearrange("(f p) d -> p f d", p=P)).then_inc(const_in, 16)
            act.dma_start(sinks, A["swa_sinks"][0:1, :].to_broadcast([P, 8])).then_inc(const_in, 16)
            for n, name in enumerate(("diff_lq1", "diff_lk1", "diff_lq2", "diff_lk2")):
                act.dma_start(lq[:, n, :], A[name][0:1, :].to_broadcast([P, DH])).then_inc(const_in, 16)
            with nc.allow_non_contiguous_dma(reason="a column of 128 gains"):
                act.dma_start(gcol, A["diff_norm_g"][0].rearrange("(p o) -> p o", o=1)).then_inc(const_in, 16)
            def split_upper(n):
                act.wait_ge(w_in[slot_of(n)], w_count(n))
                if n >= 2:
                    act.wait_ge(group_done, FREED[n - 2])
                act.activation(upper(n, width_of(n)), chunk(n, width_of(n)), ACT.Copy).then_inc(upper_ready, 1)

            def split_after(group):
                if group[5] and group[1] + 2 < NCHUNK:
                    split_upper(group[1] + 2)

            split_upper(0)
            for n in range(2 * NT):
                act.wait_ge(group_done, n + 1)
                i, half = n // 2, n % 2
                act.activation(xh[:, 4 * half:4 * half + 4, i * P:(i + 1) * P],
                               group_bank(n)[:, :].rearrange("p (k t) -> p k t", k=4), ACT.Copy).then_inc(group_out, 1)

            def group_evac(n, group):
                form, _, _, dst, scale, _ = group
                src = group_bank(n)
                q = n - G1 - GATES
                if 2 <= q < SPILL:
                    act.wait_ge(spilled[q % 2], 16 * (q // 2))
                act.wait_ge(group_done, n + 1)
                if isinstance(dst, str):
                    w = 0 if dst == "kc" else 1
                    for kv in range(2):
                        for par in range(2):
                            last = act.activation(
                                KV[DH * par:DH * par + DH, w, :, 8 * kv:8 * kv + 8],
                                src[DH * kv:DH * kv + DH, :].rearrange(
                                    "p (n l two) -> p two l n", n=NBLK, two=2)[:, par], ACT.Copy)
                    last.then_inc(group_out, 1)
                elif form == "Q":
                    q_dst, m = dst
                    for half in range(2):
                        g, j = divmod(2 * m + half, 4)
                        last = act.activation(q_dst[DH * g:DH * g + DH, j, :], src[DH * half:DH * half + DH, :],
                                              ACT.Copy, scale=scale)
                    last.then_inc(group_out, 1)
                elif form == "V":
                    i = group[2]
                    act.activation(vs[:, i, :], src[:, 0:P], ACT.Copy)
                    act.activation(vw[:, i, :], src[:, P:2 * P], ACT.Copy)
                    act.activation(ga[:, i, :], src[:, 2 * P:2 * P + 24], ACT.Sigmoid).then_inc(group_out, 1)
                elif form == "N":
                    act.activation(dst, src[:, :].rearrange("p (i c) -> p i c", i=NT), ACT.Copy).then_inc(group_out, 1)
                elif form == "N2":
                    act.activation(dst, src[:, :].rearrange("p (i c) -> p i c", i=2), ACT.Copy).then_inc(group_out, 1)
                else:
                    act.activation(dst, src[:, :], ACT.Copy, scale=scale).then_inc(group_out, 1)

            split_upper(1)
            act.wait_ge(lam_dot, 1)
            act.activation(lamt[:, 2:4], lamt[:, 0:2], ACT.Exp).then_inc(lam_exp, 1)
            def first_evac(n):
                group_evac(G0 + n, FIRST[n])
                split_after(FIRST[n])

            for n in range(COMPRESS):
                if n == 4:
                    act.wait_ge(embed_done, 1)
                    act.activation(pe2, bank[5][:, 0:64].rearrange("p (w l) -> p w l", w=2),
                                   ACT.Copy).then_inc(embed_out, 1)
                first_evac(n)
            act.wait_ge(hc_done, 1)
            act.activation(hcx[0:16, :], bank[4][0:16, :], ACT.Copy).then_inc(hc_copied, 1)
            first_evac(COMPRESS)
            act.wait_ge(hc_cubic, 1)
            act.activation(hcu[0:16, :], hcu[0:16, :], ACT.Tanh, scale=math.sqrt(2 / math.pi)).then_inc(hc_tanh, 1)
            for n in range(COMPRESS + 1, len(FIRST) - 1):
                first_evac(n)
            act.wait_ge(hct_done, 1)
            act.activation(hcT, bank[5][:, 0:64].rearrange("p (f c) -> p f c", f=4), ACT.Copy,
                           scale=0.5).then_inc(hct_out, 1)
            first_evac(len(FIRST) - 1)
            act.wait_ge(cmp_done, 1)
            act.activation(kcmp, bank[4][:, 0:8], ACT.Copy)
            act.activation(vcmp[0:8, :], bank[4][0:8, 128:256], ACT.Copy).then_inc(cmp_out, 1)

            def exps(s):
                kind, g, i = JOBS[s]
                n = keys_of(kind, i)[1] + (kind == "swa")
                act.wait_ge(max_ready, s + 1)
                for j in range(4):
                    row = S[:, 4 * (s % 2) + j, 0:n]
                    last = act.activation(row, row, ACT.Exp, bias=negm[:, s % 2, j:j + 1],
                                          accum_out=esum[:, s % 2, j:j + 1])
                last.then_inc(exped, 1)

            def turned_evacs(s, part):
                first, last = TURN0[s], TURN0[s + 1]
                for n in range(first, last)[:2] if part == 0 else range(first, last)[2:]:
                    act.wait_ge(turned, n + 1)
                    if n >= 4:
                        act.wait_ge(pv_done, n - 3)
                    act.activation(PT[:, n % 4, :], bank[4 + n % 2][:, :], ACT.Copy).then_inc(turned_out, 1)
                if CLOSES[s] and part:
                    kind, g, i = JOBS[s]
                    act.wait_ge(pv_done, TURN0[s + 1])
                    rows = slice(DH * g, DH * g + DH)
                    if kind == "dif":
                        act.activation(odn[:, i, 256 * g:256 * g + 256], bank[6][:, 0:256], ACT.Copy).then_inc(o_out, 1)
                    else:
                        dst = ob if kind == "swa" else oa
                        act.activation(dst[rows, :, i * P:(i + 1) * P],
                                       bank[6][rows, :].rearrange("p (j t) -> p j t", j=4),
                                       ACT.Copy).then_inc(o_out, 1)

            for s in range(NJ + 1):
                if s < NJ:
                    exps(s)
                if s >= 1:
                    turned_evacs(s - 1, 0)
                if s < NJ:
                    for n in range(REST_AT[s], REST_AT[s + 1]):
                        group_evac(G1 + n, REST[n])
                if s >= 1:
                    turned_evacs(s - 1, 1)
                if s < NJ:
                    for n in range(REST_AT[s], REST_AT[s + 1]):
                        split_after(REST[n])
            act.wait_ge(o_out, OUT0[NJ])
            for n in range(16):
                row = odn[:, n // 4, P * (n % 4):P * (n % 4) + P]
                last = act.activation(S[:, n // 4, P * (n % 4):P * (n % 4) + P], row, ACT.Square, accum_out=ssq[:, n:n + 1])
            last.then_inc(sq_done, 1)
            act.wait_ge(rms_in, 1)
            act.activation(rms, ssq, ACT.Sqrt).then_inc(rms_root, 1)
            act.wait_ge(group_out, G1 + len(REST))
            for n in range(24):
                if n == 8:
                    act.activation(ob_halves[0], ob, ACT.Copy).then_inc(ob_upper, 1)
                    for r in range(2):
                        act.wait_ge(spilled[r], 16 * (SPILL // 2))
                    act.wait_ge(big_in[1], big_count(B_BR + 1))
                    act.activation(wb_halves[0][0], wb[1], ACT.Copy).then_inc(wb_upper, 1)
                if n == 16:
                    act.wait_ge(big_in[0], big_count(B_BR + 2))
                    act.activation(wb_halves[1][0], wb[2], ACT.Copy).then_inc(wb_upper, 1)
                    for hd in range(4):
                        act.wait_ge(oct_done, hd + 1)
                        act.activation(oc_halves[0][:, hd, :], bank[4 + hd % 2][:, :], ACT.Copy,
                                       scale=gcol).then_inc(oct_out, 1)
                if n >= ND and n % 4 == 0:
                    act.wait_ge(gates_in[n // 4 - 2], 16)
                act.activation(gates(n), gates(n), ACT.Sigmoid).then_inc(sig_done, 1)
            for m in range(ND):
                if m == 1:
                    act.wait_ge(branch_used, 8)
                    act.wait_ge(big_in[B_WO % 2], big_count(B_WO))
                    act.activation(wo_h[0], wo_raw[0], ACT.Copy).then_inc(wo_upper, 1)
                if m == 4:
                    act.wait_ge(wo1_in, 16)
                    act.activation(wo_h[1], wo_raw[1], ACT.Copy).then_inc(wo_upper, 1)
                act.wait_ge(merged_ready, m + 1)
                act.activation(merged_h[:, m, :], merged[:, m, :], ACT.Copy).then_inc(merged_upper, 1)
            def x1t_evac(i):
                for half in range(2):
                    n = 2 * i + half
                    act.wait_ge(x1t_done, n + 1)
                    act.activation(x1T[:, 4 * half:4 * half + 4, i * P:(i + 1) * P],
                                   bank[4 + half][:, :].rearrange("p (k t) -> p k t", k=4), ACT.Copy).then_inc(x1t_out, 1)

            def residual(i):
                act.wait_ge(x1_ready, i + 1)
                act.activation(acc[:, i, :], x1[:, i, :], ACT.Copy, scale=ALPHA).then_inc(residual_in, 1)

            for i in range(NT):
                act.wait_ge(var_ready, i + 1)
                act.activation(rstd, var_e, ACT.Sqrt).then_inc(root_ready, 1)
                if i >= 1:
                    x1t_evac(i - 1)
            for k in range(2):
                act.wait_ge(pt_done, k + 1)
                act.activation(pT[:, k, :], bank[4 + k][:, :], ACT.Copy).then_inc(pt_out, 1)
            x1t_evac(NT - 1)
            act.wait_ge(route_done, 1)
            act.activation(sc, bank[6][:, 0:256].rearrange("p (i e) -> p i e", i=NT), ACT.Sigmoid).then_inc(route_sig, 1)
            for i in range(NT):
                residual(i)
            def weights_upper(b, it, r):
                n = turn(b, it, r)
                act.wait_ge(wgu_in[r], 32 * (NEXP // NR * b + it + 1))
                if isinstance(n, int) and n < 2:
                    if n == 1:
                        act.wait_ge(sh_gu, NT)
                else:
                    act.wait_ge(gu_done, n - 1)
                act.activation(gu_upper(r), gu_raw(r), ACT.Copy).then_inc(e_upper, 1)

            for n in range(2 * NT):
                act.wait_ge(ple_done, n + 1)
                if n >= 2:
                    act.wait_ge(ple_used, n - 1)
                act.activation(ple_sg[:, n % 2, :], bank[n % 2][:, :], ACT.Sigmoid).then_inc(ple_sig, 1)
                if n == 1:
                    weights_upper(0, 0, 0)
            for i in range(NT):
                act.wait_ge(sh_gu, i + 1)
                act.activation(sg[:, i % 2, :], bank[i % 2][:, 0:F], ACT.Sigmoid).then_inc(sh_sig, 1)

            def xgt_evac(b, it, r):
                n = turn(b, it, r)
                for half in range(2):
                    act.wait_ge(xgt_done, 2 * n + half + 1)
                    if half == 0 and not (isinstance(n, int) and n < 2):
                        act.wait_ge(gu_done, n - 1)
                    act.activation(xgh[:, r % 2, 4 * half:4 * half + 4, :],
                                   bank[half][:, :].rearrange("p (k s) -> p k s", k=4), ACT.Copy).then_inc(xgt_out, 1)

            def gate_sig(b, it, r):
                n = turn(b, it, r)
                act.wait_ge(gu_done, n + 1)
                if not (isinstance(n, int) and n < 2):
                    act.wait_ge(h_ready, n - 1)
                act.activation(sg[:, r % 2, :], bank[2 + r % 2][:, 0:F], ACT.Sigmoid).then_inc(e_sig, 1)

            def y_evac(b, it, r):
                n = turn(b, it, r)
                act.wait_ge(y_done, n + 1)
                act.wait_ge(ycol_ready, n + 1)
                for half in range(2):
                    act.activation(y[:, r % 2, 512 * half:512 * half + 512], bank[5 + half][:, :],
                                   ACT.Copy, scale=wgr[:, r:r + 1]).then_inc(y_out, 1)

            def expert_acts(b):
                if b:
                    weights_upper(b, 0, 0)
                weights_upper(b, 0, 1)
                xgt_evac(b, 0, 0)

                def step(it, r, before, after=2):
                    gate_sig(b, it, r)
                    if after >= 1:
                        xgt_evac(b, it + (r + 1) // NR, (r + 1) % NR)
                    if after >= 2:
                        weights_upper(b, it + (r + 2) // NR, (r + 2) % NR)
                    if before is not None:
                        y_evac(b, *before)

                for r in range(NR):
                    step(0, r, (0, r - 1) if r else None)
                last = NEXP // NR - 1
                with act.Fori(1, last) as it:
                    for r in range(NR):
                        step(it, r, (it, r - 1) if r else (it - 1, NR - 1))
                for r in range(NR):
                    step(last, r, (last, r - 1) if r else (last - 1, NR - 1), after=NR - 1 - r)
                y_evac(b, last, NR - 1)

            expert_acts(0)
            act.wait_ge(cnt_ready, 1)
            most = act.value_load(cnt[0:1, 0:1], min_val=0, max_val=T)
            with act.If(most > CAP):
                expert_acts(1)
                with act.If(most > 2 * CAP):
                    expert_acts(2)
                    with act.If(most > 3 * CAP):
                        expert_acts(3)
                        with act.If(most > 4 * CAP):
                            expert_acts(4)
                            act.nop()
                        act.nop()
                    act.nop()
                act.nop()
            for i in range(NT):
                act.wait_ge(var_ready, NT + i + 1)
                act.activation(rstd, var_e, ACT.Sqrt).then_inc(root_ready, 1)

        @block.vector
        def _(dve):
            links = [0]

            def link(ins):
                links[0] += 1
                ins.then_inc(chain, 1)
                dve.wait_ge(chain, links[0])

            dve.memset(vcmp, 0.0)
            dve.memset(esum[:, :, :].rearrange("p r j -> p (r j)"), 0.0)
            def split_lower(n):
                dve.wait_ge(upper_ready, n + 1)
                w = width_of(n)
                dve.tensor_tensor(lower(n, w), chunk(n, w), upper(n, w), ALU.subtract).then_inc(lower_ready, 1)

            split_lower(0)
            for n in range(2 * NT):
                i, half = n // 2, n % 2
                cut = (slice(None), slice(4 * half, 4 * half + 4), slice(i * P, (i + 1) * P))
                dve.wait_ge(group_out, n + 1)
                dve.tensor_tensor(xl[cut], group_bank(n)[:, :].rearrange("p (k t) -> p k t", k=4), xh[cut],
                                  ALU.subtract).then_inc(x_low, 1)

            dve.wait_ge(const_in, 16 * 10)
            link(dve.tensor_tensor(lq[:, 0:3:2, :], lq[:, 0:3:2, :], lq[:, 1:4:2, :], ALU.mult))
            dve.tensor_reduce(lamt[:, 0:2], lq[:, 0:3:2, :], axis=AXX, op=ALU.add).then_inc(lam_dot, 1)
            dve.wait_ge(lam_exp, 1)
            link(dve.tensor_tensor(lamt[:, 0:1], lamt[:, 3:4], lamt[:, 2:3], ALU.subtract))
            dve.memset(lamv, 1.0)
            link(dve.tensor_scalar(gcol, gcol, 1.0 - LAMBDA_INIT, None, ALU.mult))
            for j in (1, 3):
                last = dve.tensor_scalar(lamv[:, j:j + 1], lamt[:, 0:1], -LAMBDA_INIT, None, ALU.add)
            link(last)
            for n in range(1, 4):
                split_lower(n)
            dve.wait_ge(embed_out, 1)
            for w in range(2):
                dve.wait_ge(group_out, G0 + 4 + w + 1)
                dve.tensor_tensor(KV[:, w], KV[:, w], pe2[:, w, :].unsqueeze(2).to_broadcast([P, 32, 16]),
                                  ALU.add).then_inc(pe_added, 1)
            split_lower(4)
            dve.wait_ge(hc_copied, 1)
            link(dve.tensor_tensor(hcu[0:16, :], hcx[0:16, :], hcx[0:16, :], ALU.mult))
            link(dve.tensor_scalar(hcu[0:16, :], hcu[0:16, :], 0.044715, 1.0, ALU.mult, ALU.add))
            dve.tensor_tensor(hcu[0:16, :], hcu[0:16, :], hcx[0:16, :], ALU.mult).then_inc(hc_cubic, 1)
            dve.wait_ge(hc_tanh, 1)
            dve.scalar_tensor_tensor(hcu[0:16, :], hcu[0:16, :], 1.0, hcx[0:16, :], ALU.add,
                                     ALU.mult).then_inc(hc_ready, 1)
            split_lower(REST0)
            split_lower(REST0 + 1)
            dve.wait_ge(pool_const, 13)

            def bias_and_max(s):
                kind, g, i = JOBS[s]
                n = keys_of(kind, i)[1]
                rows = S[:, 4 * (s % 2):4 * (s % 2) + 4, :]
                if s >= 2:
                    dve.wait_ge(turned, TURN0[s - 1])
                if kind == "cmp":
                    dve.memset(rows[:, :, NBLK:P], 0.0)
                if kind == "swa":
                    dve.tensor_copy(rows[:, :, n:n + 1], sinks[:, 4 * g:4 * g + 4].unsqueeze(2))
                for j in range(4):
                    dve.wait_ge(scored, 4 * s + j + 1)
                    last = dve.scalar_tensor_tensor(rows[:, j, 0:n], distances(kind, i, n),
                                                    -slope_of(kind, g, j), bank[j][:, 0:n],
                                                    ALU.mult, ALU.add)
                    last.then_inc(biased, 1)
                dve.wait_ge(biased, 4 * s + 4)
                if s >= 2:
                    dve.wait_ge(exped, s - 1)
                m = dve.tensor_reduce(negm[:, s % 2, :], rows[:, :, 0:n + (kind == "swa")], axis=AXX,
                                      op=ALU.max, negate=True)
                if kind == "cmp":
                    link(m)
                    m = dve.tensor_scalar(negm[:, s % 2, :], negm[:, s % 2, :], 1e29, None, ALU.min)
                m.then_inc(max_ready, 1)

            def weigh(s):
                kind, g, i = JOBS[s]
                n = keys_of(kind, i)[1]
                f = fac[:, s % 2, :]
                dve.wait_ge(exped, s + 1)
                e = esum[:, s % 2, :]
                if kind == "cmp":
                    link(dve.tensor_scalar(e, e, 1e-30, None, ALU.max))
                link(dve.reciprocal(f, e))
                if kind in ("slc", "win", "cmp"):
                    br = ("cmp", "slc", "win").index(kind)
                    gates = ga[:, i, 12 * g + br:12 * g + br + 10:3]
                    link(dve.tensor_tensor(f, f, gates, ALU.mult))
                if kind == "dif":
                    link(dve.tensor_tensor(f, f, lamv, ALU.mult))
                    for hh in range(2):
                        a, b = (S[:, 4 * (s % 2) + 2 * hh + r, 0:n] for r in range(2))
                        link(dve.tensor_scalar(b, b, f[:, 2 * hh + 1:2 * hh + 2], None, ALU.mult))
                        last = dve.scalar_tensor_tensor(a, a, f[:, 2 * hh:2 * hh + 1], b, ALU.mult, ALU.add)
                else:
                    for j in range(4):
                        row = S[:, 4 * (s % 2) + j, 0:n]
                        last = dve.tensor_scalar(row, row, f[:, j:j + 1], None, ALU.mult)
                last.then_inc(probs, 1)

            for s in range(NJ):
                bias_and_max(s)
                if s >= 1:
                    for n in range(REST_AT[s - 1], REST_AT[s]):
                        if REST[n][5] and REST[n][1] + 2 < NCHUNK:
                            split_lower(REST[n][1] + 2)
                weigh(s)
            dve.wait_ge(sq_done, 1)
            dve.tensor_scalar(ssq, ssq, 1.0 / (2 * DH), EPS, ALU.mult, ALU.add).then_inc(rms_in, 1)
            dve.wait_ge(rms_root, 1)
            link(dve.reciprocal(rms, rms))
            for n in range(16):
                row = odn[:, n // 4, P * (n % 4):P * (n % 4) + P]
                last = dve.tensor_scalar(row, row, rms[:, n:n + 1], None, ALU.mult)
            last.then_inc(od_ready, 1)
            def out_weights_lower(half):
                dve.wait_ge(wo_upper, half + 1)
                dve.tensor_tensor(wo_l[half], wo_raw[half], wo_h[half], ALU.subtract).then_inc(wo_lower, 1)

            def merged_lower_of(m):
                dve.wait_ge(merged_upper, m + 1)
                dve.tensor_tensor(merged_l[:, m, :], merged[:, m, :], merged_h[:, m, :],
                                  ALU.subtract).then_inc(merged_lower, 1)

            for n in range(24):
                m = n % 8
                if n == 3:
                    dve.wait_ge(ob_upper, 1)
                    dve.tensor_tensor(ob_halves[1], ob, ob_halves[0], ALU.subtract).then_inc(ob_lower, 1)
                if n in (5, 12):
                    b = 1 if n == 5 else 2
                    dve.wait_ge(wb_upper, b)
                    dve.tensor_tensor(wb_halves[b - 1][1], wb[b], wb_halves[b - 1][0], ALU.subtract).then_inc(wb_lower, 1)
                if n in (12, 14):
                    for hd in range(n - 12, n - 10):
                        dve.wait_ge(oct_out, hd + 1)
                        dve.scalar_tensor_tensor(oc_halves[1][:, hd, :], bank[4 + hd % 2][:, :], gcol,
                                                 oc_halves[0][:, hd, :], ALU.mult, ALU.subtract).then_inc(oc_lower, 1)
                dve.wait_ge(sig_done, n + 1)
                dve.wait_ge(branch_done, n + 1)
                dst = merged[:, m, :] if n < 8 else mtmp[:, n % 2, :]
                ins = dve.tensor_tensor(dst, bank[n % 4][:, :], gates(n), ALU.mult)
                ins.then_inc(branch_used, 1)
                if n >= 8:
                    dve.wait_ge(branch_used, n + 1)
                    last = dve.tensor_tensor(merged[:, m, :], merged[:, m, :], mtmp[:, n % 2, :], ALU.add)
                if n >= 16:
                    last.then_inc(merged_ready, 1)
                    if m == 4:
                        out_weights_lower(0)
                    if m >= 1:
                        merged_lower_of(m - 1)
            merged_lower_of(ND - 1)
            out_weights_lower(1)

            def layer_norm(src, dst, root):
                for c in range(2):
                    last = dve.bn_stats(stats[:, c, :], src[:, 512 * c:512 * c + 512])
                link(last)
                link(dve.bn_aggr(mv, stats))
                if root > 1:
                    dve.wait_ge(root_ready, root - 1)
                dve.tensor_scalar(var_e, mv[:, 1:2], EPS, None, ALU.add).then_inc(var_ready, 1)
                dve.wait_ge(root_ready, root)
                link(dve.reciprocal(rstd, rstd))
                link(dve.tensor_scalar(dst, src, mv[:, 0:1], rstd, ALU.subtract, ALU.mult))
                link(dve.tensor_tensor(dst, dst, ln1[:, 0, :], ALU.mult))
                return dve.tensor_tensor(dst, dst, ln1[:, 1, :], ALU.add)

            dve.wait_ge(xr_in, 16)
            for i in range(NT):
                for half in range(2):
                    cols = slice(512 * half, 512 * half + 512)
                    dve.wait_ge(att_done, 2 * i + half + 1)
                    last = dve.scalar_tensor_tensor(z[:, i % 2, cols], xr[:, i, cols], ALPHA,
                                                    bank[2 * (i % 2) + half][:, :], ALU.mult, ALU.add)
                    last.then_inc(att_used, 1)
                dve.wait_ge(att_used, 2 * i + 2)
                if i == 0:
                    dve.wait_ge(late_in, 16 * 5)
                layer_norm(z[:, i % 2, :], x1[:, i, :], i + 1).then_inc(x1_ready, 1)

            dve.wait_ge(route_sig, 1)
            dve.memset(gs[:, :, NGRP:NGRP + 4], -1e30)
            link(dve.tensor_tensor(bi, sc, rbias.unsqueeze(1).to_broadcast([P, NT, NEXP]), ALU.add))
            for i in range(NT):
                for g in range(NGRP):
                    last = dve.max(g8[:, i, g, :], bi[:, i, GSZ * g:GSZ * g + GSZ])
            link(last)
            link(dve.tensor_tensor(gs[:, :, 0:NGRP], g8[:, :, :, 0], g8[:, :, :, 1], ALU.add))
            for i in range(NT):
                last = dve.max(gt8[:, i, :], gs[:, i, 0:NGRP])
            link(last)
            link(dve.memset(gt8[:, :, TOPG:8], -1e30))
            for i in range(NT):
                last = dve.match_replace(gr[:, i, :], gt8[:, i, :], gs[:, i, :], -2e30)
            link(last)
            link(dve.tensor_scalar(gmask, gr[:, :, 0:NGRP], -1.5e30, None, ALU.is_lt))
            link(dve.tensor_scalar(gneg, gmask, -1.0, 1e30, ALU.add, ALU.mult))

            def by_expert(t):
                return t.rearrange("p i (g c) -> p i g c", g=NGRP)

            for i in range(NT):
                gb = gmask[:, i, :].unsqueeze(2).to_broadcast([P, NGRP, GSZ])
                last = dve.tensor_tensor(by_expert(m1)[:, i], by_expert(bi)[:, i], gb, ALU.mult)
            link(last)
            for i in range(NT):
                gb = gneg[:, i, :].unsqueeze(2).to_broadcast([P, NGRP, GSZ])
                last = dve.tensor_tensor(by_expert(m1)[:, i], by_expert(m1)[:, i], gb, ALU.add)
            link(last)
            for i in range(NT):
                last = dve.max(v8[:, i, :], m1[:, i, :])
            link(last)
            for i in range(NT):
                last = dve.match_replace(rep[:, i, :], v8[:, i, :], m1[:, i, :], -3e30)
            link(last)
            link(dve.tensor_scalar(sel, rep, -2e30, None, ALU.is_lt))
            dve.tensor_copy(selb, sel).then_inc(sel_ready, 1)
            link(dve.tensor_tensor(ws, sc, sel, ALU.mult))
            link(dve.tensor_reduce(wsum, ws, axis=AXX, op=ALU.add))
            link(dve.reciprocal(wrec, wsum))
            for i in range(NT):
                last = dve.tensor_scalar(ws[:, i, :], ws[:, i, :], wrec[:, i:i + 1], ROUTED_SCALE,
                                         ALU.mult, ALU.mult)
            link(last)
            dve.wait_ge(xg_zero, 1)

            def part(c):
                return RW5[:, :, :, c].rearrange("p e i -> p i e")

            link(dve.tensor_copy(part(2), ws))
            link(dve.tensor_tensor(wr1, ws, part(2), ALU.subtract))
            link(dve.tensor_copy(part(3), wr1))
            link(dve.tensor_tensor(part(4), wr1, part(3), ALU.subtract))

            def ple(n):
                half, i = n // NT, n % NT
                cols = slice(512 * half, 512 * half + 512)
                dve.wait_ge(ple_sig, n + 1)
                ins = dve.tensor_tensor(ple_sg[:, n % 2, :], ple_sg[:, n % 2, :], bank[2 + n % 2][:, :], ALU.mult)
                link(ins)
                dve.tensor_tensor(acc[:, i, cols], acc[:, i, cols], ple_sg[:, n % 2, :],
                                  ALU.add).then_inc(ple_used, 1)

            def weights_lower(b, it, r):
                dve.wait_ge(e_upper, turn(b, it, r) + 1)
                dve.tensor_tensor(gu_lower(r), gu_raw(r), gu_upper(r), ALU.subtract).then_inc(e_lower, 1)

            dve.wait_ge(residual_in, NT)
            for n in range(NT):
                ple(n)
                if n == NT - 2:
                    weights_lower(0, 0, 0)
            dve.wait_ge(pos_done, 1)
            posp = bank[7][:, 0:256].rearrange("p (i e) -> p i e", i=NT)
            link(dve.scalar_tensor_tensor(pos1, posp, 1.0, sel, ALU.add, ALU.mult))
            count = bank[7][:, 256:320]
            link(dve.tensor_copy(before[0], count))
            link(dve.tensor_scalar(minus_p, slot_row[:, 0:1], -1.0, None, ALU.mult))
            for step in range(6):
                a, b, w = before[step % 2], before[(step + 1) % 2], 1 << step
                dve.tensor_copy(b[:, 0:w], a[:, 0:w])
                link(dve.tensor_tensor(b[:, w:], a[:, w:], a[:, 0:NEXP - w], ALU.add))
            link(dve.tensor_tensor(slot_row, slot_row, before[0], ALU.add))
            link(dve.tensor_tensor(slot_row, slot_row, count, ALU.subtract))
            dve.tensor_scalar(posE.rearrange("p e i -> p i e"), pos1, -1.0, None, ALU.add)
            for i in range(NT):
                last = dve.tensor_tensor(dd[:, i, :], sel[:, i, :], slot_row, ALU.mult)
            link(last)
            link(dve.tensor_tensor(dd, dd, pos1, ALU.add))
            for i in range(NT):
                last = dve.max(d8[:, i, :], dd[:, i, :])
            link(last)
            link(dve.tensor_scalar(d8, d8, minus_p, -1.0, ALU.add, ALU.add))
            link(dve.tensor_copy(dest, d8))
            link(dve.tensor_reduce(cmax, bank[7][:, 256:320], axis=AXX, op=ALU.max))
            dve.tensor_copy(cnt, cmax).then_inc(cnt_ready, 1)
            dve.nop().then_inc(pos_used, 1)

            def hot(r, e, n):
                if not (isinstance(n, int) and n < NHOT):
                    dve.wait_ge(hot_used, n - NHOT + 1)
                for i in range(NT):
                    last = dve.tensor_scalar(onehot[:, r, i, :], iota_s, posE[:, bass.ds(e, 1), i], None,
                                             ALU.is_equal)
                last.then_inc(hot_ready, 1)

            def index_tables(b):
                dve.wait_ge(idx_done, b + 1)
                t5 = bank[7][:, 0:320].rearrange("p (e c) -> p e c", c=5)
                dve.tensor_copy(IDX, t5[:, :, 0]).then_inc(index_chain, 1)
                dve.wait_ge(index_chain, 7 * b + 1)
                dve.tensor_tensor(IDX, IDX, t5[:, :, 1], ALU.add).then_inc(index_chain, 1)
                dve.tensor_reduce(WG, t5[:, :, 2:5], axis=AXX, op=ALU.add)
                dve.wait_ge(index_chain, 7 * b + 2)
                dve.tensor_scalar(IDX, IDX, 1024.0, None, ALU.add).then_inc(index_chain, 1)
                dve.wait_ge(index_chain, 7 * b + 3)
                dve.tensor_scalar(IDY, IDX, float(T), 65536.0, ALU.is_ge, ALU.mult).then_inc(index_chain, 1)
                dve.wait_ge(index_chain, 7 * b + 4)
                dve.tensor_tensor(IDY, IDY, slot_row, ALU.add).then_inc(index_chain, 1)
                dve.wait_ge(index_chain, 7 * b + 5)
                dve.tensor_scalar(IDY, IDY, float(CAP * b), None, ALU.add).then_inc(index_chain, 1)
                dve.wait_ge(index_chain, 7 * b + 6)
                dve.tensor_scalar(posE, posE, -float(CAP), None, ALU.add).then_inc(index_chain, 1)
                dve.wait_ge(index_chain, 7 * b + 7)
                dve.nop().then_inc(idx_used, 1)

            def index_pass(b):
                with dve.Fori(0, NEXP // 4) as it:
                    for r in range(4):
                        n = turn(b, it, r)
                        hot_loop(r, 4 * it + r, n)
                index_tables(b)

            def hot_loop(r, e, n):
                dve.wait_ge(hot_used, n - 3)
                for i in range(NT):
                    last = dve.tensor_scalar(onehot[:, r, i, :], iota_s, posE[:, bass.ds(e, 1), i], None,
                                             ALU.is_equal)
                last.then_inc(hot_ready, 1)

            def hots(batch):
                for n in range(HOT0[batch], HOT0[batch + 1]):
                    hot(n % NHOT, n, n)

            def tokens_of(it, r):
                e = NR * it + r
                dve.tensor_copy(idxr[:, r:r + 1], IDX[:, bass.ds(e, 1)]).then_inc(col_ready, 1)

            dve.wait_ge(x1_stored, 16 * NT)
            for n in range(NT, 2 * NT):
                ple(n)
                hots(n - NT)

            def rows_lower(b, it, r):
                n = turn(b, it, r)
                for half in range(2):
                    dve.wait_ge(xgt_out, 2 * n + half + 1)
                    dve.tensor_tensor(xgl[:, r % 2, 4 * half:4 * half + 4, :],
                                      bank[half][:, :].rearrange("p (k s) -> p k s", k=4),
                                      xgh[:, r % 2, 4 * half:4 * half + 4, :], ALU.subtract).then_inc(xgl_out, 1)

            def shared_hidden(i):
                dve.wait_ge(sh_sig, i + 1)
                if i >= 2:
                    dve.wait_ge(sh_ht, i - 1)
                link(dve.tensor_tensor(sg[:, i % 2, :], sg[:, i % 2, :], bank[i % 2][:, 0:F], ALU.mult))
                dve.tensor_tensor(h[:, i % 2, :], sg[:, i % 2, :], bank[i % 2][:, F:2 * F], ALU.mult).then_inc(sh_h, 1)
                if i < 2:
                    hots(NT + 2 * i)

            shared_hidden(0)
            for i in range(NT):
                dve.wait_ge(sh_ht, i + 1)
                dve.tensor_copy(hT[:, i % 2], bank[4][:, 0:256].rearrange("p (k s) -> p k s", k=NF)).then_inc(sh_hto, 1)
                if i < 2:
                    hots(NT + 2 * i + 1)
                if i + 1 < NT:
                    shared_hidden(i + 1)
                else:
                    rows_lower(0, 0, 0)
                for half in range(2):
                    cols = slice(512 * half, 512 * half + 512)
                    dve.wait_ge(sh_y, i + 1)
                    last = dve.tensor_tensor(acc[:, i, cols], acc[:, i, cols], bank[2 + half][:, :], ALU.add)
                last.then_inc(sh_used, 1)
                if i == 1:
                    index_tables(0)
                    for r in range(NR):
                        tokens_of(0, r)

            def rows_of(b, it, r):
                n = turn(b, it, r)
                e = NR * it + r
                if not (isinstance(n, int) and n < 2):
                    dve.wait_ge(scattered[r % 2], 16 * second(b, it, r))
                dve.tensor_copy(idyr[:, r:r + 1], IDY[:, bass.ds(e, 1)])
                dve.tensor_copy(wgr[:, r:r + 1], WG[:, bass.ds(e, 1)]).then_inc(ycol_ready, 1)

            silu = sem("silu")

            def hidden_all(b, it, r):
                n = turn(b, it, r)
                dve.wait_ge(e_sig, n + 1)
                if not (isinstance(n, int) and n < 2):
                    dve.wait_ge(ht_done, n - 1)
                dve.tensor_tensor(sg[:, r % 2, :], sg[:, r % 2, :], bank[2 + r % 2][:, 0:F],
                                  ALU.mult).then_inc(silu, 1)
                dve.wait_ge(silu, n + 1)
                dve.tensor_tensor(h[:, r % 2, :], sg[:, r % 2, :], bank[2 + r % 2][:, F:2 * F],
                                  ALU.mult).then_inc(h_ready, 1)

            def hidden_evac(b, it, r):
                n = turn(b, it, r)
                dve.wait_ge(ht_done, n + 1)
                if not (isinstance(n, int) and n < 2):
                    dve.wait_ge(y_done, n - 1)
                dve.tensor_copy(hT[:, r % 2], bank[4][:, 0:256].rearrange("p (k s) -> p k s", k=NF)).then_inc(ht_out, 1)

            def expert_vectors(b):
                if b:
                    index_pass(b)
                    for r in range(NR):
                        tokens_of(0, r)
                    weights_lower(b, 0, 0)
                    rows_lower(b, 0, 0)
                weights_lower(b, 0, 1)

                def step(it, r, before, after=2, more=True):
                    if before is not None:
                        hidden_evac(b, *before)
                    hidden_all(b, it, r)
                    if after >= 1:
                        rows_lower(b, it + (r + 1) // NR, (r + 1) % NR)
                    if more:
                        tokens_of(it + 1, r)
                    if after >= 2:
                        weights_lower(b, it + (r + 2) // NR, (r + 2) % NR)
                    rows_of(b, it, r)

                for r in range(NR):
                    step(0, r, (0, r - 1) if r else None)
                last = NEXP // NR - 1
                with dve.Fori(1, last) as it:
                    for r in range(NR):
                        step(it, r, (it, r - 1) if r else (it - 1, NR - 1))
                for r in range(NR):
                    step(last, r, (last, r - 1) if r else (last - 1, NR - 1), after=NR - 1 - r, more=False)
                hidden_evac(b, last, NR - 1)

            expert_vectors(0)
            dve.wait_ge(cnt_ready, 1)
            most = dve.value_load(cnt[0:1, 0:1], min_val=0, max_val=T)
            with dve.If(most > CAP):
                expert_vectors(1)
                with dve.If(most > 2 * CAP):
                    expert_vectors(2)
                    with dve.If(most > 3 * CAP):
                        expert_vectors(3)
                        with dve.If(most > 4 * CAP):
                            expert_vectors(4)
                            dve.nop()
                        dve.nop()
                    dve.nop()
                dve.nop()
            final = sem("final_chain")
            links_f = [0]

            def flink(ins):
                links_f[0] += 1
                ins.then_inc(final, 1)
                dve.wait_ge(final, links_f[0])

            for i in range(NT):
                dve.wait_ge(rows_summed, i + 1)
                for half in range(2):
                    cols = slice(512 * half, 512 * half + 512)
                    last = dve.tensor_tensor(acc[:, i, cols], acc[:, i, cols], bank[2 * (i % 2) + half][:, :], ALU.add)
                last.then_inc(sums_used, 1)
                dve.wait_ge(sums_used, i + 1)
                for k in range(PE_ROWS, TOPK):
                    n = i * TOPK + k
                    dve.wait_ge(row_in[n % NROW], 16 * (n // NROW + 1))
                    flink(dve.tensor_tensor(acc[:, i, :], acc[:, i, :], last_rows(n), ALU.add))
                for c in range(2):
                    last = dve.bn_stats(stats[:, c, :], acc[:, i, 512 * c:512 * c + 512])
                flink(last)
                flink(dve.bn_aggr(mv, stats))
                dve.tensor_scalar(var_e, mv[:, 1:2], EPS, None, ALU.add).then_inc(var_ready, 1)
                dve.wait_ge(root_ready, NT + i + 1)
                flink(dve.reciprocal(rstd, rstd))
                flink(dve.tensor_scalar(acc[:, i, :], acc[:, i, :], mv[:, 0:1], rstd, ALU.subtract, ALU.mult))
                if i == 0:
                    dve.wait_ge(ln2_in, 32)
                flink(dve.tensor_tensor(acc[:, i, :], acc[:, i, :], ln2[:, 0, :], ALU.mult))
                dve.tensor_tensor(acc[:, i, :], acc[:, i, :], ln2[:, 1, :], ALU.add).then_inc(out_ready, 1)

        @block.tensor
        def _(pe):
            mm = pe.matmul
            pe.wait_ge(pool_const, 13)
            for n in range(2 * NT):
                i, half = n // 2, n % 2
                if half == 0:
                    pe.wait_ge(x_in[i], 16)
                if n >= 4:
                    pe.wait_ge(x_low, n - 3)
                for k in range(4):
                    last = pe.transpose(group_bank(n)[:, k * P:(k + 1) * P],
                                        x0[:, i, (4 * half + k) * P:(4 * half + k + 1) * P], ident)
                last.then_inc(group_done, 1)
            def products(dst, stationary, moving, tiles=ND, ready=None):
                (sh, sl), (mh, ml) = stationary, moving
                for k in range(tiles):
                    if ready is not None:
                        pe.wait_ge(ready, k + 1)
                    mm(dst, sh(k), mh(k), start=(k == 0), stop=False)
                    mm(dst, sh(k), ml(k), start=False, stop=False)
                    last = mm(dst, sl(k), mh(k), start=False, stop=(k == tiles - 1))
                return last

            def group(n, desc):
                form, c, col, _, _, _ = desc
                dstb = group_bank(n)
                pe.wait_ge(lower_ready, c + 1)
                pe.wait_ge(group_out, n - 1 if n < G1 else n)
                w_halves = upper(c, width_of(c)), lower(c, width_of(c))
                if form in ("T", "Q"):
                    last = products(dstb[:, :], [lambda k, a=a: a[:, k, col:col + P] for a in w_halves],
                                    [lambda k, a=a: a[:, k, :] for a in (xh, xl)])
                else:
                    tiles, c0, width = {"N": (range(NT), col, P), "N2": (range(col, col + 2), 0, 2 * P),
                                        "V": (range(col, col + 1), 0, width_of(c))}[form]
                    for a, i in enumerate(tiles):
                        last = products(dstb[:, a * width:(a + 1) * width],
                                        [lambda k, a=a, i=i: a[:, k, i * P:(i + 1) * P] for a in (xh, xl)],
                                        [lambda k, a=a: a[:, k, c0:c0 + width] for a in w_halves])
                last.then_inc(group_done, 1)

            pe.wait_ge(x_low, 2 * NT)
            for n in range(COMPRESS):
                if n == 4:
                    pe.wait_ge(const_in, 16 * 10)
                    for w in range(2):
                        last = pe.transpose(bank[5][:, 32 * w:32 * w + 32], pe_raw[0:32, w, :], ident[0:32, 0:32])
                    last.then_inc(embed_done, 1)
                group(G0 + n, FIRST[n])
            for w in range(2):
                pe.wait_ge(pe_added, w + 1)
                pe.wait_ge(w1_in[w], 16 * NW1)
                for c in range(NW1):
                    for a in range(ND):
                        la = c * ND + a
                        last = mm(bank[4][0:16, 256 * w:256 * w + 256], KV[:, w, la, :], w1_chunk(w, c)[:, a, :],
                                  start=(la == 0), stop=(la == NW1 * ND - 1))
            last.then_inc(hc_done, 1)
            for n in range(COMPRESS, len(FIRST) - 1):
                group(G0 + n, FIRST[n])
            pe.wait_ge(hc_ready, 1)
            for f in range(4):
                last = pe.transpose(bank[5][:, 16 * f:16 * f + 16], hcu[0:16, P * f:P * f + P], ident[0:16, 0:16])
            last.then_inc(hct_done, 1)
            group(G1 - 1, FIRST[-1])
            pe.wait_ge(hct_out, 1)
            w2k = w2[:, 0:128].rearrange("p (f d) -> p f d", f=2)
            w2v = w2[:, 128:256].rearrange("p (f d) -> p f d", f=2)
            for g in range(2):
                for f in range(2):
                    mm(bank[4][DH * g:DH * g + DH, 0:8], w2k[:, f, :], hcT[:, f, 8 * g:8 * g + 8],
                       start=(f == 0), stop=(f == 1))
            for g in range(2):
                for f in range(2):
                    last = mm(bank[4][0:8, 128 + DH * g:128 + DH * g + DH], hcT[:, 2 + f, 8 * g:8 * g + 8],
                              w2v[:, f, :], start=(f == 0), stop=(f == 1))
            last.then_inc(cmp_done, 1)
            pe.wait_ge(cmp_out, 1)

            def scores(s):
                kind, g, i = JOBS[s]
                n = keys_of(kind, i)[1]
                pe.wait_ge(group_out, need_group(kind))
                for j in range(4):
                    if s >= 1:
                        pe.wait_ge(biased, 4 * (s - 1) + j + 1)
                    q, k = unit_operands(kind, g, i, j)
                    mm(bank[j][:, 0:n], q, k, start=True, stop=True).then_inc(scored, 1)

            def turn_and_value(s, between):
                kind, g, i = JOBS[s]
                lo = keys_of(kind, i)[0]
                nb = blocks_of(kind, i)
                pe.wait_ge(probs, s + 1)
                first_of_out = s == 0 or CLOSES[s - 1]

                def transposes(n, a):
                    if n >= 2:
                        pe.wait_ge(turned_out, n - 1)
                    for q in range(nb if kind == "dif" else 4):
                        if kind == "dif":
                            src = S[:, 4 * (s % 2) + 2 * a, q * P:(q + 1) * P]
                        else:
                            src = S[:, 4 * (s % 2) + q, a * P:(a + 1) * P]
                        last = pe.transpose(bank[4 + n % 2][:, q * P:(q + 1) * P], src, ident)
                    last.then_inc(turned, 1)

                def values(n, a):
                    pe.wait_ge(turned_out, n + 1)
                    if first_of_out and a == 0 and OUT0[s] >= 1:
                        pe.wait_ge(o_out, OUT0[s])
                    rows = slice(DH * g, DH * g + DH)
                    if kind == "dif":
                        hd = 2 * g + a
                        for q in range(nb):
                            last = mm(bank[6][:, P * a:P * a + P], PT[:, n % 4, q * P:(q + 1) * P],
                                      vd[:, q, P * hd:P * hd + P], start=(q == 0), stop=(q == nb - 1))
                    else:
                        v = {"slc": lambda: vs[:, a, rows], "win": lambda: vw[:, a, rows],
                             "swa": lambda: vb[:, lo + a, rows], "cmp": lambda: vcmp[:, rows]}[kind]()
                        last = mm(bank[6][rows, :], v, PT[:, n % 4, :], start=first_of_out and a == 0,
                                  stop=CLOSES[s] and a == turns - 1)
                    last.then_inc(pv_done, 1)

                turns = turns_of(kind, i)
                t0 = TURN0[s]
                ahead = min(2, turns)
                for a in range(ahead):
                    transposes(t0 + a, a)
                between()
                for a in range(turns):
                    values(t0 + a, a)
                    if a + ahead < turns:
                        transposes(t0 + a + ahead, a + ahead)

            for s in range(NJ + 1):
                def project():
                    if s < NJ:
                        for n in range(REST_AT[s], REST_AT[s + 1]):
                            group(G1 + n, REST[n])

                if s < NJ:
                    scores(s)
                if s >= 1:
                    turn_and_value(s - 1, project)
                else:
                    project()

            pe.wait_ge(o_out, OUT0[NJ])
            for n in range(24):
                b, m = n // 8, n % 8
                if n == 0:
                    pe.wait_ge(big_in[0], big_count(B_BR))
                if n == 8:
                    pe.wait_ge(ob_lower, 1)
                    pe.wait_ge(wb_lower, 1)
                if n in (12, 14):
                    pe.wait_ge(od_ready, 1)
                    for hd in range(n - 12, n - 10):
                        if hd >= 2:
                            pe.wait_ge(oc_lower, hd - 1)
                        for i in range(NT):
                            last = pe.transpose(bank[4 + hd % 2][:, i * P:(i + 1) * P],
                                                odn[:, i, P * hd:P * hd + P], ident)
                        last.then_inc(oct_done, 1)
                if n == 16:
                    pe.wait_ge(oc_lower, 4)
                    pe.wait_ge(wb_lower, 2)
                if n >= 4:
                    pe.wait_ge(branch_used, n - 3)
                cols = slice(m * P, (m + 1) * P)
                if b == 0:
                    for j in range(4):
                        last = mm(bank[n % 4][:, :], wb[0][:, j, cols], oa[:, j, :], start=(j == 0), stop=(j == 3))
                else:
                    last = products(bank[n % 4][:, :], [lambda j, a=a: a[:, j, cols] for a in wb_halves[b - 1]],
                                    [lambda j, a=a: a[:, j, :] for a in (ob_halves, oc_halves)[b - 1]], tiles=4)
                last.then_inc(branch_done, 1)

            def att_out(i):
                for half in range(2):
                    if i == 0:
                        pe.wait_ge(wo_lower, half + 1)
                    if i >= 2:
                        pe.wait_ge(att_used, 2 * (i - 2) + half + 1)
                    last = products(bank[2 * (i % 2) + half][:, :],
                                    [lambda m, a=a: a[:, m, i * P:(i + 1) * P] for a in (merged_h, merged_l)],
                                    [lambda m, a=a: a[:, m, :] for a in (wo_h[half], wo_l[half])],
                                    ready=merged_lower if i == 0 and half == 0 else None)
                    last.then_inc(att_done, 1)

            def x1_turn(i):
                pe.wait_ge(x1_ready, i + 1)
                for half in range(2):
                    if i == NT - 1:
                        pe.wait_ge(pt_out, half + 1)
                    elif i >= 1:
                        pe.wait_ge(x1t_out, 2 * (i - 1) + half + 1)
                    for k in range(4):
                        last = pe.transpose(bank[4 + half][:, k * P:(k + 1) * P],
                                            x1[:, i, (4 * half + k) * P:(4 * half + k + 1) * P], ident)
                    last.then_inc(x1t_done, 1)

            for i in range(NT):
                att_out(i)
                if i >= 1:
                    x1_turn(i - 1)
            pe.wait_ge(late_in, 16 * 5)
            for k in range(2):
                pe.wait_ge(x1t_out, 2 * (NT - 2) + k + 1)
                for i in range(NT):
                    last = pe.transpose(bank[4 + k][:, i * P:(i + 1) * P], pn[:, i, k * P:(k + 1) * P], ident)
                last.then_inc(pt_done, 1)

            def route(i):
                for k in range(ND):
                    last = mm(bank[6][:, NEXP * i:NEXP * i + NEXP], x1T[:, k, i * P:(i + 1) * P], rw[:, k, :],
                              start=(k == 0), stop=(k == ND - 1))
                return last

            for i in range(NT - 1):
                route(i)
            x1_turn(NT - 1)
            pe.wait_ge(x1t_out, 2 * NT)
            route(NT - 1).then_inc(route_done, 1)

            def places():
                pe.wait_ge(sel_ready, 1)
                for i in range(NT):
                    for a in range(i):
                        mm(bank[7][:, NEXP * i:NEXP * i + NEXP], ones, selb[:, a, :], start=(a == 0), stop=False)
                    mm(bank[7][:, NEXP * i:NEXP * i + NEXP], tri, selb[:, i, :], start=(i == 0), stop=True)
                for i in range(NT):
                    last = mm(bank[7][:, 256:320], ones, selb[:, i, :], start=(i == 0), stop=(i == NT - 1))
                last.then_inc(pos_done, 1)

            def index_of(r, e, n):
                pe.wait_ge(hot_ready, n + 1)
                for i in range(NT):
                    last = mm(bank[7][:, bass.ds(5 * e, 5)], onehot[:, r, i, :],
                              RW5[:, bass.ds(e, 1), i, :].rearrange("p e c -> p (e c)"),
                              start=(i == 0), stop=(i == NT - 1))
                last.then_inc(hot_used, 1)

            def indices(batch):
                if batch == 0:
                    pe.wait_ge(pos_used, 1)
                for n in range(HOT0[batch], HOT0[batch + 1]):
                    index_of(n % NHOT, n, n)

            pe.wait_ge(pt_out, 2)
            pe.wait_ge(ppw_in, 16)
            for n in range(2 * NT):
                half, i = n // NT, n % NT
                if n == NT:
                    places()
                if n >= 2:
                    pe.wait_ge(ple_used, n - 1)
                else:
                    pe.wait_ge(att_used, 2 * NT)
                if i == 0:
                    pe.wait_ge(big_in[(B_PG + half) % 2], big_count(B_PG + half))
                for k in range(ND):
                    mm(bank[n % 2][:, :], x1T[:, k, i * P:(i + 1) * P], pg_h[half][:, k, :],
                       start=(k == 0), stop=(k == ND - 1))
                for k in range(2):
                    last = mm(bank[2 + n % 2][:, :], pT[:, k, i * P:(i + 1) * P],
                              ppw[:, k, 512 * half:512 * half + 512], start=(k == 0), stop=(k == 1))
                last.then_inc(ple_done, 1)
                if n > NT:
                    indices(n - NT - 1)
            def rows_turn(b, it, r):
                n = turn(b, it, r)
                pe.wait_ge(gathered[r], 16 * (NEXP // NR * b + it + 1))
                for half in range(2):
                    if not (isinstance(n, int) and n < 1):
                        pe.wait_ge(xgl_out, 2 * n - 1 + half)
                    for k in range(4):
                        kk = 4 * half + k
                        last = pe.transpose(bank[half][:, k * P:(k + 1) * P], xg[:, r, kk:D:ND], ident)
                    last.then_inc(xgt_done, 1)

            def shared_up(i):
                if i == 0:
                    pe.wait_ge(sgu_in, 32)
                if i >= 2:
                    pe.wait_ge(sh_h, i - 1)
                else:
                    pe.wait_ge(ple_used, 2 * NT - 1 + i)
                for k in range(ND):
                    last = mm(bank[i % 2][:, :].rearrange("p (w f) -> p w f", w=2), x1T[:, k, i * P:(i + 1) * P],
                              sgu[:, :, k, :], start=(k == 0), stop=(k == ND - 1))
                last.then_inc(sh_gu, 1)

            shared_up(0)
            indices(NT - 1)
            for i in range(NT):
                pe.wait_ge(sh_h, i + 1)
                if i >= 1:
                    pe.wait_ge(sh_hto, i)
                for k in range(NF):
                    last = pe.transpose(bank[4][:, k * P:(k + 1) * P], h[:, i % 2, k * P:(k + 1) * P], ident)
                last.then_inc(sh_ht, 1)
                if i + 1 < NT:
                    shared_up(i + 1)
                else:
                    rows_turn(0, 0, 0)
                pe.wait_ge(sh_hto, i + 1)
                if i == 0:
                    pe.wait_ge(sdn_in, 16)
                else:
                    pe.wait_ge(sh_used, i)
                for half in range(2):
                    for k in range(NF):
                        last = mm(bank[2 + half][:, :], hT[:, i % 2, k, :], sdn[:, k, 512 * half:512 * half + 512],
                                  start=(k == 0), stop=(k == NF - 1))
                last.then_inc(sh_y, 1)
                if i < 2:
                    indices(NT + 2 * i)
                    indices(NT + 2 * i + 1)
                if i == 1:
                    pe.wait_ge(hot_used, NEXP)
                    pe.sem_inc(idx_done, 1)
            pe.wait_ge(sh_used, NT)

            def index_pass(b):
                pe.wait_ge(idx_used, b)
                with pe.Fori(0, NEXP // 4) as it:
                    for r in range(4):
                        index_of(r, 4 * it + r, turn(b, it, r))
                pe.wait_ge(hot_used, NEXP * (b + 1))
                pe.sem_inc(idx_done, 1)

            def up(b, it, r, ks_):
                n = turn(b, it, r)
                wh, wl = gate_up(gu_upper(r)), gate_up(gu_lower(r))
                if ks_[0] == 0:
                    pe.wait_ge(xgl_out, 2 * n + 2)
                    pe.wait_ge(e_lower, n + 1)
                    if not (isinstance(n, int) and n < 2):
                        pe.wait_ge(h_ready, n - 1)
                dst = bank[2 + r % 2][:, :].rearrange("p (w f) -> p w f", w=2)
                for k in ks_:
                    mm(dst, xgh[:, r % 2, k, :], wh[:, :, k, :], start=(k == 0), stop=False)
                    mm(dst, xgh[:, r % 2, k, :], wl[:, :, k, :], start=False, stop=False)
                    last = mm(dst, xgl[:, r % 2, k, :], wh[:, :, k, :], start=False, stop=(k == ND - 1))
                if ks_[-1] == ND - 1:
                    last.then_inc(gu_done, 1)

            def hidden_turn(b, it, r):
                n = turn(b, it, r)
                pe.wait_ge(h_ready, n + 1)
                if not (isinstance(n, int) and n < 1):
                    pe.wait_ge(ht_out, n)
                for k in range(NF):
                    last = pe.transpose(bank[4][:, k * P:(k + 1) * P], h[:, r % 2, k:F:NF], ident)
                last.then_inc(ht_done, 1)

            def down(b, it, r):
                n = turn(b, it, r)
                dn = down_w(r)
                pe.wait_ge(ht_out, n + 1)
                pe.wait_ge(wd_in[r % 2], 16 * (second(b, it, r) + 1))
                if not (isinstance(n, int) and n < 1):
                    pe.wait_ge(y_out, 2 * n)
                for half in range(2):
                    for k in range(NF):
                        last = mm(bank[5 + half][:, :], hT[:, r % 2, k, :], dn[:, k, 512 * half:512 * half + 512],
                                  start=(k == 0), stop=(k == NF - 1))
                last.then_inc(y_done, 1)

            def expert_products(b):
                if b:
                    index_pass(b)
                    rows_turn(b, 0, 0)

                def step(it, r, before, after=True):
                    up(b, it, r, range(0, 4))
                    if before is not None:
                        hidden_turn(b, *before)
                    up(b, it, r, range(4, ND))
                    if after:
                        rows_turn(b, it + (r + 1) // NR, (r + 1) % NR)
                    if before is not None:
                        down(b, *before)

                for r in range(NR):
                    step(0, r, (0, r - 1) if r else None)
                last = NEXP // NR - 1
                with pe.Fori(1, last) as it:
                    for r in range(NR):
                        step(it, r, (it, r - 1) if r else (it - 1, NR - 1))
                for r in range(NR):
                    step(last, r, (last, r - 1) if r else (last - 1, NR - 1), after=r < NR - 1)
                hidden_turn(b, last, NR - 1)
                down(b, last, NR - 1)

            expert_products(0)
            pe.wait_ge(cnt_ready, 1)
            most = pe.value_load(cnt[0:1, 0:1], min_val=0, max_val=T)
            with pe.If(most > CAP):
                expert_products(1)
                with pe.If(most > 2 * CAP):
                    expert_products(2)
                    with pe.If(most > 3 * CAP):
                        expert_products(3)
                        with pe.If(most > 4 * CAP):
                            expert_products(4)
                            pe.nop()
                        pe.nop()
                    pe.nop()
                pe.nop()
            for i in range(NT):
                if i >= 2:
                    pe.wait_ge(sums_used, i - 1)
                for k in range(PE_ROWS):
                    n = i * TOPK + k
                    pe.wait_ge(row_in[n % NROW], 16 * (n // NROW + 1))
                    for half in range(2):
                        last = mm(bank[2 * (i % 2) + half][:, :], ident, last_rows(n)[:, 512 * half:512 * half + 512],
                                  start=(k == 0), stop=(k == PE_ROWS - 1))
                last.then_inc(rows_summed, 1)


_INS = ["x", "p", "w_in", "nsa_pe_k", "nsa_w1_k", "nsa_w2_k", "nsa_pe_v", "nsa_w1_v", "nsa_w2_v", "swa_sinks",
        "diff_lq1", "diff_lk1", "diff_lq2", "diff_lk2", "diff_norm_g", "w_branch_a", "w_branch_b", "w_branch_c",
        "w_out", "ln1_g", "ln1_b", "router_w", "router_bias", "exp_w_gate", "exp_w_up", "exp_w_down",
        "sh_w_gate", "sh_w_up", "sh_w_down", "ple_w_proj", "ple_w_gate", "ln2_g", "ln2_b"]


def kernel(**inputs):
    import numpy as _np
    import concourse.bacc as _bacc
    from concourse import mybir as _mybir
    from concourse.bass_utils import run_bass_kernel_spmd as _run

    nc = _bacc.Bacc("TRN2", target_bir_lowering=False, num_devices=1)
    arrays, aps = {}, {}
    for name in _INS:
        a = _np.ascontiguousarray(inputs[name])
        arrays[f"in_{name}_dram"] = a
        aps[name] = nc.dram_tensor(f"in_{name}_dram", a.shape, _mybir.dt.from_np(a.dtype), kind="ExternalInput").ap()
    out = nc.dram_tensor("out_0_dram", (1, T, D), F32, kind="ExternalOutput").ap()
    build(nc, aps, out)
    r = _run(nc, [arrays], core_ids=[0])
    return r.results[0]["out_0_dram"]
```
